# Optimizing a Trainium2 kernel written in Bass

```python
import math
import jax
import jax.numpy as jnp
from jax import lax
import numpy as np

D_MODEL = 1024
BATCH = 1
SEQ = 256
DEPTH = 2

N_META = 16
LEAD = 128
HG_WIDTH = 512
HG_HEADS = 4
HG_DK = 128
HG_DV = 128
HG_CHUNK = 64
DA_WIDTH = 512
DA_HEADS = 4
DA_DQK = 64
DA_DV = 128
Q_BLOCK = 128
REL_BUCKETS = 32
REL_MAX_DIST = 128
D_FF_DENSE = 2816
N_EXPERTS = 8
TOP_K = 2
D_FF_EXPERT = 3584
MOE_BLOCK = 128
EPS = 1e-6
NEG = -1e30
LB_MAX = 0.999
MIX_WIDTH = HG_WIDTH + DA_WIDTH
W_IN_COLS = 4 * HG_WIDTH + 2 * (DA_HEADS * 2 * DA_DQK) + DA_HEADS * DA_DV
N_DENSE = (DEPTH + 1) // 2
N_MOE = DEPTH // 2

kernel_name = 'hybrid_hgrn2_diffattn_moe'

def rmsnorm(x, w):
    xf = x.astype(jnp.float32)
    y = xf * lax.rsqrt(jnp.mean(xf * xf, axis=-1, keepdims=True) + EPS)
    return (y * w.astype(jnp.float32)).astype(x.dtype)

def t5_causal_bucket(dist):
    n = jnp.maximum(dist, 0)
    max_exact = REL_BUCKETS // 2
    nf = jnp.maximum(n, max_exact).astype(jnp.float32)
    large = max_exact + (jnp.log(nf / max_exact) / math.log(REL_MAX_DIST / max_exact)
                         * (REL_BUCKETS - max_exact)).astype(jnp.int32)
    large = jnp.minimum(large, REL_BUCKETS - 1)
    return jnp.where(n < max_exact, n, large)

def attention_block_biases(rel_bias, pos, valid):
    tab = rel_bias.astype(jnp.float32)
    out = []
    for i in range(pos.shape[0] // Q_BLOCK):
        k_end = (i + 1) * Q_BLOCK
        qp = pos[i * Q_BLOCK:k_end]
        kp = pos[:k_end]
        bias = jnp.transpose(tab[t5_causal_bucket(qp[:, None] - kp[None, :])], (2, 0, 1))
        allowed = (kp[None, :] <= qp[:, None]) & valid[None, :k_end]
        out.append(jnp.where(allowed[None], bias, NEG))
    return out

def hgrn2_mixer(q, f_pre, v, g, lb, norm_w, valid):
    B, L, _ = q.shape
    n_chunks = L // HG_CHUNK

    def to_chunks(t):
        return t.reshape(B, n_chunks, HG_CHUNK, HG_HEADS, -1).transpose(1, 0, 3, 2, 4)

    qf = jax.nn.silu(q.astype(jnp.float32))
    log_f = jnp.logaddexp(jnp.log(lb), jnp.log1p(-lb) + jax.nn.log_sigmoid(f_pre.astype(jnp.float32)))
    k = -jnp.expm1(log_f)
    vmask = valid[None, :, None]
    log_f = jnp.where(vmask, log_f, 0.0)
    k = jnp.where(vmask, k, 0.0)
    qc, kc, vc, lc = (to_chunks(t) for t in (qf, k, v.astype(jnp.float32), log_f))
    bc = jnp.cumsum(lc, axis=-2)
    causal = jnp.tril(jnp.ones((HG_CHUNK, HG_CHUNK), dtype=bool))

    def step(S, inp):
        qi, ki, vi, bi = inp
        inter = jnp.einsum('bhtk,bhkv->bhtv', qi * jnp.exp(bi), S)
        rel = bi[..., :, None, :] - bi[..., None, :, :]
        decay = jnp.exp(jnp.where(causal[:, :, None], rel, -jnp.inf))
        scores = jnp.einsum('bhtk,bhsk,bhtsk->bhts', qi, ki, decay)
        intra = jnp.einsum('bhts,bhsv->bhtv', scores, vi)
        b_end = bi[..., -1:, :]
        S_new = jnp.exp(b_end[..., 0, :])[..., None] * S + jnp.einsum(
            'bhsk,bhsv->bhkv', ki * jnp.exp(b_end - bi), vi)
        return S_new, inter + intra

    S0 = jnp.zeros((B, HG_HEADS, HG_DK, HG_DV), jnp.float32)
    _, o = lax.scan(step, S0, (qc, kc, vc, bc))
    o = o.transpose(1, 0, 3, 2, 4).reshape(B, L, HG_HEADS, HG_DV)
    o = rmsnorm(o, norm_w).reshape(B, L, HG_WIDTH) * jax.nn.silu(g.astype(jnp.float32))
    return o.astype(q.dtype)

def diff_attention(q, k, v, lam, lam_init, subln_w, block_biases):
    B, L, _ = q.shape
    q = (q.reshape(B, L, DA_HEADS, 2, DA_DQK) * (DA_DQK ** -0.5)).transpose(0, 2, 3, 1, 4)
    k = k.reshape(B, L, DA_HEADS, 2, DA_DQK).transpose(0, 2, 3, 1, 4)
    vf = v.reshape(B, L, DA_HEADS, DA_DV).transpose(0, 2, 1, 3).astype(jnp.float32)
    outs = []
    for i, bias in enumerate(block_biases):
        k_end = (i + 1) * Q_BLOCK
        s = jnp.einsum('bhcqd,bhckd->bhcqk', q[:, :, :, i * Q_BLOCK:k_end], k[:, :, :, :k_end]).astype(jnp.float32)
        p = jax.nn.softmax(s + bias[None, :, None], axis=-1)
        a = p[:, :, 0] - lam * p[:, :, 1]
        outs.append(jnp.einsum('bhqk,bhkv->bhqv', a, vf[:, :, :k_end]))
    o = jnp.concatenate(outs, axis=2)
    o = rmsnorm(o, subln_w) * (1.0 - lam_init)
    return o.transpose(0, 2, 1, 3).reshape(B, L, DA_HEADS * DA_DV).astype(v.dtype)

def swiglu(h, w1, w3, w2):
    return (jax.nn.silu(h @ w1) * (h @ w3)) @ w2

def moe_swiglu(h, router, w1, w3, w2):
    N, D = h.shape
    logits = (h @ router).astype(jnp.float32)
    top_logit, top_idx = lax.top_k(logits, TOP_K)
    gate = jax.nn.softmax(top_logit, axis=-1)
    M = N * TOP_K
    flat_e = top_idx.reshape(M)
    flat_tok = jnp.repeat(jnp.arange(N, dtype=jnp.int32), TOP_K)
    flat_gate = gate.reshape(M)
    order = jnp.argsort(flat_e)
    e_sorted = flat_e[order]
    counts = jnp.bincount(flat_e, length=N_EXPERTS)
    padded = (counts + MOE_BLOCK - 1) // MOE_BLOCK * MOE_BLOCK
    pad_end = jnp.cumsum(padded)
    pad_start = pad_end - padded
    start = jnp.cumsum(counts) - counts
    dest = pad_start[e_sorted] + jnp.arange(M, dtype=jnp.int32) - start[e_sorted]
    n_blocks = -(-M // MOE_BLOCK) + N_EXPERTS
    P = n_blocks * MOE_BLOCK
    slot_tok = jnp.full((P,), N, jnp.int32).at[dest].set(flat_tok[order])
    slot_gate = jnp.zeros((P,), jnp.float32).at[dest].set(flat_gate[order])
    block_expert = jnp.minimum(
        jnp.searchsorted(pad_end, jnp.arange(n_blocks, dtype=jnp.int32) * MOE_BLOCK, side='right'),
        N_EXPERTS - 1)
    h_ext = jnp.concatenate([h, jnp.zeros((1, D), h.dtype)], axis=0)
    xb = h_ext[slot_tok].reshape(n_blocks, MOE_BLOCK, D)

    def expert_block(args):
        xblk, e = args
        return swiglu(xblk, w1[e], w3[e], w2[e])

    yb = lax.map(expert_block, (xb, block_expert)).reshape(P, D)
    y = yb.astype(jnp.float32) * slot_gate[:, None]
    out = jnp.zeros((N + 1, D), jnp.float32).at[slot_tok].add(y)[:N]
    return out.astype(h.dtype)

def setup_inputs(seed: int = 0) -> dict:
    key = jax.random.key(seed)
    ks = jax.random.split(key, 20)
    f32 = jnp.float32
    nrm = lambda k, shape, scale: jax.random.normal(k, shape, f32) * scale
    gain = lambda k, shape: 1.0 + 0.02 * jax.random.normal(k, shape, f32)
    return {
        'x': nrm(ks[0], (BATCH, SEQ, D_MODEL), 1.0),
        'meta': nrm(ks[1], (N_META, D_MODEL), 1.0),
        'rel_bias': nrm(ks[2], (REL_BUCKETS, DA_HEADS), 0.5),
        'norm_mix': gain(ks[3], (DEPTH, D_MODEL)),
        'w_in': nrm(ks[4], (DEPTH, D_MODEL, W_IN_COLS), D_MODEL ** -0.5),
        'hg_lb_logits': nrm(ks[5], (DEPTH, HG_WIDTH), 0.5),
        'hg_norm_w': gain(ks[6], (DEPTH, HG_DV)),
        'da_lambda': nrm(ks[7], (DEPTH, 4, DA_DQK), 0.1),
        'da_subln_w': gain(ks[8], (DEPTH, DA_DV)),
        'w_out': nrm(ks[9], (DEPTH, MIX_WIDTH, D_MODEL), MIX_WIDTH ** -0.5),
        'norm_ffn': gain(ks[10], (DEPTH, D_MODEL)),
        'dense_w1': nrm(ks[11], (N_DENSE, D_MODEL, D_FF_DENSE), D_MODEL ** -0.5),
        'dense_w3': nrm(ks[12], (N_DENSE, D_MODEL, D_FF_DENSE), D_MODEL ** -0.5),
        'dense_w2': nrm(ks[13], (N_DENSE, D_FF_DENSE, D_MODEL), D_FF_DENSE ** -0.5),
        'moe_router': nrm(ks[14], (N_MOE, D_MODEL, N_EXPERTS), D_MODEL ** -0.5),
        'moe_w1': nrm(ks[15], (N_MOE, N_EXPERTS, D_MODEL, D_FF_EXPERT), D_MODEL ** -0.5),
        'moe_w3': nrm(ks[16], (N_MOE, N_EXPERTS, D_MODEL, D_FF_EXPERT), D_MODEL ** -0.5),
        'moe_w2': nrm(ks[17], (N_MOE, N_EXPERTS, D_FF_EXPERT, D_MODEL), D_FF_EXPERT ** -0.5),
        'final_norm': gain(ks[18], (D_MODEL,)),
    }

def reference(x, meta, rel_bias, norm_mix, w_in, hg_lb_logits, hg_norm_w, da_lambda, da_subln_w,
              w_out, norm_ffn, dense_w1, dense_w3, dense_w2, moe_router, moe_w1, moe_w3, moe_w2,
              final_norm):
    B, S, D = x.shape
    L = LEAD + S
    h0 = jnp.concatenate([
        jnp.zeros((B, LEAD - N_META, D), x.dtype),
        jnp.broadcast_to(meta[None].astype(x.dtype), (B, N_META, D)),
        x], axis=1)
    pos = jnp.arange(L, dtype=jnp.int32) - (LEAD - N_META)
    valid = pos >= 0
    block_biases = attention_block_biases(rel_bias, pos, valid)

    lb_cum = jnp.cumsum(jax.nn.softmax(hg_lb_logits.astype(jnp.float32), axis=0), axis=0)
    lb_all = jnp.clip(lb_cum - lb_cum[0:1], 0.0, LB_MAX)

    c = np.cumsum([0, HG_WIDTH, HG_WIDTH, HG_WIDTH, HG_WIDTH,
                   DA_HEADS * 2 * DA_DQK, DA_HEADS * 2 * DA_DQK, DA_HEADS * DA_DV]).tolist()
    h = h0
    for l in range(DEPTH):
        u = rmsnorm(h, norm_mix[l])
        proj = u @ w_in[l]
        hq, hf, hv, hg, dq, dk, dv = (proj[..., c[j]:c[j + 1]] for j in range(7))
        o_hg = hgrn2_mixer(hq, hf, hv, hg, lb_all[l], hg_norm_w[l], valid)
        lam_init = 0.8 - 0.6 * math.exp(-0.3 * l)
        lv = da_lambda[l].astype(jnp.float32)
        lam = jnp.exp(jnp.sum(lv[0] * lv[1])) - jnp.exp(jnp.sum(lv[2] * lv[3])) + lam_init
        o_da = diff_attention(dq, dk, dv, lam, lam_init, da_subln_w[l], block_biases)
        h = h + (jnp.concatenate([o_hg, o_da], axis=-1) @ w_out[l]).astype(h.dtype)
        u = rmsnorm(h, norm_ffn[l])
        if l % 2 == 0:
            i = l // 2
            ff = swiglu(u, dense_w1[i], dense_w3[i], dense_w2[i])
        else:
            i = l // 2
            ff = moe_swiglu(u.reshape(B * L, D), moe_router[i], moe_w1[i], moe_w3[i], moe_w2[i]).reshape(B, L, D)
        h = h + ff.astype(h.dtype)
    out = rmsnorm(h, final_norm)
    return out[:, LEAD:]


_drawn_inputs = setup_inputs


def setup_inputs(seed=0):
    import zlib

    import numpy as np

    out = dict(_drawn_inputs(seed))
    spreads = {}
    factors = {'hg_norm_w': 8.956,
     'final_norm': 24.375,
     'da_subln_w': 3.466,
     'hg_lb_logits': 3.027,
     'norm_ffn': 3.079}
    for name, (base, spread) in spreads.items():
        noise = np.random.default_rng([zlib.crc32(name.encode()), seed]).standard_normal(out[name].shape)
        drawn = base * np.exp(spread * noise) if base else spread * noise
        out[name] = jnp.asarray(drawn.astype(out[name].dtype))
    for name, factor in factors.items():
        out[name] = (out[name] * factor).astype(out[name].dtype)
    return out
```

```python
from contextlib import ExitStack
import math

import numpy as np
import concourse.bass as bass
from concourse import mybir

P = 128
D = 1024
DC = D // P
META = 16
SEQ = 256
T = META + SEQ
SEG = [(0, META), (META, P), (META + P, P)]
HEADS = 4
HW = 512
PROJ = {"hq": 0, "hf": 1, "hv": 2, "hg": 3, "dq": 4, "dk": 5, "dv": 6}
ORDER1 = ["dq", "dk", "dv"]
ORDER2 = ["hf", "hq", "hg", "hv"]
NPROJ = 7
FD = 2816
FC = FD // P
FE = 3584
NE = 8
SL = 512
NS = FE // SL
JC = SL // P
RING = 7
SLOT = 4096
OVER = 3
NBLK = NE + OVER
BUCKETS = 32
MAXD = 128
RELW = 400
EPS = 1e-6
NEG = -1e30
LB_MAX = 0.999
FLOOR = -87.0
LEVELS = [0, 1, 2, 4, 8, 16, 32, 64]
NGB = 3

F32 = mybir.dt.float32
I32 = mybir.dt.int32
U32 = mybir.dt.uint32
U8 = mybir.dt.uint8
ALU = mybir.AluOpType
ACT = mybir.ActivationFunctionType
AX = mybir.AxisListType


def lam_init(layer):
    return 0.8 - 0.6 * math.exp(-0.3 * layer)


def segs_out(layer):
    return [0, 1, 2] if layer == 0 else [1, 2]


def attention_units(layer):
    return [(q, h) for q in reversed(segs_out(layer)) for h in range(HEADS)]


def level_tasks(layer):
    return [(v, s) for v in range(len(LEVELS)) for s in segs_out(layer)
            if LEVELS[v] * 2 <= SEG[s][1]]


def general_tasks():
    order = [("vec",), ("rel",)] + [("xT", c) for c in range(DC)]
    for l in (0, 1):
        order.append(("ssq", 2 * l))
        order += [("proj", l, s, j) for s in ORDER1 for j in range(JC)]
        order += [("vt", l, "dv", g) for g in range(3)]
        order += [("proj", l, s, j) for s in ORDER2 for j in range(JC)]
        order += [("vt", l, "hv", g) for g in range(3)]
        order += [("kt", l, g) for g in (0, 1)]
        order += [("state", l, g) for g in (0, 1)]
        order += [("o", l, g) for g in segs_out(l)]
        order += [("ms", l, c) for c in (4, 5, 6, 7, 0, 1, 2, 3)]
        if l == 0:
            order += [("wo", d) for d in range(DC)]
            order.append(("ssq", 1))
            for f in range(FC):
                order += [("g", f), ("u", f)]
            order += [("dn", d) for d in range(DC)]
        else:
            order += [("hTt", t, g) for t in (0, 1) for g in (0, 1)]
            order += [("wo1", half, t) for half in (0, 1) for t in (0, 1)]
            order += [("rT", t, g) for t in (0, 1) for g in (0, 1)]
            order += [("logit", t) for t in (0, 1)]
            order += [("rank", 0), ("rank", 1), ("cnt",)]
    return order


TURN = {name: i for i, name in enumerate(general_tasks())}


def prefix_slots():
    slots = []
    for l in (0, 1):
        for s in ORDER1 + ORDER2:
            slots.append(("w_in", (l, s), ("proj", l, s, JC - 1)))
        for half in (0, 1):
            last = ("wo", 4 * half + 3) if l == 0 else ("wo1", half, 1)
            slots.append(("w_out", (l, half), last))
        if l == 0:
            for i in range(6):
                n = min(JC, FC - JC * i)
                slots.append(("w1", i, ("u", JC * i + n - 1)))
                slots.append(("w3", i, ("u", JC * i + n - 1)))
            for half in (0, 1):
                for i in range(3):
                    slots.append(("w2", (half, i), ("dn", 4 * half + 3)))
    return slots


PREFIX = prefix_slots()
SLOT_OF = {(k, i): n for n, (k, i, _) in enumerate(PREFIX)}


def expert_slots():
    order = [("w1", 0), ("w3", 0)]
    for s in range(1, NS):
        order += [("w1", s), ("w3", s), ("w2", s - 1)]
    return order + [("w2", NS - 1)]


EXPERT = expert_slots()
EXPERT_AT = {key: n for n, key in enumerate(EXPERT)}
PER_BLOCK = len(EXPERT)
assert PER_BLOCK % RING == 0
G_USES = [5, 4]
U_USES = [6, 5]


def build(nc, A, out):
    with ExitStack() as ctx:
        def sb(name, shape, dt=F32):
            return ctx.enter_context(nc.sbuf_tensor(name, shape, dt))

        def sem(name):
            return ctx.enter_context(nc.semaphore(name))

        ring = sb("ring", [P, RING * SLOT])
        hT = sb("hT", [P, DC, T])
        uT = sb("uT", [P, DC, T])
        tiles = sb("tiles", [P, 12 * HEADS * T])
        small = sb("small", [P, 2 * 2 * T + 2 * T + 3 * P])
        vtok = sb("vtok", [P, 2, 3, HW])
        bias = sb("bias", [P, HEADS, T])
        ident = sb("ident", [P, P])
        ones = sb("ones", [P, P])
        masks = sb("masks", [P, len(LEVELS), P], U8)
        vecT = sb("vecT", [P, 48])
        lbt = sb("lbt", [P, 2, HEADS])
        omlb = sb("omlb", [P, 2, HEADS])
        lamt = sb("lamt", [P, 16])
        subw = sb("subw", [P, 2])
        eps_t = sb("eps_t", [P, 1])
        stat = sb("stat", [P, 16])
        bend = sb("bend", [P, HEADS])
        rt = sb("rt", [P, 216])
        rti = sb("rti", [P, 32], U32)
        regs = sb("regs", [P, 8], I32)
        scratch = nc.dram_tensor("bias_rows", [HEADS, P, RELW], F32, kind="Internal")

        def tile(i, n=1):
            return tiles[:, i * HEADS * T:(i + n) * HEADS * T]

        def heads(i):
            return tile(i).rearrange("p (h t) -> p h t", h=HEADS)

        DQ, DK, DV, HV = heads(0), heads(1), heads(2), heads(3)
        EF, SG, Q, G, K, LF, B, ODA = (heads(i) for i in range(4, 12))
        X = [DQ, DK]
        DD = [DV, HV]
        TMP = DV
        OHG = K
        KEND, QB = EF, SG
        VEC = tile(4)[0:48, 0:P]
        ONEHOT = tile(5)[0:33, 0:RELW]
        REL = tile(6)[0:33, 0:HEADS]
        RELROW = tile(7)[0:HEADS, 0:RELW]
        LAMIN = tile(8)[:, 0:512]
        LAMP = tile(9)[:, 0:256]
        XTOK = ring[:, 4 * SLOT:4 * SLOT + 2 * D].rearrange("p (t d) -> p t d", t=2)
        MTOK = ring[0:META, 5 * SLOT:5 * SLOT + D]
        MASKF = ring[:, 6 * SLOT:6 * SLOT + len(LEVELS) * P].rearrange("p (v t) -> p v t", t=P)
        SQ = tile(0, 2).rearrange("p (c t) -> p c t", c=DC)
        rstd = SQ[:, 0, :]
        S2 = [small[:, i * 2 * T:(i + 1) * 2 * T].rearrange("p (c t) -> p c t", c=2) for i in (0, 1)]
        AA = [small[:, 4 * T + i * T:4 * T + (i + 1) * T] for i in (0, 1)]
        AT = small[:, 6 * T:6 * T + 3 * P].rearrange("p (g q) -> p g q", g=3)
        KTOK = small[:, 0:2 * HW].rearrange("p (g n) -> p g n", g=2)
        flat = uT[:, :, :].rearrange("p c t -> p (c t)")
        ST = [flat[:, 2 * HW:2 * HW + 64].rearrange("p (h t) -> p h t", h=HEADS),
              flat[:, 0:HW].rearrange("p (h t) -> p h t", h=HEADS),
              flat[:, HW:2 * HW].rearrange("p (h t) -> p h t", h=HEADS)]
        STATE = [flat[:, 2 * HW + 64 + i * HW:2 * HW + 64 + (i + 1) * HW].rearrange("p (h v) -> p h v", h=HEADS)
                 for i in (0, 1)]
        MIX = uT
        ACTT = tiles[:, 2 * HEADS * T:2 * HEADS * T + FC * T].rearrange("p (f t) -> p f t", f=FC)
        SGF = tile(10)[:, 0:2 * T].rearrange("p (b t) -> p b t", b=2)
        XG = tiles[:, 0:D].rearrange("p (c s) -> p c s", c=DC)
        YS = tiles[:, D:2 * D]
        HTOK = tiles[:, 2 * HEADS * T:2 * HEADS * T + 2 * D].rearrange("p (t d) -> p t d", t=2)
        eb = 4 * HEADS * T
        SGE = tiles[:, eb:eb + 1024].rearrange("p (b n) -> p b n", b=2)
        HE = tiles[:, eb + 1024:eb + 2048].rearrange("p (b n) -> p b n", b=2)
        HET = tiles[:, eb + 2048:eb + 3072].rearrange("p (b n) -> p b n", b=2)
        FNW = tiles[:, eb + 3072:eb + 4096]
        PH = tiles[:, eb + 4096:eb + 4352].rearrange("p (t s) -> p t s", t=2)
        PG = tiles[:, eb + 4352:eb + 4608].rearrange("p (t s) -> p t s", t=2)
        PT = tiles[:, eb + 4608:eb + 4864].rearrange("p (t s) -> p t s", t=2)
        IOTA = tiles[:, eb + 4864:eb + 4992]
        UPPER = tiles[:, eb + 4992:eb + 5120]
        ROUT = tiles[:, eb + 5120:eb + 5184].rearrange("p (c e) -> p c e", c=DC)
        NFW = bias[:, :, :].rearrange("p h t -> p (h t)")[:, 0:D]
        UTOK = flat[:, 0:2 * D].rearrange("p (t d) -> p t d", t=2)
        UTR = hT[:, :, :].rearrange("p c t -> p (c t)")[:, 0:2 * D].rearrange("p (c t) -> p c t", c=DC)
        JUNK = hT[:, :, :].rearrange("p c t -> p (c t)")[:, 0:D]
        OUTT = UTOK

        def cols(at, n):
            return rt[:, at:at + n]
        LG = cols(0, 16).rearrange("p (t e) -> p t e", t=2)
        MX = cols(16, 16).rearrange("p (t e) -> p t e", t=2)
        IDXF = cols(32, 4).rearrange("p (t k) -> p t k", t=2)
        OH = cols(36, 32).rearrange("p (t k e) -> p t k e", t=2, k=2)
        MASK = cols(68, 16).rearrange("p (t e) -> p t e", t=2)
        GATE2 = cols(84, 4).rearrange("p (t k) -> p t k", t=2)
        RM = cols(88, 24).rearrange("p (t i) -> p t i", t=2)
        GX = cols(112, 24).rearrange("p (t i) -> p t i", t=2)
        CNT = cols(136, 8)
        OV = cols(144, 8)
        CUM = cols(152, 8)
        SEL = cols(160, 8)
        TMP8 = cols(168, 16).rearrange("p (t e) -> p t e", t=2)
        EID = cols(184, 4)
        ONE8 = cols(188, 8)
        IOTA8 = cols(196, 8)
        RSUM = cols(204, 4)
        TMPG = cols(208, 8)

        banks = [ctx.enter_context(nc.psum_tensor(f"bank{i}", [P, 512], F32)) for i in range(8)]

        g_full = [sem(f"general_full{i}") for i in range(NGB)]
        g_drained = [sem(f"general_drained{i}") for i in range(NGB)]

        def gbank(task):
            return banks[TURN[task] % NGB]

        def full(eng, task):
            i = TURN[task]
            eng.wait_ge(g_full[i % NGB], i // NGB + 1)

        def drained(eng, task):
            i = TURN[task]
            eng.wait_ge(g_drained[i % NGB], i // NGB + 1)

        def drain(ins, task):
            return ins.then_inc(g_drained[TURN[task] % NGB], 1)

        slot_full = [sem(f"slot_full{i}") for i in range(RING)]

        def slot(n):
            return ring[:, (n % RING) * SLOT:(n % RING + 1) * SLOT]

        consts_in = sem("consts_in")
        vec_in = sem("vec_in")
        x_in = sem("x_in")
        rows_out = sem("bias_rows_written")
        bias_in = sem("bias_in")
        lam_in = sem("lambda_in")
        tables_in = sem("expert_tables_in")
        fnw_in = sem("final_norm_in")
        init_done = sem("init_done")
        sq_ready = sem("squares_ready")
        rstd_ready = sem("rstd_ready")
        u_ready = sem("u_ready")
        lam_ready = sem("lambda_ready")
        score_full = sem("attention_scores_full")
        biased = sem("attention_biased")
        exp_done = sem("attention_exp_done")
        a_ready = sem("attention_weights_ready")
        aT_full = sem("attention_weightsT_full")
        aT_drained = sem("attention_weightsT_drained")
        av_full = sem("attention_out_full")
        av_drained = sem("attention_out_drained")
        f_exp = sem("forget_exp_ready")
        f_sig = sem("forget_sigmoid_ready")
        f_gate = sem("forget_gate_ready")
        f_log = sem("forget_log_ready")
        k_ready = sem("k_ready")
        b_ready = sem("b_ready")
        t_clamped = sem("silu_clamped")
        t_sig = sem("silu_sigmoid_ready")
        qg_ready = sem("silu_ready")
        expb = sem("exp_b_ready")
        qb_ready = sem("qb_ready")
        kdiff = sem("kend_difference_ready")
        kexp = sem("kend_exp_ready")
        kend_ready = sem("kend_ready")
        st_zero = sem("scores_zeroed")
        diff_ready = sem("level_difference_ready")
        decay_ready = sem("level_decay_ready")
        xq_ready = sem("level_q_ready")
        xk_ready = sem("level_k_ready")
        lv_full = sem("level_scores_full")
        lv_drained = sem("level_scores_drained")
        mix_sq = sem("mix_squares_ready")
        mix_rstd = sem("mix_rstd_ready")
        mix_ready = sem("mix_ready")
        tok_sum = sem("token_sum_ready")
        tok_rstd = sem("token_rstd_ready")
        utok_ready = sem("u_token_ready")
        top_ready = sem("top_values_ready")
        gate_exp = sem("gate_exp_ready")
        mask_ready = sem("mask_ready")
        regs_ready = sem("registers_ready")
        p_ready = sem("onehot_ready")
        pg_ready = sem("gated_onehot_ready")
        G_full = [sem(f"gate_full{i}") for i in (0, 1)]
        G_free = [sem(f"gate_free{i}") for i in (0, 1)]
        U_full = [sem(f"up_full{i}") for i in (0, 1)]
        scatter_added = [sem(f"scatter_added{i}") for i in (0, 1)]
        col_ready = sem("routing_column_ready")
        he_ready = sem("expert_h_ready")
        heT_full = sem("expert_hT_full")
        heT_ready = sem("expert_hT_ready")
        down_done = sem("expert_down_done")
        y_ready = sem("expert_y_ready")
        pT_full = sem("scatter_onehot_full")
        pT_ready = sem("scatter_onehot_ready")
        out_ready = sem("out_ready")
        out_written = sem("out_written")
        dve_step = sem("dve_step")
        act_step = sem("act_step")
        pool_step = sem("pool_step")

        def chain(eng, signal):
            count = [0]

            def link(ins):
                count[0] += 1
                ins.then_inc(signal, 1)
                eng.wait_ge(signal, count[0])
            return link

        def level_part(x, m, half):
            if m <= 8:
                return x.rearrange("p h (n two m) -> p (h n) two m", two=2, m=m)[:, :, half, :]
            return x[:, :, META:T].rearrange("p h (n two m) -> p h n two m", two=2, m=m)[:, :, :, half, :]

        w_in = A["w_in"].rearrange("l (c p) n -> l p c n", p=P)
        w_out = A["w_out"].rearrange("l (c p) n -> l p c n", p=P)
        d1 = A["dense_w1"][0].rearrange("(c p) n -> p c n", p=P)
        d3 = A["dense_w3"][0].rearrange("(c p) n -> p c n", p=P)
        d2 = A["dense_w2"][0].rearrange("(c p) n -> p c n", p=P)
        e1 = A["moe_w1"][0].rearrange("e (c p) n -> e p c n", p=P)
        e3 = A["moe_w3"][0].rearrange("e (c p) n -> e p c n", p=P)
        e2 = A["moe_w2"][0].rearrange("e (c p) n -> e p c n", p=P)

        block = ctx.enter_context(nc.Block())

        @block.sync
        def _(sp):
            sp.dma_start(XTOK, A["x"][0].rearrange("(t p) d -> p t d", p=P)).then_inc(x_in, 16)
            sp.dma_start(MTOK, A["meta"]).then_inc(x_in, 16)
            for n, (kind, i, _) in enumerate(PREFIX):
                if n == 4:
                    drained(sp, ("xT", DC - 1))
                if n == 6:
                    sp.wait_ge(init_done, 1)
                if n >= RING:
                    full(sp, PREFIX[n - RING][2])
                if kind == "w_in":
                    c0 = PROJ[i[1]] * HW
                    src = w_in[i[0]][:, :, c0:c0 + HW]
                elif kind == "w_out":
                    src = w_out[i[0]][:, :, i[1] * HW:(i[1] + 1) * HW]
                elif kind == "w2":
                    src = d2[:, 8 * i[1]:min(8 * i[1] + 8, FC), i[0] * HW:(i[0] + 1) * HW]
                else:
                    src = (d1 if kind == "w1" else d3)[:, :, i * SL:min((i + 1) * SL, FD)]
                dst = slot(n)[:, 0:src.shape[1] * src.shape[2]].rearrange("p (c n) -> p c n", c=src.shape[1])
                sp.dma_start(dst, src).then_inc(slot_full[n % RING], 16)

            def expert_load(key, n, expert):
                kind, s = key
                if kind == "w2":
                    sp.dma_start(slot(n).rearrange("p (c n) -> p c n", c=JC),
                                 e2[expert, :, s * JC:(s + 1) * JC, :]).then_inc(slot_full[n % RING], 16)
                else:
                    sp.dma_start(slot(n).rearrange("p (c n) -> p c n", c=DC),
                                 (e1 if kind == "w1" else e3)[expert, :, :, s * SL:(s + 1) * SL]
                                 ).then_inc(slot_full[n % RING], 16)

            def used(key, blk):
                kind, s = key
                if kind == "w1":
                    sp.wait_ge(G_full[s % 2], blk * G_USES[s % 2] + s // 2 + 2)
                elif kind == "w3":
                    sp.wait_ge(U_full[s % 2], blk * U_USES[s % 2] + s // 2 + 1)
                else:
                    sp.wait_ge(down_done, blk * NS + s + 1)

            def block_load(expert, blk, first):
                for m, key in enumerate(EXPERT):
                    if m < RING and first:
                        full(sp, PREFIX[len(PREFIX) - RING + m][2])
                    elif m < RING:
                        used(EXPERT[PER_BLOCK - RING + m], blk - 1)
                    else:
                        used(EXPERT[m - RING], blk)
                    expert_load(key, len(PREFIX) + m, expert)

            block_load(0, 0, True)
            with sp.Fori(1, NE) as e:
                block_load(e, e, False)
            sp.wait_ge(regs_ready, 1)
            over = sp.value_load(regs[0:1, 0:1], min_val=0, max_val=OVER)
            eids = [sp.value_load(regs[0:1, 1 + j:2 + j], min_val=0, max_val=NE - 1) for j in range(OVER)]
            for j in range(OVER):
                with sp.If(over > j):
                    block_load(eids[j], NE + j, False)
            sp.wait_ge(out_ready, 1)
            sp.dma_start(out[0].rearrange("(t p) d -> p t d", p=P), OUTT).then_inc(out_written, 16)
            sp.wait_ge(out_written, 16)

        @block.tensor
        def _(pe):
            def bank_free(task):
                i = TURN[task]
                if i >= NGB:
                    pe.wait_ge(g_drained[i % NGB], i // NGB)

            def fin(ins, task):
                ins.then_inc(g_full[TURN[task] % NGB], 1)

            def slot_in(n):
                pe.wait_ge(slot_full[n % RING], 16 * (n // RING + 1))

            pe.wait_ge(consts_in, 32)
            pe.wait_ge(vec_in, 16 * 7)
            pe.transpose(gbank(("vec",))[:, 0:44], VEC[0:44, :], ident[0:44, 0:44]).then_inc(
                g_full[TURN[("vec",)] % NGB], 1)
            pe.wait_ge(init_done, 1)
            fin(pe.matmul(gbank(("rel",))[0:HEADS, 0:RELW], REL, ONEHOT, start=True, stop=True), ("rel",))
            pe.wait_ge(x_in, 32)
            for c in range(DC):
                task = ("xT", c)
                bank_free(task)
                pe.transpose(gbank(task)[:, 0:META], MTOK[:, c * P:(c + 1) * P], ident[0:META, 0:META])
                for t in (0, 1):
                    i = pe.transpose(gbank(task)[:, META + t * P:META + (t + 1) * P],
                                     XTOK[:, t, c * P:(c + 1) * P], ident[:, :])
                fin(i, task)

            def sum_squares(k):
                task = ("ssq", k)
                bank_free(task)
                for c in range(DC):
                    pe.wait_ge(sq_ready, DC * k + c + 1)
                    i = pe.matmul(gbank(task)[:, 0:T], ones[:, :], SQ[:, c, :], start=c == 0, stop=c == DC - 1)
                fin(i, task)

            def product(task, n, j, width, rhs, chunks=DC):
                w = slot(n)[:, 0:chunks * width].rearrange("p (c n) -> p c n", c=chunks)
                bank_free(task)
                for c in range(chunks):
                    i = pe.matmul(gbank(task)[:, 0:T], w[:, c, j * P:(j + 1) * P], rhs[:, c, :],
                                  start=c == 0, stop=c == chunks - 1)
                fin(i, task)

            def project(l, s, j):
                n = SLOT_OF[("w_in", (l, s))]
                if j == 0:
                    slot_in(n)
                product(("proj", l, s, j), n, j, HW, uT)

            def to_tokens(l, name, src, k):
                for g, (t0, tn) in enumerate(SEG):
                    task = ("vt", l, name, g)
                    bank_free(task)
                    for h in range(HEADS):
                        i = pe.transpose(gbank(task)[0:tn, h * P:(h + 1) * P], src[:, h, t0:t0 + tn], ident[:, :])
                    fin(i, task)

            units0 = 0
            lv0 = 0
            av0 = 0
            for l in (0, 1):
                sum_squares(2 * l)
                pe.wait_ge(u_ready, DC * (2 * l + 1))
                for s in ORDER1:
                    for j in range(JC):
                        project(l, s, j)
                drained(pe, ("proj", l, "dv", JC - 1))
                to_tokens(l, "dv", DV, 0)

                units = attention_units(l)

                def score(i):
                    q, h = units[i]
                    q0, qn = SEG[q]
                    kn = q0 + qn
                    if units0 + i > 0:
                        pe.wait_ge(biased, units0 + i)
                    for c in (0, 1):
                        r = slice(64 * c, 64 * c + 64)
                        ins = pe.matmul(banks[3 + c][0:qn, 0:kn], DQ[r, h, q0:q0 + qn], DK[r, h, 0:kn],
                                        start=True, stop=True)
                    ins.then_inc(score_full, 1)

                def weights_t(i):
                    q, h = units[i]
                    qn = SEG[q][1]
                    pe.wait_ge(a_ready, units0 + i + 1)
                    if units0 + i > 0:
                        pe.wait_ge(aT_drained, units0 + i)
                    for g in range(q + 1):
                        k0, kn = SEG[g]
                        ins = pe.transpose(banks[5][0:kn, g * P:g * P + qn], AA[i % 2][0:qn, k0:k0 + kn],
                                           ident[0:qn, 0:qn])
                    ins.then_inc(aT_full, 1)

                def weigh_v(i):
                    q, h = units[i]
                    qn = SEG[q][1]
                    n = av0 + i // HEADS
                    pe.wait_ge(aT_drained, units0 + i + 1)
                    if h == 0 and n >= 2:
                        pe.wait_ge(av_drained, n - 1)
                    for g in range(q + 1):
                        kn = SEG[g][1]
                        ins = pe.matmul(banks[6 + n % 2][:, h * P:h * P + qn], vtok[0:kn, 0, g, h * P:(h + 1) * P],
                                        AT[0:kn, g, 0:qn], start=g == 0, stop=g == q)
                    ins.then_inc(av_full, 1)

                if l == 0:
                    pe.wait_ge(bias_in, 16)
                drained(pe, ("vt", l, "dv", 2))
                for i in range(16):
                    project(l, ORDER2[i // 4], i % 4)
                    if i < len(units):
                        score(i)
                    if 0 <= i - 2 < len(units):
                        weights_t(i - 2)
                    if 0 <= i - 3 < len(units):
                        weigh_v(i - 3)
                drained(pe, ("proj", l, "hv", JC - 1))
                to_tokens(l, "hv", HV, 1)
                pe.wait_ge(kend_ready, l + 1)
                for g in (0, 1):
                    t0, tn = SEG[g]
                    task = ("kt", l, g)
                    bank_free(task)
                    for h in range(HEADS):
                        i = pe.transpose(gbank(task)[0:tn, h * P:(h + 1) * P], KEND[:, h, t0:t0 + tn], ident[:, :])
                    fin(i, task)
                for g in (0, 1):
                    tn = SEG[g][1]
                    task = ("state", l, g)
                    drained(pe, ("kt", l, g))
                    drained(pe, ("vt", l, "hv", g))
                    bank_free(task)
                    for h in range(HEADS):
                        i = pe.matmul(gbank(task)[:, h * P:(h + 1) * P], KTOK[0:tn, g, h * P:(h + 1) * P],
                                      vtok[0:tn, 1, g, h * P:(h + 1) * P], start=True, stop=True)
                    fin(i, task)
                levels = level_tasks(l)
                pe.wait_ge(k_ready, l + 1)
                pe.wait_ge(qg_ready, 2 * l + 1)
                for i, (v, g) in enumerate(levels):
                    t0, tn = SEG[g]
                    n = lv0 + i
                    if i < 2:
                        pe.wait_ge(av_drained, av0 + len(units) // HEADS)
                    if n >= 2:
                        pe.wait_ge(lv_drained, n - 1)
                    if v > 0:
                        pe.wait_ge(xq_ready, 7 * l + v)
                        pe.wait_ge(xk_ready, 7 * l + v)
                    for h in range(HEADS):
                        lo = K if v == 0 else X[v % 2]
                        hi = Q if v == 0 else X[v % 2]
                        ins = pe.matmul(banks[6 + n % 2][0:tn, h * P:h * P + tn], lo[:, h, t0:t0 + tn],
                                        hi[:, h, t0:t0 + tn], start=True, stop=True)
                    ins.then_inc(lv_full, 1)
                pe.wait_ge(lv_drained, lv0 + len(levels))
                pe.wait_ge(qb_ready, l + 1)
                for g in segs_out(l):
                    t0, tn = SEG[g]
                    task = ("o", l, g)
                    drained(pe, ("vt", l, "hv", g))
                    if g > 0:
                        drained(pe, ("state", l, g - 1))
                    bank_free(task)
                    for h in range(HEADS):
                        o = gbank(task)[:, h * P:h * P + tn]
                        i = pe.matmul(o, vtok[0:tn, 1, g, h * P:(h + 1) * P], ST[g][0:tn, h, :], start=True,
                                      stop=g == 0)
                        if g > 0:
                            i = pe.matmul(o, STATE[g - 1][:, h, :], QB[:, h, t0:t0 + tn], start=False, stop=True)
                    fin(i, task)
                o0 = 0 if l == 0 else META
                for n, c in enumerate((4, 5, 6, 7, 0, 1, 2, 3)):
                    task = ("ms", l, c)
                    pe.wait_ge(mix_sq, 2 * l + (1 if c >= 4 else 2))
                    src = LF if c >= 4 else DQ
                    bank_free(task)
                    fin(pe.matmul(gbank(task)[:, o0:T], ones[:, :], src[:, c % 4, o0:T], start=True, stop=True), task)
                units0 += len(units)
                lv0 += len(levels)
                av0 += len(units) // HEADS
                if l == 0:
                    pe.wait_ge(mix_ready, 8)
                    for d in range(DC):
                        n = SLOT_OF[("w_out", (0, d // 4))]
                        slot_in(n)
                        product(("wo", d), n, d % 4, HW, MIX)
                    sum_squares(1)
                    pe.wait_ge(u_ready, 2 * DC)
                    for f in range(FC):
                        width = min(SL, FD - (f // 4) * SL)
                        for kind, w in (("g", "w1"), ("u", "w3")):
                            n = SLOT_OF[(w, f // 4)]
                            slot_in(n)
                            product((kind, f), n, f % 4, width, uT)
                    drained(pe, ("u", FC - 1))
                    for d in range(DC):
                        task = ("dn", d)
                        bank_free(task)
                        for f in range(FC):
                            n = SLOT_OF[("w2", (d // 4, f // 8))]
                            if f % 8 == 0:
                                slot_in(n)
                            w = slot(n)[:, (f % 8) * HW + (d % 4) * P:(f % 8) * HW + (d % 4 + 1) * P]
                            i = pe.matmul(gbank(task)[:, 0:T], w, ACTT[:, f, :], start=f == 0, stop=f == FC - 1)
                        fin(i, task)
            for t in (0, 1):
                for g in (0, 1):
                    task = ("hTt", t, g)
                    bank_free(task)
                    for c in range(4):
                        i = pe.transpose(gbank(task)[:, c * P:(c + 1) * P],
                                         hT[:, 4 * g + c, META + t * P:META + (t + 1) * P], ident[:, :])
                    fin(i, task)
            pe.wait_ge(mix_ready, 16)
            for half in (0, 1):
                n = SLOT_OF[("w_out", (1, half))]
                slot_in(n)
                for t in (0, 1):
                    task = ("wo1", half, t)
                    bank_free(task)
                    for c in range(DC):
                        i = pe.matmul(gbank(task)[:, :], MIX[:, c, META + t * P:META + (t + 1) * P],
                                      slot(n)[:, c * HW:(c + 1) * HW], start=c == 0, stop=c == DC - 1)
                    fin(i, task)
            for t in (0, 1):
                pe.wait_ge(utok_ready, t + 1)
                for g in (0, 1):
                    task = ("rT", t, g)
                    bank_free(task)
                    for c in range(4):
                        i = pe.transpose(gbank(task)[:, c * P:(c + 1) * P], UTOK[:, t, (4 * g + c) * P:(4 * g + c + 1) * P],
                                         ident[:, :])
                    fin(i, task)
            pe.wait_ge(tables_in, 16 * 4)
            for t in (0, 1):
                task = ("logit", t)
                drained(pe, ("rT", t, 0))
                drained(pe, ("rT", t, 1))
                bank_free(task)
                for c in range(DC):
                    i = pe.matmul(gbank(task)[:, 0:NE], UTR[:, c, t * P:(t + 1) * P], ROUT[:, c, :],
                                  start=c == 0, stop=c == DC - 1)
                fin(i, task)
            pe.wait_ge(mask_ready, 2)
            task = ("rank", 0)
            bank_free(task)
            fin(pe.matmul(gbank(task)[:, 0:NE], UPPER, MASK[:, 0, :], start=True, stop=True), task)
            for task, first in ((("rank", 1), UPPER), (("cnt",), ones[:, :])):
                bank_free(task)
                pe.matmul(gbank(task)[:, 0:NE], ones[:, :], MASK[:, 0, :], start=True, stop=False)
                fin(pe.matmul(gbank(task)[:, 0:NE], first, MASK[:, 1, :], start=False, stop=True), task)
            drained(pe, ("rank", 0))
            drained(pe, ("rank", 1))
            drained(pe, ("cnt",))

            def gather(n, wait_banks):
                pe.wait_ge(p_ready, n + 1)
                for b in (0, 1):
                    if wait_banks:
                        pe.wait_ge(G_free[b], n * G_USES[b])
                    for c in range(4):
                        o = banks[b][:, c * P:(c + 1) * P]
                        for t in (0, 1):
                            i = pe.matmul(o, UTOK[:, t, (4 * b + c) * P:(4 * b + c + 1) * P], PH[:, t, :],
                                          start=t == 0, stop=t == 1)
                    i.then_inc(G_full[b], 1)

            def expert_block(n):
                base = n * (16 * PER_BLOCK // RING)

                def weights_in(key):
                    m = len(PREFIX) + EXPERT_AT[key]
                    pe.wait_ge(slot_full[m % RING], base + 16 * (m // RING + 1))
                    return slot(m)

                def up(kind, s):
                    b = s % 2
                    bank0, fulls = (0, G_full) if kind == "w1" else (2, U_full)
                    w = weights_in((kind, s))
                    if kind == "w1":
                        pe.wait_ge(G_free[b], n * G_USES[b] + s // 2 + 1)
                    elif s >= 2:
                        pe.wait_ge(he_ready, n * NS + s - 1)
                    else:
                        pe.wait_ge(scatter_added[b], 2 * n + 1)
                    for c in range(DC):
                        i = pe.matmul(banks[bank0 + b][:, :], XG[:, c, :], w[:, c * SL:(c + 1) * SL],
                                      start=c == 0, stop=c == DC - 1)
                    i.then_inc(fulls[b], 1)

                def turn_h(s):
                    pe.wait_ge(he_ready, n * NS + s + 1)
                    if s > 0:
                        pe.wait_ge(heT_ready, n * NS + s)
                    for j in range(JC):
                        i = pe.transpose(banks[4][:, j * P:(j + 1) * P], HE[:, s % 2, j * P:(j + 1) * P], ident[:, :])
                    i.then_inc(heT_full, 1)

                def down(s):
                    w = weights_in(("w2", s))
                    pe.wait_ge(heT_ready, n * NS + s + 1)
                    for half in (0, 1):
                        for j in range(JC):
                            i = pe.matmul(banks[5 + half][:, :], HET[:, s % 2, j * P:(j + 1) * P],
                                          w[:, j * D + half * 512:j * D + half * 512 + 512],
                                          start=s == 0 and j == 0, stop=s == NS - 1 and j == JC - 1)
                    i.then_inc(down_done, 1)

                pe.wait_ge(G_free[1], n * G_USES[1] + 1)
                for s in range(NS):
                    up("w1", s)
                    if s == 0:
                        pe.wait_ge(pg_ready, n + 1)
                        for t in (0, 1):
                            i = pe.transpose(banks[7][:, t * P:(t + 1) * P], PG[:, t, :], ident[:, :])
                        i.then_inc(pT_full, 1)
                    else:
                        turn_h(s - 1)
                    up("w3", s)
                    if s > 0:
                        down(s - 1)
                gather(n + 1, True)
                turn_h(NS - 1)
                down(NS - 1)
                pe.wait_ge(pT_ready, n + 1)
                pe.wait_ge(y_ready, 2 * n + 2)
                for t in (0, 1):
                    for half in (0, 1):
                        if t == 1:
                            pe.wait_ge(scatter_added[half], 2 * n + 2)
                        pe.matmul(banks[2 + half][:, :], PT[:, t, :], YS[:, half * 512:(half + 1) * 512],
                                  start=True, stop=True).then_inc(U_full[half], 1)

            gather(0, False)
            with pe.Fori(0, NE) as e:
                expert_block(e)
            pe.wait_ge(regs_ready, 1)
            over = pe.value_load(regs[0:1, 0:1], min_val=0, max_val=OVER)
            for j in range(OVER):
                with pe.If(over > j):
                    expert_block(NE + j)

        @block.scalar
        def _(act):
            link = chain(act, act_step)
            act.dma_start(VEC[0:16, :], A["norm_mix"].rearrange("l (c p) -> (l c) p", p=P)).then_inc(vec_in, 16)
            act.dma_start(VEC[16:32, :], A["norm_ffn"].rearrange("l (c p) -> (l c) p", p=P)).then_inc(vec_in, 16)
            act.dma_start(VEC[32:40, :], A["hg_lb_logits"].rearrange("l (c p) -> (l c) p", p=P)).then_inc(vec_in, 16)
            act.dma_start(VEC[40:42, :], A["hg_norm_w"]).then_inc(vec_in, 16)
            act.dma_start(VEC[42:44, :], A["da_subln_w"]).then_inc(vec_in, 16)
            act.dma_start(REL[0:32, :], A["rel_bias"]).then_inc(vec_in, 16)
            act.dma_start(ONEHOT, A["buckets"]).then_inc(vec_in, 16)
            act.dma_start(ident[:, :], A["ident"]).then_inc(consts_in, 16)
            act.dma_start(MASKF, A["masks"]).then_inc(consts_in, 16)
            act.dma_start(LAMIN, A["da_lambda"].rearrange("l a d -> (l a d)").partition_broadcast(P)).then_inc(lam_in, 16)
            full(act, ("rel",))
            drain(act.copy(RELROW, gbank(("rel",))[0:HEADS, 0:RELW]), ("rel",))
            drained(act, ("rel",))
            act.dma_start(scratch.ap(), RELROW.unsqueeze(1).to_broadcast([HEADS, P, RELW])).then_inc(rows_out, 16)
            act.wait_ge(rows_out, 16)
            shifted = scratch.ap().rearrange("h p j -> (h p j)")
            act.dma_start(bias[:, :, :], bass.AP(shifted.tensor, P - 1, [[RELW - 1, P], [P * RELW, HEADS], [1, T]])
                          ).then_inc(bias_in, 16)

            act.wait_ge(lam_ready, 1)
            act.activation(lamt[:, 4:8], lamt[:, 0:4], ACT.Exp).then_inc(lam_ready, 1)
            act.wait_ge(lam_ready, 3)
            act.activation(lbt[:, 1, :], lbt[:, 1, :], ACT.Exp).then_inc(lam_ready, 1)
            act.wait_ge(init_done, 2)

            def squares(k):
                if k == 0:
                    for c in range(DC):
                        drained(act, ("xT", c))
                        act.activation(SQ[:, c, :], hT[:, c, :], ACT.Square).then_inc(sq_ready, 1)
                else:
                    for c in range(DC):
                        drained(act, ("wo", c) if k == 1 else ("dn", c))
                        act.activation(SQ[:, c, :], hT[:, c, :], ACT.Square).then_inc(sq_ready, 1)
                task = ("ssq", k)
                full(act, task)
                drain(act.activation(rstd, gbank(task)[:, 0:T], ACT.Ln, scale=1.0 / D, bias=eps_t[:, 0:1]), task)
                drained(act, task)
                act.activation(rstd, rstd, ACT.Exp, scale=-0.5).then_inc(rstd_ready, 1)

            def copy_proj(l, s, dst):
                for j in range(JC):
                    task = ("proj", l, s, j)
                    full(act, task)
                    drain(act.copy(dst[:, j, :], gbank(task)[:, 0:T]), task)

            def copy_vt(l, name, k):
                for g, (t0, tn) in enumerate(SEG):
                    task = ("vt", l, name, g)
                    full(act, task)
                    drain(act.copy(vtok[0:tn, k, g, :], gbank(task)[0:tn, :]), task)

            units0 = 0
            av0 = 0
            for l in (0, 1):
                squares(2 * l)
                copy_proj(l, "dq", DQ)
                copy_proj(l, "dk", DK)
                copy_proj(l, "dv", DV)
                copy_vt(l, "dv", 0)
                units = attention_units(l)

                def exps(i):
                    q, h = units[i]
                    qn = SEG[q][1]
                    kn = SEG[q][0] + qn
                    b = i % 2
                    act.wait_ge(biased, units0 + i + 1)
                    for c in (0, 1):
                        ins = act.activation(S2[b][0:qn, c, 0:kn], S2[b][0:qn, c, 0:kn], ACT.Exp,
                                             bias=stat[0:qn, 4 * b + c:4 * b + c + 1],
                                             accum_out=stat[0:qn, 8 + 4 * b + c:8 + 4 * b + c + 1])
                    ins.then_inc(exp_done, 1)

                def copy_at(i):
                    q, h = units[i]
                    qn = SEG[q][1]
                    act.wait_ge(aT_full, units0 + i + 1)
                    if i > 0:
                        act.wait_ge(av_full, units0 + i)
                    for g in range(q + 1):
                        kn = SEG[g][1]
                        ins = act.copy(AT[0:kn, g, 0:qn], banks[5][0:kn, g * P:g * P + qn])
                    ins.then_inc(aT_drained, 1)

                def copy_av(i):
                    q = units[i][0]
                    t0, tn = SEG[q]
                    n = av0 + i // HEADS
                    act.wait_ge(av_full, units0 + i + 1)
                    act.copy(ODA[:, :, t0:t0 + tn],
                             banks[6 + n % 2][:, :].rearrange("p (h t) -> p h t", h=HEADS)[:, :, 0:tn]
                             ).then_inc(av_drained, 1)

                def sigmoid_of_tmp(i):
                    act.wait_ge(t_clamped, 2 * l + i + 1)
                    link(act.activation(TMP, TMP, ACT.Exp, scale=-1.0))
                    link(act.activation(TMP, TMP, ACT.Ln, bias=1.0))
                    act.activation(TMP, TMP, ACT.Exp, scale=-1.0).then_inc(t_sig, 1)

                dsts = {"hq": Q, "hg": G, "hv": HV}
                for i in range(16):
                    s, j = ORDER2[i // 4], i % 4
                    if i < len(units):
                        exps(i)
                    if s != "hf":
                        task = ("proj", l, s, j)
                        full(act, task)
                        drain(act.copy(dsts[s][:, j, :], gbank(task)[:, 0:T]), task)
                    if 0 <= i - 2 < len(units):
                        copy_at(i - 2)
                    if 0 <= i - 3 < len(units) and (i - 3) % HEADS == HEADS - 1:
                        copy_av(i - 3)
                    if i == 5:
                        drained(act, ("proj", l, "hf", JC - 1))
                        act.activation(EF, EF, ACT.Exp, scale=-1.0).then_inc(f_exp, 1)
                        act.wait_ge(f_exp, l + 1)
                        link(act.activation(SG, EF, ACT.Ln, bias=1.0))
                        act.activation(SG, SG, ACT.Exp, scale=-1.0).then_inc(f_sig, 1)
                    if i == 8:
                        act.wait_ge(f_gate, l + 1)
                        act.activation(LF, LF, ACT.Ln).then_inc(f_log, 1)
                    if i == 10:
                        sigmoid_of_tmp(0)
                    if i == 14:
                        act.wait_ge(b_ready, l + 1)
                        act.wait_ge(k_ready, l + 1)
                        act.wait_ge(kdiff, l + 1)
                        act.activation(SG, B, ACT.Exp).then_inc(expb, 1)
                        act.activation(bend[:, :], B[:, :, SEG[1][0] + P - 1], ACT.Exp).then_inc(expb, 1)
                        act.activation(KEND[:, :, 0:SEG[2][0]], KEND[:, :, 0:SEG[2][0]], ACT.Exp).then_inc(kexp, 1)
                sigmoid_of_tmp(1)
                copy_vt(l, "hv", 1)
                for g in (0, 1):
                    tn = SEG[g][1]
                    task = ("kt", l, g)
                    full(act, task)
                    drain(act.copy(KTOK[0:tn, g, :], gbank(task)[0:tn, :]), task)
                for v in range(1, len(LEVELS)):
                    m = LEVELS[v]
                    act.wait_ge(diff_ready, 7 * l + v)
                    for half in (0, 1):
                        part = level_part(DD[v % 2], m, half)
                        ins = act.activation(part, part, ACT.Exp, scale=1.0 if half else -1.0)
                    ins.then_inc(decay_ready, 1)
                for g in segs_out(l):
                    t0, tn = SEG[g]
                    task = ("o", l, g)
                    full(act, task)
                    drain(act.copy(OHG[:, :, t0:t0 + tn],
                                   gbank(task)[:, :].rearrange("p (h t) -> p h t", h=HEADS)[:, :, 0:tn]), task)
                o0 = 0 if l == 0 else META
                act.wait_ge(av_drained, av0 + len(units) // HEADS)
                act.activation(LF[:, :, o0:T], ODA[:, :, o0:T], ACT.Square).then_inc(mix_sq, 1)
                drained(act, ("o", l, 2))
                act.activation(DQ[:, :, o0:T], OHG[:, :, o0:T], ACT.Square).then_inc(mix_sq, 1)
                for c in (4, 5, 6, 7, 0, 1, 2, 3):
                    task = ("ms", l, c)
                    dst = LF if c >= 4 else DQ
                    full(act, task)
                    drain(act.activation(dst[:, c % 4, o0:T], gbank(task)[:, o0:T], ACT.Ln, scale=1.0 / P,
                                         bias=eps_t[:, 0:1]), task)
                    if c % 4 == 3:
                        drained(act, task)
                        act.activation(dst[:, :, o0:T], dst[:, :, o0:T], ACT.Exp, scale=-0.5).then_inc(mix_rstd, 1)
                units0 += len(units)
                av0 += len(units) // HEADS
                if l == 0:
                    squares(1)
                    for f in range(FC):
                        task = ("g", f)
                        full(act, task)
                        if f >= 2:
                            drained(act, ("u", f - 2))
                        drain(act.activation(SGF[:, f % 2, :], gbank(task)[:, 0:T], ACT.Silu), task)
            act.wait_ge(mix_ready, 16)
            for t in (0, 1):
                for g in (0, 1):
                    task = ("hTt", t, g)
                    full(act, task)
                    drain(act.copy(HTOK[:, t, g * 512:(g + 1) * 512], gbank(task)[:, :]), task)
            for t in (0, 1):
                drained(act, ("wo1", 0, t))
                drained(act, ("wo1", 1, t))
                act.activation(JUNK, HTOK[:, t, :], ACT.Square, accum_out=RSUM[:, t:t + 1]).then_inc(tok_sum, 1)
                act.wait_ge(tok_sum, t + 1)
                link(act.activation(RSUM[:, t:t + 1], RSUM[:, t:t + 1], ACT.Ln, scale=1.0 / D, bias=eps_t[:, 0:1]))
                act.activation(RSUM[:, t:t + 1], RSUM[:, t:t + 1], ACT.Exp, scale=-0.5).then_inc(tok_rstd, 1)
            for t in (0, 1):
                for g in (0, 1):
                    task = ("rT", t, g)
                    full(act, task)
                    drain(act.copy(UTR[:, 4 * g:4 * g + 4, t * P:(t + 1) * P],
                                   gbank(task)[:, :].rearrange("p (c t) -> p c t", c=4)), task)
            act.wait_ge(top_ready, 2)
            act.activation(GATE2[:, :, 1], GATE2[:, :, 1], ACT.Exp).then_inc(gate_exp, 1)

            def copy_gather(b, n):
                act.wait_ge(G_full[b], n)
                act.copy(XG[:, 4 * b:4 * b + 4, :], banks[b][:, :].rearrange("p (c s) -> p c s", c=4)
                         ).then_inc(G_free[b], 1)

            for b in (0, 1):
                copy_gather(b, 1)

            def expert_block(n):
                for s in range(NS):
                    b = s % 2
                    act.wait_ge(G_full[b], n * G_USES[b] + s // 2 + 2)
                    if s >= 2:
                        act.wait_ge(he_ready, n * NS + s - 1)
                    act.activation(SGE[:, b, :], banks[b][:, :], ACT.Silu).then_inc(G_free[b], 1)
                    if s == 0:
                        act.wait_ge(pT_full, n + 1)
                        act.copy(PT, banks[7][:, 0:2 * P].rearrange("p (t s) -> p t s", t=2)).then_inc(pT_ready, 1)
                    else:
                        turn(n, s - 1)
                for b in (0, 1):
                    copy_gather(b, n * G_USES[b] + G_USES[b] + 1)
                turn(n, NS - 1)
                act.wait_ge(down_done, n * NS + NS)
                act.copy(YS[:, 0:512], banks[5][:, :]).then_inc(y_ready, 1)

            def turn(n, s):
                act.wait_ge(heT_full, n * NS + s + 1)
                if s >= 2:
                    act.wait_ge(down_done, n * NS + s - 1)
                act.copy(HET[:, s % 2, :], banks[4][:, :]).then_inc(heT_ready, 1)

            with act.Fori(0, NE) as e:
                expert_block(e)
            act.wait_ge(regs_ready, 1)
            over = act.value_load(regs[0:1, 0:1], min_val=0, max_val=OVER)
            for j in range(OVER):
                with act.If(over > j):
                    expert_block(NE + j)
            act.wait_ge(tok_sum, 3)
            for t in (0, 1):
                link(act.activation(JUNK, HTOK[:, t, :], ACT.Square, accum_out=RSUM[:, 2 + t:3 + t]))
            link(act.activation(RSUM[:, 2:4], RSUM[:, 2:4], ACT.Ln, scale=1.0 / D, bias=eps_t[:, 0:1]))
            act.activation(RSUM[:, 2:4], RSUM[:, 2:4], ACT.Exp, scale=-0.5).then_inc(tok_rstd, 1)

        @block.vector
        def _(dve):
            link = chain(dve, dve_step)
            dve.memset(ones[:, :], 1.0)
            dve.wait_ge(consts_in, 32)
            dve.tensor_copy(masks[:, :, :], MASKF)
            dve.memset(eps_t[:, :], EPS)
            dve.memset(ONE8, 1.0)
            dve.memset(lbt[:, 0, :], 0.0)
            dve.memset(omlb[:, 0, :], 1.0)
            dve.memset(REL[32:33, :], NEG).then_inc(init_done, 1)
            dve.wait_ge(lam_in, 16)
            lv = LAMIN.rearrange("p (k two d) -> p k two d", two=2, d=64)
            link(dve.tensor_tensor(LAMP.rearrange("p (k d) -> p k d", d=64), lv[:, :, 0, :], lv[:, :, 1, :], ALU.mult))
            dve.tensor_reduce(lamt[:, 0:4], LAMP.rearrange("p (k d) -> p k d", d=64), AX.X, ALU.add).then_inc(lam_ready, 1)
            full(dve, ("vec",))
            drain(dve.tensor_copy(vecT[:, 0:44], gbank(("vec",))[:, 0:44]), ("vec",))
            drained(dve, ("vec",))
            dve.wait_ge(lam_ready, 2)
            link(dve.tensor_tensor(lbt[:, 1, :], vecT[:, 32:36], vecT[:, 36:40], ALU.subtract))
            dve.tensor_scalar(lbt[:, 1, :], lbt[:, 1, :], -FLOOR, None, ALU.min).then_inc(lam_ready, 1)
            for l in (0, 1):
                e = lamt[:, 4 + 2 * l:6 + 2 * l]
                link(dve.tensor_tensor(lamt[:, 8 + l:9 + l], e[:, 1:2], e[:, 0:1], ALU.subtract))
                link(dve.tensor_scalar(lamt[:, 8 + l:9 + l], lamt[:, 8 + l:9 + l], -lam_init(l), None, ALU.add))
                link(dve.tensor_scalar(subw[:, l:l + 1], vecT[:, 42 + l:43 + l], 1.0 - lam_init(l), None, ALU.mult))
            dve.wait_ge(lam_ready, 4)
            link(dve.tensor_scalar(lbt[:, 1, :], lbt[:, 1, :], 1.0, None, ALU.add))
            link(dve.reciprocal(lbt[:, 1, :], lbt[:, 1, :]))
            link(dve.tensor_scalar(lbt[:, 1, :], lbt[:, 1, :], 0.0, LB_MAX, ALU.max, ALU.min))
            dve.tensor_scalar(omlb[:, 1, :], lbt[:, 1, :], -1.0, 1.0, ALU.mult, ALU.add).then_inc(init_done, 1)
            for c in range(DC):
                task = ("xT", c)
                full(dve, task)
                drain(dve.tensor_copy(hT[:, c, :], gbank(task)[:, 0:T]), task)

            def normed(k, col):
                dve.wait_ge(rstd_ready, k + 1)
                for c in range(DC):
                    dve.scalar_tensor_tensor(uT[:, c, :], hT[:, c, :], vecT[:, col + c:col + c + 1], rstd,
                                             ALU.mult, ALU.mult).then_inc(u_ready, 1)

            def softmax_in(l, i):
                q, h = attention_units(l)[i]
                qn = SEG[q][1]
                kn = SEG[q][0] + qn
                b = i % 2
                n = units0 + i
                dve.wait_ge(score_full, n + 1)
                if n >= 2:
                    dve.wait_ge(a_ready, n - 1)
                if n == 0:
                    dve.wait_ge(bias_in, 16)
                b0 = SEG[2][0] - SEG[q][0]
                for c in (0, 1):
                    ins = dve.scalar_tensor_tensor(S2[b][0:qn, c, 0:kn], banks[3 + c][0:qn, 0:kn], 0.125,
                                                   bias[0:qn, h, b0:b0 + kn], ALU.mult, ALU.add)
                link(ins)
                link(dve.tensor_reduce(stat[0:qn, 4 * b:4 * b + 2], S2[b][0:qn, :, 0:kn], AX.X, ALU.max))
                dve.tensor_scalar(stat[0:qn, 4 * b:4 * b + 2], stat[0:qn, 4 * b:4 * b + 2], -1.0, None,
                                  ALU.mult).then_inc(biased, 1)

            def softmax_out(l, i):
                q, h = attention_units(l)[i]
                qn = SEG[q][1]
                kn = SEG[q][0] + qn
                b = i % 2
                n = units0 + i
                r = stat[0:qn, 8 + 4 * b:10 + 4 * b]
                dve.wait_ge(exp_done, n + 1)
                link(dve.reciprocal(r, r))
                link(dve.tensor_tensor(r[:, 1:2], r[:, 1:2], lamt[0:qn, 8 + l:9 + l], ALU.mult))
                if i >= 2:
                    dve.wait_ge(aT_full, n - 1)
                link(dve.tensor_scalar(AA[b][0:qn, 0:kn], S2[b][0:qn, 1, 0:kn], r[:, 1:2], None, ALU.mult))
                dve.scalar_tensor_tensor(AA[b][0:qn, 0:kn], S2[b][0:qn, 0, 0:kn], r[:, 0:1], AA[b][0:qn, 0:kn],
                                         ALU.mult, ALU.add).then_inc(a_ready, 1)

            units0 = 0
            lv0 = 0
            for l in (0, 1):
                normed(2 * l, 8 * l)
                units = attention_units(l)
                for i in range(16):
                    if i < 4:
                        task = ("proj", l, "hf", i)
                        full(dve, task)
                        drain(dve.tensor_scalar(EF[:, i, :], gbank(task)[:, 0:T], FLOOR, None, ALU.max), task)
                    if i < len(units):
                        softmax_in(l, i)
                    if 0 <= i - 1 < len(units):
                        softmax_out(l, i - 1)
                    if i == 7:
                        dve.wait_ge(f_sig, l + 1)
                        for h in range(HEADS):
                            ins = dve.scalar_tensor_tensor(K[:, h, :], EF[:, h, :], omlb[:, l, h:h + 1], SG[:, h, :],
                                                           ALU.mult, ALU.mult)
                        ins.then_inc(k_ready, 1)
                    if i == 10:
                        dve.wait_ge(f_log, l + 1)
                        for h in range(HEADS):
                            for t0, tn in SEG:
                                ins = dve.tensor_tensor_scan(B[:, h, t0:t0 + tn], ones[:, 0:tn], LF[:, h, t0:t0 + tn],
                                                             0.0, ALU.mult, ALU.add)
                        ins.then_inc(b_ready, 1)
                levels = level_tasks(l)
                dve.wait_ge(qg_ready, 2 * l + 1)
                dve.wait_ge(st_zero, l + 1)

                def decayed_q(v):
                    m = LEVELS[v]
                    dve.wait_ge(decay_ready, 7 * l + v)
                    if v > 2:
                        dve.wait_ge(lv_full, lv0 + sum(1 for a, _ in levels if a <= v - 2))
                    dve.tensor_tensor(level_part(X[v % 2], m, 1), level_part(Q, m, 1), level_part(DD[v % 2], m, 1),
                                      ALU.mult).then_inc(xq_ready, 1)

                for v in range(len(LEVELS)):
                    if v + 1 < len(LEVELS):
                        decayed_q(v + 1)
                    for i, (a, g) in enumerate(levels):
                        if a != v:
                            continue
                        tn = SEG[g][1]
                        n = lv0 + i
                        dve.wait_ge(lv_full, n + 1)
                        if n > 0:
                            dve.wait_ge(lv_drained, n)
                        m = masks[0:tn, v, 0:tn].unsqueeze(1).to_broadcast([tn, HEADS, tn])
                        dve.copy_predicated(ST[g][0:tn, :, :], m,
                                            banks[6 + n % 2][0:tn, :].rearrange("p (h t) -> p h t", h=HEADS)[:, :, 0:tn]
                                            ).then_inc(lv_drained, 1)
                for g in (0, 1):
                    task = ("state", l, g)
                    full(dve, task)
                    if g == 0:
                        drain(dve.tensor_copy(STATE[0].rearrange("p h v -> p (h v)"), gbank(task)[:, :]), task)
                        drained(dve, task)
                        dve.wait_ge(expb, 2 * l + 2)
                    else:
                        for h in range(HEADS):
                            ins = dve.scalar_tensor_tensor(STATE[1][:, h, :], STATE[0][:, h, :], bend[:, h:h + 1],
                                                           gbank(task)[:, h * P:(h + 1) * P], ALU.mult, ALU.add)
                        drain(ins, task)
                o0 = 0 if l == 0 else META
                full(dve, ("o", l, 2))
                dve.wait_ge(mix_rstd, 2 * l + 1)
                for h in range(HEADS):
                    dve.scalar_tensor_tensor(MIX[:, 4 + h, o0:T], ODA[:, h, o0:T], subw[:, l:l + 1], LF[:, h, o0:T],
                                             ALU.mult, ALU.mult).then_inc(mix_ready, 1)
                dve.wait_ge(mix_rstd, 2 * l + 2)
                dve.wait_ge(qg_ready, 2 * l + 2)
                for h in range(HEADS):
                    link(dve.scalar_tensor_tensor(MIX[:, h, o0:T], OHG[:, h, o0:T], vecT[:, 40 + l:41 + l],
                                                  DQ[:, h, o0:T], ALU.mult, ALU.mult))
                    dve.tensor_tensor(MIX[:, h, o0:T], MIX[:, h, o0:T], G[:, h, o0:T], ALU.mult).then_inc(mix_ready, 1)
                units0 += len(units)
                lv0 += len(levels)
                if l == 0:
                    for d in range(DC):
                        task = ("wo", d)
                        full(dve, task)
                        drain(dve.tensor_tensor(hT[:, d, :], hT[:, d, :], gbank(task)[:, 0:T], ALU.add), task)
                    drained(dve, ("wo", DC - 1))
                    normed(1, 16)
                    for f in range(FC):
                        task = ("u", f)
                        full(dve, task)
                        drained(dve, ("g", f))
                        drain(dve.tensor_tensor(ACTT[:, f, :], SGF[:, f % 2, :], gbank(task)[:, 0:T], ALU.mult), task)
                    for d in range(DC):
                        task = ("dn", d)
                        full(dve, task)
                        drain(dve.tensor_tensor(hT[:, d, :], hT[:, d, :], gbank(task)[:, 0:T], ALU.add), task)
                    drained(dve, ("dn", DC - 1))
            for half in (0, 1):
                for t in (0, 1):
                    task = ("wo1", half, t)
                    full(dve, task)
                    drained(dve, ("hTt", t, half))
                    h = HTOK[:, t, half * 512:(half + 1) * 512]
                    drain(dve.tensor_tensor(h, h, gbank(task)[:, :], ALU.add), task)
            drained(dve, ("wo1", 1, 1))
            dve.wait_ge(tables_in, 16 * 4)
            for t in (0, 1):
                dve.wait_ge(tok_rstd, t + 1)
                dve.scalar_tensor_tensor(UTOK[:, t, :], HTOK[:, t, :], RSUM[:, t:t + 1], NFW, ALU.mult,
                                         ALU.mult).then_inc(utok_ready, 1)
            for t in (0, 1):
                task = ("logit", t)
                full(dve, task)
                drain(dve.tensor_copy(LG[:, t, :], gbank(task)[:, 0:NE]), task)
                drained(dve, task)
                link(dve.max(MX[:, t, :], LG[:, t, :]))
                link(dve.max_index(rti[:, 8 * t:8 * t + 8], MX[:, t, :], LG[:, t, :]))
                link(dve.tensor_copy(IDXF[:, t, :], rti[:, 8 * t:8 * t + 2]))
                for k in (0, 1):
                    link(dve.tensor_scalar(OH[:, t, k, :], IOTA[:, 0:NE], IDXF[:, t, k:k + 1], None, ALU.is_equal))
                dve.tensor_tensor(MASK[:, t, :], OH[:, t, 0, :], OH[:, t, 1, :], ALU.add).then_inc(mask_ready, 1)
                dve.tensor_tensor(GATE2[:, t, 1:2], MX[:, t, 1:2], MX[:, t, 0:1], ALU.subtract).then_inc(top_ready, 1)
            dve.wait_ge(mask_ready, 2)
            dve.wait_ge(gate_exp, 1)
            link(dve.tensor_scalar(GATE2[:, :, 0], GATE2[:, :, 1], 1.0, None, ALU.add))
            link(dve.reciprocal(GATE2[:, :, 0], GATE2[:, :, 0]))
            link(dve.tensor_tensor(GATE2[:, :, 1], GATE2[:, :, 1], GATE2[:, :, 0], ALU.mult))
            link(dve.memset(rt[:, 88:136], 0.0))
            for t in (0, 1):
                link(dve.tensor_scalar(TMP8[:, t, :], OH[:, t, 0, :], GATE2[:, t, 0:1], None, ALU.mult))
                link(dve.scalar_tensor_tensor(GX[:, t, 0:NE], OH[:, t, 1, :], GATE2[:, t, 1:2], TMP8[:, t, :],
                                              ALU.mult, ALU.add))
                task = ("rank", t)
                full(dve, task)
                link(dve.tensor_scalar(TMP8[:, t, :], gbank(task)[:, 0:NE], 1.0, None, ALU.add))
                drain(dve.tensor_tensor(TMP8[:, t, :], TMP8[:, t, :], MASK[:, t, :], ALU.mult), task)
                drained(dve, task)
                link(dve.tensor_scalar(RM[:, t, 0:NE], TMP8[:, t, :], -1.0, None, ALU.add))
            full(dve, ("cnt",))
            drain(dve.tensor_scalar(OV, gbank(("cnt",))[:, 0:NE], float(P), None, ALU.is_gt), ("cnt",))
            drained(dve, ("cnt",))
            link(dve.tensor_tensor_scan(CUM, ONE8, OV, 0.0, ALU.mult, ALU.add))
            link(dve.tensor_copy(EID[:, 0:1], CUM[:, 7:8]))
            for j in range(OVER):
                link(dve.tensor_scalar(SEL, CUM, float(j + 1), None, ALU.is_equal))
                link(dve.tensor_tensor(SEL, SEL, OV, ALU.mult))
                link(dve.tensor_tensor(TMPG, SEL, IOTA[:, 0:NE], ALU.mult))
                link(dve.tensor_reduce(EID[:, 1 + j:2 + j], TMPG, AX.X, ALU.add))
                for t in (0, 1):
                    link(dve.tensor_scalar(TMP8[:, t, :], RM[:, t, 0:NE], -float(P), None, ALU.add))
                    link(dve.tensor_tensor(TMP8[:, t, :], TMP8[:, t, :], SEL, ALU.mult))
                    link(dve.tensor_reduce(RM[:, t, NE + j:NE + j + 1], TMP8[:, t, :], AX.X, ALU.add))
                    link(dve.tensor_tensor(TMP8[:, t, :], GX[:, t, 0:NE], SEL, ALU.mult))
                    link(dve.tensor_reduce(GX[:, t, NE + j:NE + j + 1], TMP8[:, t, :], AX.X, ALU.add))
            dve.tensor_copy(regs[:, 0:4], EID).then_inc(regs_ready, 1)

            def onehot(n, step):
                dve.tensor_copy(TMPG[:, 0:2], RM[:, :, n]).then_inc(col_ready, 1)
                dve.wait_ge(col_ready, step)
                for t in (0, 1):
                    ins = dve.tensor_scalar(PH[:, t, :], IOTA, TMPG[:, t:t + 1], None, ALU.is_equal)
                ins.then_inc(p_ready, 1)

            dve.wait_ge(regs_ready, 1)
            onehot(0, 1)
            for b in (0, 1):
                dve.memset(TMPG[:, 6 + b:7 + b], 0.0).then_inc(scatter_added[b], 1)

            def expert_block(n):
                dve.wait_ge(p_ready, n + 1)
                dve.tensor_copy(TMPG[:, 4:6], GX[:, :, n]).then_inc(col_ready, 1)
                dve.wait_ge(col_ready, 2 * n + 2)
                for t in (0, 1):
                    ins = dve.tensor_scalar(PG[:, t, :], PH[:, t, :], TMPG[:, 4 + t:5 + t], None, ALU.mult)
                ins.then_inc(pg_ready, 1)
                dve.wait_ge(pg_ready, n + 1)
                dve.wait_ge(G_full[1], n * G_USES[1] + 1)
                onehot(n + 1, 2 * n + 3)
                for s in range(NS):
                    b = s % 2
                    dve.wait_ge(U_full[b], n * U_USES[b] + s // 2 + 1)
                    dve.wait_ge(G_free[b], n * G_USES[b] + s // 2 + 2)
                    if s >= 2:
                        dve.wait_ge(heT_full, n * NS + s - 1)
                    dve.tensor_tensor(HE[:, b, :], SGE[:, b, :], banks[2 + b][:, :], ALU.mult).then_inc(he_ready, 1)
                dve.wait_ge(down_done, n * NS + NS)
                dve.tensor_copy(YS[:, 512:1024], banks[6][:, :]).then_inc(y_ready, 1)
                for t in (0, 1):
                    for half in (0, 1):
                        dve.wait_ge(U_full[half], n * U_USES[half] + (5 if half == 0 else 4) + t)
                        h = HTOK[:, t, half * 512:(half + 1) * 512]
                        dve.tensor_tensor(h, h, banks[2 + half][:, :], ALU.add
                                          ).then_inc(scatter_added[half], 1)

            with dve.Fori(0, NE) as e:
                expert_block(e)
            over = dve.value_load(regs[0:1, 0:1], min_val=0, max_val=OVER)
            for j in range(OVER):
                with dve.If(over > j):
                    expert_block(NE + j)
            dve.wait_ge(fnw_in, 16)
            dve.memset(stat[:, 0:1], 0.0).then_inc(tok_sum, 1)
            dve.wait_ge(tok_rstd, 3)
            for t in (0, 1):
                ins = dve.scalar_tensor_tensor(OUTT[:, t, :], HTOK[:, t, :], RSUM[:, 2 + t:3 + t], FNW, ALU.mult, ALU.mult)
            ins.then_inc(out_ready, 1)

        @block.gpsimd
        def _(pool):
            link = chain(pool, pool_step)
            pool.wait_ge(init_done, 2)
            for l in (0, 1):
                pool.wait_ge(f_sig, l + 1)
                for h in range(HEADS):
                    ins = pool.tensor_scalar(LF[:, h, :], SG[:, h, :], omlb[:, l, h:h + 1], lbt[:, l, h:h + 1],
                                             ALU.mult, ALU.add)
                ins.then_inc(f_gate, 1)
                full(pool, ("vt", l, "dv", 2))
                drained(pool, ("proj", l, "hq", JC - 1))
                pool.tensor_scalar(TMP, Q, 3e38, FLOOR, ALU.min, ALU.max).then_inc(t_clamped, 1)
                pool.wait_ge(t_sig, 2 * l + 1)
                pool.tensor_tensor(Q, Q, TMP, ALU.mult).then_inc(qg_ready, 1)
                pool.wait_ge(b_ready, l + 1)
                pool.wait_ge(k_ready, l + 1)
                for t0, tn in SEG[0:2]:
                    end = B[:, :, t0 + tn - 1:t0 + tn].to_broadcast([P, HEADS, tn])
                    ins = pool.tensor_tensor(KEND[:, :, t0:t0 + tn], end, B[:, :, t0:t0 + tn], ALU.subtract)
                ins.then_inc(kdiff, 1)
                drained(pool, ("proj", l, "hg", JC - 1))
                pool.wait_ge(qg_ready, 2 * l + 1)
                pool.tensor_scalar(TMP, G, 3e38, FLOOR, ALU.min, ALU.max).then_inc(t_clamped, 1)
                pool.wait_ge(expb, 2 * l + 1)
                pool.tensor_tensor(QB[:, :, META:T], Q[:, :, META:T], SG[:, :, META:T], ALU.mult).then_inc(qb_ready, 1)
                pool.wait_ge(kexp, l + 1)
                pool.tensor_tensor(KEND[:, :, 0:SEG[2][0]], K[:, :, 0:SEG[2][0]], KEND[:, :, 0:SEG[2][0]],
                                   ALU.mult).then_inc(kend_ready, 1)
                pool.wait_ge(t_sig, 2 * l + 2)
                pool.tensor_tensor(G, G, TMP, ALU.mult).then_inc(qg_ready, 1)
                full(pool, ("proj", l, "hv", JC - 1))
                pool.memset(flat[:, 0:2 * HW + 64], 0.0).then_inc(st_zero, 1)
                full(pool, ("vt", l, "hv", 2))
                pool.wait_ge(qg_ready, 2 * l + 2)

                def difference(v):
                    m = LEVELS[v]
                    if v > 2:
                        pool.wait_ge(xq_ready, 7 * l + v - 2)
                    for half in (0, 1):
                        src = level_part(B, m, half)
                        ref = level_part(B, m, 0)
                        ref = ref[:, :, m - 1:m] if m <= 8 else ref[:, :, :, m - 1:m]
                        ins = pool.tensor_tensor(level_part(DD[v % 2], m, half), src,
                                                 ref.to_broadcast(list(src.shape)), ALU.subtract)
                    ins.then_inc(diff_ready, 1)

                difference(1)
                for v in range(1, len(LEVELS)):
                    if v + 1 < len(LEVELS):
                        if v + 1 > 2:
                            pool.wait_ge(xk_ready, 7 * l + v - 1)
                        difference(v + 1)
                    m = LEVELS[v]
                    pool.wait_ge(decay_ready, 7 * l + v)
                    if v > 2:
                        levels = level_tasks(l)
                        pool.wait_ge(lv_full, (0 if l == 0 else len(level_tasks(0)))
                                     + sum(1 for a, _ in levels if a <= v - 2))
                    pool.tensor_tensor(level_part(X[v % 2], m, 0), level_part(K, m, 0), level_part(DD[v % 2], m, 0),
                                       ALU.mult).then_inc(xk_ready, 1)
            pool.wait_ge(mix_ready, 16)
            pool.dma_start(NFW, A["norm_ffn"][1].partition_broadcast(P)).then_inc(tables_in, 16)
            pool.dma_start(IOTA, A["iota"]).then_inc(tables_in, 16)
            pool.dma_start(UPPER, A["upper"]).then_inc(tables_in, 16)
            pool.dma_start(ROUT, A["moe_router"][0].rearrange("(c p) e -> p c e", p=P)).then_inc(tables_in, 16)
            pool.wait_ge(tables_in, 16 * 4)
            pool.dma_start(FNW, A["final_norm"].partition_broadcast(P)).then_inc(fnw_in, 16)
            pool.wait_ge(fnw_in, 16)


_INS = ['x', 'meta', 'rel_bias', 'norm_mix', 'w_in', 'hg_lb_logits', 'hg_norm_w', 'da_lambda', 'da_subln_w',
        'w_out', 'norm_ffn', 'dense_w1', 'dense_w3', 'dense_w2', 'moe_router', 'moe_w1', 'moe_w3', 'moe_w2',
        'final_norm']


def constants():
    dist = T - 1 - np.arange(RELW)
    exact = BUCKETS // 2
    n = np.maximum(dist, 0)
    nf = np.maximum(n, exact).astype(np.float32)
    large = exact + (np.log(nf / np.float32(exact)) / np.float32(math.log(MAXD / exact))
                     * np.float32(BUCKETS - exact)).astype(np.int32)
    bucket = np.where(n < exact, n, np.minimum(large, BUCKETS - 1))
    buckets = np.zeros((BUCKETS + 1, RELW), np.float32)
    for j in range(RELW):
        buckets[bucket[j] if dist[j] >= 0 else BUCKETS, j] = 1.0
    s = np.arange(P)[:, None]
    t = np.arange(P)[None, :]
    masks = np.zeros((P, len(LEVELS), P), np.float32)
    for v, m in enumerate(LEVELS):
        if m == 0:
            masks[:, v, :] = s == t
        else:
            masks[:, v, :] = (s // (2 * m) == t // (2 * m)) & (s % (2 * m) < m) & (t % (2 * m) >= m)
    return {
        "ident": np.eye(P, dtype=np.float32),
        "masks": masks,
        "buckets": buckets,
        "iota": np.broadcast_to(np.arange(P, dtype=np.float32), (P, P)).copy(),
        "upper": (s < t).astype(np.float32),
    }


def kernel(**inputs):
    import numpy as _np
    import concourse.bacc as _bacc
    from concourse import mybir as _mybir
    from concourse.bass_utils import run_bass_kernel_spmd as _run

    nc = _bacc.Bacc("TRN2", target_bir_lowering=False, num_devices=1)
    arrays, aps = {}, {}
    everything = {name: _np.ascontiguousarray(inputs[name]) for name in _INS}
    everything.update(constants())
    for name, a in everything.items():
        arrays[f"in_{name}_dram"] = a
        aps[name] = nc.dram_tensor(f"in_{name}_dram", a.shape, _mybir.dt.from_np(a.dtype), kind="ExternalInput").ap()
    out = nc.dram_tensor("out_0_dram", (1, SEQ, D), F32, kind="ExternalOutput").ap()
    build(nc, aps, out)
    r = _run(nc, [arrays], core_ids=[0])
    return r.results[0]["out_0_dram"]
```

```python
from contextlib import ExitStack
import math

import numpy as np
import concourse.bass as bass
from concourse import mybir

P = 128
D = 1024
DC = D // P
META = 16
SEQ = 256
T = META + SEQ
SEG = [(0, META), (META, P), (META + P, P)]
HEADS = 4
HW = 512
PROJ = {"hq": 0, "hf": 1, "hv": 2, "hg": 3, "dq": 4, "dk": 5, "dv": 6}
ORDER1 = ["dq", "dk", "dv"]
ORDER2 = ["hf", "hq", "hg", "hv"]
NPROJ = 7
FD = 2816
FC = FD // P
FE = 3584
NE = 8
SL = 512
NS = FE // SL
JC = SL // P
RING = 3
SLOT = 4096
HRING = 14
HSLOT = SLOT // 2
UNIT = 1024
NW = 4
AHEAD = NW - 1
OVER = 3
NBLK = NE + OVER
BUCKETS = 32
MAXD = 128
RELW = 400
EPS = 1e-6
NEG = -1e30
LB_MAX = 0.999
FLOOR = -87.0
LEVELS = [0, 1, 2, 4, 8, 16, 32, 64]
NGB = 3

F32 = mybir.dt.float32
F32R = mybir.dt.float32r
I32 = mybir.dt.int32
U32 = mybir.dt.uint32
U8 = mybir.dt.uint8
ALU = mybir.AluOpType
ACT = mybir.ActivationFunctionType
AX = mybir.AxisListType


def lam_init(layer):
    return 0.8 - 0.6 * math.exp(-0.3 * layer)


def segs_out(layer):
    return [0, 1, 2] if layer == 0 else [1, 2]


def attention_units(layer):
    return [(q, h) for q in reversed(segs_out(layer)) for h in range(HEADS)]


def level_tasks(layer):
    return [(v, s) for v in range(len(LEVELS)) for s in segs_out(layer)
            if LEVELS[v] * 2 <= SEG[s][1]]


def general_tasks():
    order = [("vec",), ("rel",)] + [("xT", c) for c in range(DC)]
    for l in (0, 1):
        order.append(("ssq", 2 * l))
        order += [("proj", l, s, j) for s in ORDER1 for j in range(JC)]
        order += [("vt", l, "dv", g) for g in range(3)]
        order += [("proj", l, s, j) for s in ORDER2 for j in range(JC)]
        order += [("vt", l, "hv", g) for g in range(3)]
        order += [("kt", l, g) for g in (0, 1)]
        order += [("state", l, g) for g in (0, 1)]
        order += [("o", l, g) for g in segs_out(l)]
        order += [("ms", l, c) for c in (4, 5, 6, 7, 0, 1, 2, 3)]
        if l == 0:
            order += [("wo", d) for d in range(DC)]
            order.append(("ssq", 1))
            for i in range(0, FC, JC):
                order += [(k, f) for k in ("g", "u") for f in range(i, min(i + JC, FC))]
        else:
            order += [("hTt", t, g) for t in (0, 1) for g in (0, 1)]
            order += [("wo1", half, t) for half in (0, 1) for t in (0, 1)]
            order += [("rT", t, g) for t in (0, 1) for g in (0, 1)]
            order += [("logit", t) for t in (0, 1)]
            order += [("rank", 0), ("rank", 1), ("cnt",)]
    return order


TURN = {name: i for i, name in enumerate(general_tasks())}


def prefix_slots():
    slots = []
    for l in (0, 1):
        slots += [("w_in", (l, s)) for s in ORDER1 + ORDER2]
        slots += [("w_out", (l, half)) for half in (0, 1)]
        if l == 0:
            slots += [(w, i) for i in range(-(-FC // JC)) for w in ("w1", "w3")]
            slots += [("w2", (half, i)) for half in (0, 1) for i in range(3)]
    return slots


PREFIX = prefix_slots()
SLOT_OF = {key: n for n, key in enumerate(PREFIX)}


def prefix_units():
    units = []
    done = [0]

    def count():
        done[0] += 1
        return ("count", done[0])

    for l in (0, 1):
        for s in ORDER1 + ORDER2:
            units += [(SLOT_OF[("w_in", (l, s))], "cols", j, HW, ("proj", l, s, j)) for j in range(JC)]
        if l == 0:
            units += [(SLOT_OF[("w_out", (0, d // 4))], "cols", d % 4, HW, ("wo", d)) for d in range(DC)]
            for i in range(0, FC, JC):
                n = min(JC, FC - i)
                for k, w in (("g", "w1"), ("u", "w3")):
                    units += [(SLOT_OF[(w, i // JC)], "cols", j, n * P, (k, i + j)) for j in range(n)]
            for half in (0, 1):
                for u in range(FC // 2):
                    units.append((SLOT_OF[("w2", (half, u // 4))], "rows", u % 4, HW,
                                  count() if u < FC // 2 - 1 else ("down", half)))
        else:
            for half in (0, 1):
                for u in range(DC // 2):
                    units.append((SLOT_OF[("w_out", (1, half))], "rows", u, HW,
                                  count() if u < DC // 2 - 1 else ("wo1", half, 1)))
    return units, done[0]


UNITS, UNITS_COUNTED = prefix_units()
UNIT_OF = {u[4]: n for n, u in enumerate(UNITS)}
LAST_UNIT = {u[0]: n for n, u in enumerate(UNITS)}


def expert_slots():
    order = [("w1", 0), ("w3", 0)]
    for s in range(1, NS):
        order += [("w1", s), ("w3", s), ("w2", s - 1)]
    return order + [("w2", NS - 1)]


EXPERT = expert_slots()
EXPERT_AT = {key: n for n, key in enumerate(EXPERT)}
BLOCK_HALVES = 2 * len(EXPERT)
BLOCK_UNITS = 4 * len(EXPERT)
assert BLOCK_HALVES % HRING == 0 and BLOCK_UNITS % NW == 0
EARLY = AHEAD // 2 + 1
COUNTED = 3 * len(EXPERT)
G_USES = [5, 4]
U_USES = [6, 5]


def build(nc, A, out):
    with ExitStack() as ctx:
        def sb(name, shape, dt=F32):
            return ctx.enter_context(nc.sbuf_tensor(name, shape, dt))

        def sem(name):
            return ctx.enter_context(nc.semaphore(name))

        ident = sb("ident", [P, P])
        ones = sb("ones", [P, P])
        masks = sb("masks", [P, len(LEVELS), P], U8)
        vecT = sb("vecT", [P, 48])
        lbt = sb("lbt", [P, 2, HEADS])
        omlb = sb("omlb", [P, 2, HEADS])
        lamt = sb("lamt", [P, 16])
        subw = sb("subw", [P, 2])
        eps_t = sb("eps_t", [P, 1])
        stat = sb("stat", [P, 16])
        bend = sb("bend", [P, HEADS])
        rt = sb("rt", [P, 216])
        rti = sb("rti", [P, 32], U32)
        regs = sb("regs", [P, 8], I32)
        MAP = 51800
        base = nc.sbuf_base
        sb("plan", [P, MAP])

        def at(name, word, shape, dt=F32):
            assert word + int(np.prod(shape[1:])) <= MAP, name
            return nc.alloc_sbuf_tensor_at(name, shape, dt, offset=base + 4 * word)

        W_TILES = HRING // 2 * HSLOT
        W_SPLIT = HRING * HSLOT
        W_HT = W_SPLIT + 2 * NW * UNIT
        W_X = W_HT + DC * T
        W_VTOK = W_X + 2 * DC * T
        W_BIAS = W_VTOK + 6 * HW
        W_END = W_BIAS + HEADS * T
        ring = at("ring", 0, [P, HRING * HSLOT])
        tiles = at("tiles", W_TILES, [P, 12 * HEADS * T])
        WH = at("w_hi", W_SPLIT, [P, NW, UNIT], F32R)
        WL = at("w_lo", W_SPLIT + NW * UNIT, [P, NW, UNIT], F32R)
        hT = at("hT", W_HT, [P, DC, T])
        XH = at("x_hi", W_X, [P, DC, T], F32R)
        XL = at("x_lo", W_X + DC * T, [P, DC, T], F32R)
        scores = at("hgrn_scores", W_X, [P, DC * T])
        vtok = at("vtok", W_VTOK, [P, 2, 3, HW])
        bias = at("bias", W_BIAS, [P, HEADS, T])
        small = at("small", W_END, [P, 2 * 2 * T + 2 * T + 3 * P])
        act_hi = at("act_hi", W_TILES, [P, FC, T], F32R)
        act_lo = at("act_lo", W_TILES + FC * T, [P, FC, T], F32R)
        xg_hi = at("xg_hi", W_X + DC * T, [P, DC, P], F32R)
        xg_lo = at("xg_lo", W_X + DC * T + D, [P, DC, P], F32R)
        h_tok = at("h_tok", W_VTOK, [P, 2, D])
        HE = at("expert_h", W_VTOK + 2 * D, [P, 2, SL])
        u_tok = at("u_tok", W_X, [P, 2, D])
        norm_w = at("norm_w", W_BIAS, [P, D])
        u_tokT = at("u_tokT", W_HT, [P, DC, 2 * P])
        junk = at("junk", W_HT, [P, D])
        y_sb = at("expert_y", W_HT + D, [P, D])
        SGE = at("expert_silu", W_END, [P, 2, SL])
        het_hi = at("expert_hT_hi", W_END + 2 * SL, [P, 2, SL], F32R)
        het_lo = at("expert_hT_lo", W_END + 4 * SL, [P, 2, SL], F32R)
        tabs = at("expert_tables", W_END + 6 * SL, [P, 8 * P + DC * NE])
        scratch = nc.dram_tensor("bias_rows", [HEADS, P, RELW], F32, kind="Internal")

        def tile(i, n=1):
            return tiles[:, i * HEADS * T:(i + n) * HEADS * T]

        def heads(i):
            return tile(i).rearrange("p (h t) -> p h t", h=HEADS)

        DQ, DK, DV, HV = heads(0), heads(1), heads(2), heads(3)
        EF, SG, Q, G, K, LF, B, ODA = (heads(i) for i in range(4, 12))
        X = [DQ, DK]
        DD = [DV, HV]
        TMP = DV
        OHG = K
        KEND, QB = EF, SG
        VEC = tile(4)[0:48, 0:P]
        ONEHOT = tile(5)[0:33, 0:RELW]
        REL = tile(6)[0:33, 0:HEADS]
        RELROW = tile(7)[0:HEADS, 0:RELW]
        LAMIN = tile(8)[:, 0:512]
        LAMP = tile(9)[:, 0:256]
        XTOK = tile(10, 2)[:, 0:2 * D].rearrange("p (t d) -> p t d", t=2)
        MTOK = tile(2)[0:META, 0:D]
        MASKF = tile(3)[:, 0:len(LEVELS) * P].rearrange("p (v t) -> p v t", t=P)
        SQ = tile(0, 2).rearrange("p (c t) -> p c t", c=DC)
        UF = tile(2, 2).rearrange("p (c t) -> p c t", c=DC)
        rstd = SQ[:, 0, :]
        S2 = [small[:, i * 2 * T:(i + 1) * 2 * T].rearrange("p (c t) -> p c t", c=2) for i in (0, 1)]
        AA = [small[:, 4 * T + i * T:4 * T + (i + 1) * T] for i in (0, 1)]
        AT = small[:, 6 * T:6 * T + 3 * P].rearrange("p (g q) -> p g q", g=3)
        KTOK = small[:, 0:2 * HW].rearrange("p (g n) -> p g n", g=2)
        ST = [scores[:, 2 * HW:2 * HW + 64].rearrange("p (h t) -> p h t", h=HEADS),
              scores[:, 0:HW].rearrange("p (h t) -> p h t", h=HEADS),
              scores[:, HW:2 * HW].rearrange("p (h t) -> p h t", h=HEADS)]
        STATE = [scores[:, 2 * HW + 64 + i * HW:2 * HW + 64 + (i + 1) * HW].rearrange("p (h v) -> p h v", h=HEADS)
                 for i in (0, 1)]
        SGF = tile(11).rearrange("p (b t) -> p b t", b=JC)
        ACTF = small[:, 0:2 * T].rearrange("p (b t) -> p b t", b=2)
        HTOK, UTOK, UTR, NFW, FNW, YS, JUNK, OUTT = h_tok, u_tok, u_tokT, norm_w, norm_w, y_sb, junk, u_tok
        PH, PG, PT = (tabs[:, 2 * i * P:2 * (i + 1) * P].rearrange("p (t s) -> p t s", t=2) for i in range(3))
        IOTA = tabs[:, 6 * P:7 * P]
        UPPER = tabs[:, 7 * P:8 * P]
        ROUT = tabs[:, 8 * P:8 * P + DC * NE].rearrange("p (c e) -> p c e", c=DC)

        def cols(at, n):
            return rt[:, at:at + n]
        LG = cols(0, 16).rearrange("p (t e) -> p t e", t=2)
        MX = cols(16, 16).rearrange("p (t e) -> p t e", t=2)
        IDXF = cols(32, 4).rearrange("p (t k) -> p t k", t=2)
        OH = cols(36, 32).rearrange("p (t k e) -> p t k e", t=2, k=2)
        MASK = cols(68, 16).rearrange("p (t e) -> p t e", t=2)
        GATE2 = cols(84, 4).rearrange("p (t k) -> p t k", t=2)
        RM = cols(88, 24).rearrange("p (t i) -> p t i", t=2)
        GX = cols(112, 24).rearrange("p (t i) -> p t i", t=2)
        CNT = cols(136, 8)
        OV = cols(144, 8)
        CUM = cols(152, 8)
        SEL = cols(160, 8)
        TMP8 = cols(168, 16).rearrange("p (t e) -> p t e", t=2)
        EID = cols(184, 4)
        ONE8 = cols(188, 8)
        IOTA8 = cols(196, 8)
        RSUM = cols(204, 4)
        TMPG = cols(208, 8)

        banks = [ctx.enter_context(nc.psum_tensor(f"bank{i}", [P, 512], F32)) for i in range(8)]

        g_full = [sem(f"general_full{i}") for i in range(NGB)]
        g_drained = [sem(f"general_drained{i}") for i in range(NGB)]

        def gbank(task):
            return banks[TURN[task] % NGB]

        def full(eng, task):
            i = TURN[task]
            eng.wait_ge(g_full[i % NGB], i // NGB + 1)

        def drained(eng, task):
            i = TURN[task]
            eng.wait_ge(g_drained[i % NGB], i // NGB + 1)

        def drain(ins, task):
            return ins.then_inc(g_drained[TURN[task] % NGB], 1)

        slot_full = [sem(f"slot_full{i}") for i in range(RING)]
        half_full = [sem(f"half_slot_full{i}") for i in range(HRING)]
        hi_ready = sem("weights_hi_ready")
        lo_ready = sem("weights_lo_ready")
        unit_done = sem("unit_done")
        down_full = sem("dense_down_full")
        down_drained = sem("dense_down_drained")
        uf_ready = sem("u_float_ready")
        xh_ready = sem("u_hi_ready")
        mh_ready = sem("mix_hi_ready")
        ah_ready = sem("act_hi_ready")
        al_ready = sem("act_lo_ready")

        def slot(n):
            return ring[:, (n % RING) * SLOT:(n % RING + 1) * SLOT]

        def half_slot(g):
            return ring[:, (g % HRING) * HSLOT:(g % HRING + 1) * HSLOT]

        def unit_used(eng, n):
            end = UNITS[n][4]
            if end[0] == "count":
                eng.wait_ge(unit_done, end[1])
            elif end[0] == "down":
                eng.wait_ge(down_full, 4 * end[1] + 4)
            else:
                full(eng, end)

        def unit_source(n):
            slot_n, kind, i, width, _ = UNITS[n]
            if kind == "cols":
                w = slot(slot_n)[:, 0:DC * width].rearrange("p (c n) -> p c n", c=DC)
                return w[:, :, i * P:(i + 1) * P], DC
            return slot(slot_n)[:, 2 * i * HW:(2 * i + 2) * HW].rearrange("p (c n) -> p c n", c=2), 2

        def split(buffer, n, chunks):
            return buffer[:, n % NW, :].rearrange("p (c n) -> p c n", c=chunks)

        def expert_unit_used(eng, n, m):
            kind, s = EXPERT[m // 4]
            if m % 4 < 3:
                eng.wait_ge(unit_done, UNITS_COUNTED + n * COUNTED + 3 * (m // 4) + m % 4 + 1)
            elif kind == "w1":
                eng.wait_ge(G_full[s % 2], n * G_USES[s % 2] + s // 2 + 2)
            elif kind == "w3":
                eng.wait_ge(U_full[s % 2], n * U_USES[s % 2] + s // 2 + 1)
            else:
                eng.wait_ge(down_done, n * NS + s + 2)

        def split_hi(act, n):
            if n >= len(UNITS):
                return
            src, chunks = unit_source(n)
            act.wait_ge(slot_full[UNITS[n][0] % RING], 16 * (UNITS[n][0] // RING + 1))
            if n >= NW:
                unit_used(act, n - NW)
            act.copy(split(WH, n, chunks), src).then_inc(hi_ready, 1)

        def split_lo(dve, n):
            if n >= len(UNITS):
                return
            src, chunks = unit_source(n)
            dve.wait_ge(hi_ready, n + 1)
            dve.tensor_tensor(split(WL, n, chunks), src, split(WH, n, chunks).bitcast(F32),
                              ALU.subtract).then_inc(lo_ready, 1)

        consts_in = sem("consts_in")
        vec_in = sem("vec_in")
        x_in = sem("x_in")
        rows_out = sem("bias_rows_written")
        bias_in = sem("bias_in")
        lam_in = sem("lambda_in")
        tables_in = sem("expert_tables_in")
        fnw_in = sem("final_norm_in")
        init_done = sem("init_done")
        sq_ready = sem("squares_ready")
        rstd_ready = sem("rstd_ready")
        u_ready = sem("u_ready")
        lam_ready = sem("lambda_ready")
        score_full = sem("attention_scores_full")
        biased = sem("attention_biased")
        exp_done = sem("attention_exp_done")
        a_ready = sem("attention_weights_ready")
        aT_full = sem("attention_weightsT_full")
        aT_drained = sem("attention_weightsT_drained")
        av_full = sem("attention_out_full")
        av_drained = sem("attention_out_drained")
        f_exp = sem("forget_exp_ready")
        f_sig = sem("forget_sigmoid_ready")
        f_gate = sem("forget_gate_ready")
        f_log = sem("forget_log_ready")
        k_ready = sem("k_ready")
        b_ready = sem("b_ready")
        t_clamped = sem("silu_clamped")
        t_sig = sem("silu_sigmoid_ready")
        qg_ready = sem("silu_ready")
        expb = sem("exp_b_ready")
        qb_ready = sem("qb_ready")
        kdiff = sem("kend_difference_ready")
        kexp = sem("kend_exp_ready")
        kend_ready = sem("kend_ready")
        st_zero = sem("scores_zeroed")
        diff_ready = sem("level_difference_ready")
        decay_ready = sem("level_decay_ready")
        xq_ready = sem("level_q_ready")
        xk_ready = sem("level_k_ready")
        lv_full = sem("level_scores_full")
        lv_drained = sem("level_scores_drained")
        mix_sq = sem("mix_squares_ready")
        mix_rstd = sem("mix_rstd_ready")
        mix_ready = sem("mix_ready")
        tok_sum = sem("token_sum_ready")
        tok_rstd = sem("token_rstd_ready")
        utok_ready = sem("u_token_ready")
        top_ready = sem("top_values_ready")
        gate_exp = sem("gate_exp_ready")
        mask_ready = sem("mask_ready")
        regs_ready = sem("registers_ready")
        p_ready = sem("onehot_ready")
        pg_ready = sem("gated_onehot_ready")
        G_full = [sem(f"gate_full{i}") for i in (0, 1)]
        G_free = [sem(f"gate_free{i}") for i in (0, 1)]
        U_full = [sem(f"up_full{i}") for i in (0, 1)]
        scatter_added = [sem(f"scatter_added{i}") for i in (0, 1)]
        col_ready = sem("routing_column_ready")
        het_hi_ready = sem("expert_hT_hi_ready")
        he_ready = sem("expert_h_ready")
        heT_full = sem("expert_hT_full")
        heT_ready = sem("expert_hT_ready")
        down_done = sem("expert_down_done")
        y_half_full = sem("expert_y_half_full")
        y_ready = [sem(f"expert_y_ready{i}") for i in (0, 1)]
        pT_full = sem("scatter_onehot_full")
        pT_ready = sem("scatter_onehot_ready")
        xg_hi_ready = sem("gathered_hi_ready")
        mix_float = sem("mix_float_ready")
        out_ready = sem("out_ready")
        out_written = sem("out_written")
        dve_step = sem("dve_step")
        act_step = sem("act_step")
        pool_step = sem("pool_step")

        def chain(eng, signal):
            count = [0]

            def link(ins):
                count[0] += 1
                ins.then_inc(signal, 1)
                eng.wait_ge(signal, count[0])
            return link

        def level_part(x, m, half):
            if m <= 8:
                return x.rearrange("p h (n two m) -> p (h n) two m", two=2, m=m)[:, :, half, :]
            return x[:, :, META:T].rearrange("p h (n two m) -> p h n two m", two=2, m=m)[:, :, :, half, :]

        w_in = A["w_in"].rearrange("l (c p) n -> l p c n", p=P)
        w_out = A["w_out"].rearrange("l (c p) n -> l p c n", p=P)
        d1 = A["dense_w1"][0].rearrange("(c p) n -> p c n", p=P)
        d3 = A["dense_w3"][0].rearrange("(c p) n -> p c n", p=P)
        d2 = A["dense_w2"][0].rearrange("(c p) n -> p c n", p=P)
        e1 = A["moe_w1"][0].rearrange("e (c p) n -> e p c n", p=P)
        e3 = A["moe_w3"][0].rearrange("e (c p) n -> e p c n", p=P)
        e2 = A["moe_w2"][0].rearrange("e (c p) n -> e p c n", p=P)

        block = ctx.enter_context(nc.Block())

        @block.sync
        def _(sp):
            sp.dma_start(XTOK, A["x"][0].rearrange("(t p) d -> p t d", p=P)).then_inc(x_in, 16)
            sp.dma_start(MTOK, A["meta"]).then_inc(x_in, 16)
            for n, (kind, i) in enumerate(PREFIX):
                if n >= RING:
                    sp.wait_ge(lo_ready, LAST_UNIT[n - RING] + 1)
                if kind == "w_in":
                    c0 = PROJ[i[1]] * HW
                    src = w_in[i[0]][:, :, c0:c0 + HW]
                elif kind == "w_out":
                    src = w_out[i[0]][:, :, i[1] * HW:(i[1] + 1) * HW]
                elif kind == "w2":
                    src = d2[:, 8 * i[1]:min(8 * i[1] + 8, FC), i[0] * HW:(i[0] + 1) * HW]
                else:
                    src = (d1 if kind == "w1" else d3)[:, :, i * SL:min((i + 1) * SL, FD)]
                dst = slot(n)[:, 0:src.shape[1] * src.shape[2]].rearrange("p (c n) -> p c n", c=src.shape[1])
                sp.dma_start(dst, src).then_inc(slot_full[n % RING], 16)

            def half_load(m, expert):
                kind, s = EXPERT[m // 2]
                if kind == "w2":
                    c = s * JC + (m % 2) * 2
                    sp.dma_start(half_slot(m).rearrange("p (c n) -> p c n", c=2),
                                 e2[expert, :, c:c + 2, :]).then_inc(half_full[m % HRING], 16)
                else:
                    c = (m % 2) * 4
                    sp.dma_start(half_slot(m).rearrange("p (c n) -> p c n", c=4),
                                 (e1 if kind == "w1" else e3)[expert, :, c:c + 4, s * SL:(s + 1) * SL]
                                 ).then_inc(half_full[m % HRING], 16)

            def load_when_split(m, expert, blk):
                sp.wait_ge(lo_ready, len(UNITS) + blk * BLOCK_UNITS + 2 * (m - HRING) + 2)
                half_load(m, expert)

            def block_load(expert, blk, after):
                for m in range(EARLY, BLOCK_HALVES):
                    load_when_split(m, expert, blk)
                for m in range(EARLY):
                    load_when_split(m, after, blk + 1)

            for m in range(BLOCK_HALVES):
                if m < 2 * RING:
                    sp.wait_ge(lo_ready, LAST_UNIT[len(PREFIX) - RING + m // 2] + 1)
                elif m == HRING // 2:
                    sp.wait_ge(mix_ready, 16)
                elif m >= HRING:
                    sp.wait_ge(lo_ready, len(UNITS) + 2 * (m - HRING) + 2)
                half_load(m, 0)
            for m in range(EARLY):
                load_when_split(m, 1, 1)
            with sp.Fori(1, NE - 1) as e:
                block_load(e, e, e + 1)
            sp.wait_ge(regs_ready, 1)
            over = sp.value_load(regs[0:1, 0:1], min_val=0, max_val=OVER)
            eids = [sp.value_load(regs[0:1, 1 + j:2 + j], min_val=0, max_val=NE - 1) for j in range(OVER)]
            block_load(NE - 1, NE - 1, eids[0])
            for j in range(OVER):
                with sp.If(over > j):
                    block_load(eids[j], NE + j, eids[min(j + 1, OVER - 1)])
            sp.wait_ge(out_ready, 1)
            sp.dma_start(out[0].rearrange("(t p) d -> p t d", p=P), OUTT[:, :, :]).then_inc(out_written, 16)
            sp.wait_ge(out_written, 16)

        @block.tensor
        def _(pe):
            def bank_free(task):
                i = TURN[task]
                if i >= NGB:
                    pe.wait_ge(g_drained[i % NGB], i // NGB)

            def fin(ins, task):
                ins.then_inc(g_full[TURN[task] % NGB], 1)

            pe.wait_ge(consts_in, 32)
            pe.wait_ge(vec_in, 16 * 7)
            pe.transpose(gbank(("vec",))[:, 0:44], VEC[0:44, :], ident[0:44, 0:44]).then_inc(
                g_full[TURN[("vec",)] % NGB], 1)
            pe.wait_ge(init_done, 1)
            fin(pe.matmul(gbank(("rel",))[0:HEADS, 0:RELW], REL, ONEHOT, start=True, stop=True), ("rel",))
            pe.wait_ge(x_in, 32)
            for c in range(DC):
                task = ("xT", c)
                bank_free(task)
                pe.transpose(gbank(task)[:, 0:META], MTOK[:, c * P:(c + 1) * P], ident[0:META, 0:META])
                for t in (0, 1):
                    i = pe.transpose(gbank(task)[:, META + t * P:META + (t + 1) * P],
                                     XTOK[:, t, c * P:(c + 1) * P], ident[:, :])
                fin(i, task)

            def sum_squares(k):
                task = ("ssq", k)
                bank_free(task)
                for c in range(DC):
                    pe.wait_ge(sq_ready, DC * k + c + 1)
                    i = pe.matmul(gbank(task)[:, 0:T], ones[:, :], SQ[:, c, :], start=c == 0, stop=c == DC - 1)
                fin(i, task)

            def split_products(out, w_first, pairs, start, stop):
                for k, (wh, wl, xh, xl) in enumerate(pairs):
                    for p, (w, x) in enumerate(((wh, xh), (wh, xl), (wl, xh))):
                        i = pe.matmul(out, *((w, x) if w_first else (x, w)), start=start and k == 0 and p == 0,
                                      stop=stop and k == len(pairs) - 1 and p == 2)
                return i

            def product(task):
                n = UNIT_OF[task]
                wh, wl = split(WH, n, DC), split(WL, n, DC)
                bank_free(task)
                pe.wait_ge(lo_ready, n + 1)
                fin(split_products(gbank(task)[:, 0:T], True,
                                   [(wh[:, c, :], wl[:, c, :], XH[:, c, :], XL[:, c, :]) for c in range(DC)],
                                   True, True), task)

            def project(l, s, j):
                product(("proj", l, s, j))

            def to_tokens(l, name, src, k):
                for g, (t0, tn) in enumerate(SEG):
                    task = ("vt", l, name, g)
                    bank_free(task)
                    for h in range(HEADS):
                        i = pe.transpose(gbank(task)[0:tn, h * P:(h + 1) * P], src[:, h, t0:t0 + tn], ident[:, :])
                    fin(i, task)

            units0 = 0
            lv0 = 0
            av0 = 0
            for l in (0, 1):
                sum_squares(2 * l)
                pe.wait_ge(u_ready, DC * (2 * l + 1))
                for s in ORDER1:
                    for j in range(JC):
                        project(l, s, j)
                drained(pe, ("proj", l, "dv", JC - 1))
                to_tokens(l, "dv", DV, 0)

                units = attention_units(l)

                def score(i):
                    q, h = units[i]
                    q0, qn = SEG[q]
                    kn = q0 + qn
                    if units0 + i > 0:
                        pe.wait_ge(biased, units0 + i)
                    for c in (0, 1):
                        r = slice(64 * c, 64 * c + 64)
                        ins = pe.matmul(banks[3 + c][0:qn, 0:kn], DQ[r, h, q0:q0 + qn], DK[r, h, 0:kn],
                                        start=True, stop=True)
                    ins.then_inc(score_full, 1)

                def weights_t(i):
                    q, h = units[i]
                    qn = SEG[q][1]
                    pe.wait_ge(a_ready, units0 + i + 1)
                    if units0 + i > 0:
                        pe.wait_ge(aT_drained, units0 + i)
                    for g in range(q + 1):
                        k0, kn = SEG[g]
                        ins = pe.transpose(banks[5][0:kn, g * P:g * P + qn], AA[i % 2][0:qn, k0:k0 + kn],
                                           ident[0:qn, 0:qn])
                    ins.then_inc(aT_full, 1)

                def weigh_v(i):
                    q, h = units[i]
                    qn = SEG[q][1]
                    n = av0 + i // HEADS
                    pe.wait_ge(aT_drained, units0 + i + 1)
                    if h == 0 and n >= 2:
                        pe.wait_ge(av_drained, n - 1)
                    for g in range(q + 1):
                        kn = SEG[g][1]
                        ins = pe.matmul(banks[6 + n % 2][:, h * P:h * P + qn], vtok[0:kn, 0, g, h * P:(h + 1) * P],
                                        AT[0:kn, g, 0:qn], start=g == 0, stop=g == q)
                    ins.then_inc(av_full, 1)

                if l == 0:
                    pe.wait_ge(bias_in, 16)
                drained(pe, ("vt", l, "dv", 2))
                for i in range(16):
                    project(l, ORDER2[i // 4], i % 4)
                    if i < len(units):
                        score(i)
                    if 0 <= i - 2 < len(units):
                        weights_t(i - 2)
                    if 0 <= i - 3 < len(units):
                        weigh_v(i - 3)
                drained(pe, ("proj", l, "hv", JC - 1))
                to_tokens(l, "hv", HV, 1)
                pe.wait_ge(kend_ready, l + 1)
                for g in (0, 1):
                    t0, tn = SEG[g]
                    task = ("kt", l, g)
                    bank_free(task)
                    for h in range(HEADS):
                        i = pe.transpose(gbank(task)[0:tn, h * P:(h + 1) * P], KEND[:, h, t0:t0 + tn], ident[:, :])
                    fin(i, task)
                for g in (0, 1):
                    tn = SEG[g][1]
                    task = ("state", l, g)
                    drained(pe, ("kt", l, g))
                    drained(pe, ("vt", l, "hv", g))
                    bank_free(task)
                    for h in range(HEADS):
                        i = pe.matmul(gbank(task)[:, h * P:(h + 1) * P], KTOK[0:tn, g, h * P:(h + 1) * P],
                                      vtok[0:tn, 1, g, h * P:(h + 1) * P], start=True, stop=True)
                    fin(i, task)
                levels = level_tasks(l)
                pe.wait_ge(k_ready, l + 1)
                pe.wait_ge(qg_ready, 2 * l + 1)
                for i, (v, g) in enumerate(levels):
                    t0, tn = SEG[g]
                    n = lv0 + i
                    if i < 2:
                        pe.wait_ge(av_drained, av0 + len(units) // HEADS)
                    if n >= 2:
                        pe.wait_ge(lv_drained, n - 1)
                    if v > 0:
                        pe.wait_ge(xq_ready, 7 * l + v)
                        pe.wait_ge(xk_ready, 7 * l + v)
                    for h in range(HEADS):
                        lo = K if v == 0 else X[v % 2]
                        hi = Q if v == 0 else X[v % 2]
                        ins = pe.matmul(banks[6 + n % 2][0:tn, h * P:h * P + tn], lo[:, h, t0:t0 + tn],
                                        hi[:, h, t0:t0 + tn], start=True, stop=True)
                    ins.then_inc(lv_full, 1)
                pe.wait_ge(lv_drained, lv0 + len(levels))
                pe.wait_ge(qb_ready, l + 1)
                for g in segs_out(l):
                    t0, tn = SEG[g]
                    task = ("o", l, g)
                    drained(pe, ("vt", l, "hv", g))
                    if g > 0:
                        drained(pe, ("state", l, g - 1))
                    bank_free(task)
                    for h in range(HEADS):
                        o = gbank(task)[:, h * P:h * P + tn]
                        i = pe.matmul(o, vtok[0:tn, 1, g, h * P:(h + 1) * P], ST[g][0:tn, h, :], start=True,
                                      stop=g == 0)
                        if g > 0:
                            i = pe.matmul(o, STATE[g - 1][:, h, :], QB[:, h, t0:t0 + tn], start=False, stop=True)
                    fin(i, task)
                o0 = 0 if l == 0 else META
                for n, c in enumerate((4, 5, 6, 7, 0, 1, 2, 3)):
                    task = ("ms", l, c)
                    pe.wait_ge(mix_sq, 2 * l + (1 if c >= 4 else 2))
                    src = LF if c >= 4 else DQ
                    bank_free(task)
                    fin(pe.matmul(gbank(task)[:, o0:T], ones[:, :], src[:, c % 4, o0:T], start=True, stop=True), task)
                units0 += len(units)
                lv0 += len(levels)
                av0 += len(units) // HEADS
                if l == 0:
                    pe.wait_ge(mix_ready, 8)
                    for d in range(DC):
                        product(("wo", d))
                    sum_squares(1)
                    pe.wait_ge(u_ready, 2 * DC)
                    for i in range(0, FC, JC):
                        for k in ("g", "u"):
                            for f in range(i, min(i + JC, FC)):
                                product((k, f))
                    drained(pe, ("u", FC - 1))
                    for half in (0, 1):
                        for u in range(FC // 2):
                            n = UNIT_OF[("down", 1)] - (2 - half) * (FC // 2) + 1 + u
                            wh, wl = split(WH, n, 2), split(WL, n, 2)
                            pe.wait_ge(lo_ready, n + 1)
                            pe.wait_ge(al_ready, 2 * u + 2)
                            for d in range(4):
                                c = slice(d * P, (d + 1) * P)
                                i = split_products(banks[(3 + 4 * half + d) % 8][:, 0:T], True,
                                                   [(wh[:, k, c], wl[:, k, c], act_hi[:, 2 * u + k, :],
                                                     act_lo[:, 2 * u + k, :]) for k in (0, 1)],
                                                   u == 0, u == FC // 2 - 1)
                                if u == FC // 2 - 1:
                                    i.then_inc(down_full, 1)
                            if u < FC // 2 - 1:
                                i.then_inc(unit_done, 1)
                    pe.wait_ge(down_drained, 8)
            for t in (0, 1):
                for g in (0, 1):
                    task = ("hTt", t, g)
                    bank_free(task)
                    for c in range(4):
                        i = pe.transpose(gbank(task)[:, c * P:(c + 1) * P],
                                         hT[:, 4 * g + c, META + t * P:META + (t + 1) * P], ident[:, :])
                    fin(i, task)
            pe.wait_ge(mix_ready, 16)
            for half in (0, 1):
                for t in (0, 1):
                    bank_free(("wo1", half, t))
                for u in range(DC // 2):
                    n = UNIT_OF[("wo1", 1, 1)] - (2 - half) * (DC // 2) + 1 + u
                    wh, wl = split(WH, n, 2), split(WL, n, 2)
                    pe.wait_ge(lo_ready, n + 1)
                    last = u == DC // 2 - 1
                    for t in (0, 1):
                        task = ("wo1", half, t)
                        r = slice(META + t * P, META + (t + 1) * P)
                        i = split_products(gbank(task)[:, :], False,
                                           [(wh[:, k, :], wl[:, k, :], XH[:, 2 * u + k, r], XL[:, 2 * u + k, r])
                                            for k in (0, 1)], u == 0, last)
                        if last:
                            fin(i, task)
                    if not last:
                        i.then_inc(unit_done, 1)
            for t in (0, 1):
                pe.wait_ge(utok_ready, t + 1)
                for g in (0, 1):
                    task = ("rT", t, g)
                    bank_free(task)
                    for c in range(4):
                        i = pe.transpose(gbank(task)[:, c * P:(c + 1) * P], UTOK[:, t, (4 * g + c) * P:(4 * g + c + 1) * P],
                                         ident[:, :])
                    fin(i, task)
            pe.wait_ge(tables_in, 16 * 4)
            for t in (0, 1):
                task = ("logit", t)
                drained(pe, ("rT", t, 0))
                drained(pe, ("rT", t, 1))
                bank_free(task)
                for c in range(DC):
                    i = pe.matmul(gbank(task)[:, 0:NE], UTR[:, c, t * P:(t + 1) * P], ROUT[:, c, :],
                                  start=c == 0, stop=c == DC - 1)
                fin(i, task)
            pe.wait_ge(mask_ready, 2)
            task = ("rank", 0)
            bank_free(task)
            fin(pe.matmul(gbank(task)[:, 0:NE], UPPER, MASK[:, 0, :], start=True, stop=True), task)
            for task, first in ((("rank", 1), UPPER), (("cnt",), ones[:, :])):
                bank_free(task)
                pe.matmul(gbank(task)[:, 0:NE], ones[:, :], MASK[:, 0, :], start=True, stop=False)
                fin(pe.matmul(gbank(task)[:, 0:NE], first, MASK[:, 1, :], start=False, stop=True), task)
            drained(pe, ("rank", 0))
            drained(pe, ("rank", 1))
            drained(pe, ("cnt",))

            def gather(n, wait_banks):
                pe.wait_ge(p_ready, n + 1)
                for b in (0, 1):
                    if wait_banks:
                        pe.wait_ge(G_free[b], n * G_USES[b])
                    for c in range(4):
                        o = banks[b][:, c * P:(c + 1) * P]
                        for t in (0, 1):
                            i = pe.matmul(o, UTOK[:, t, (4 * b + c) * P:(4 * b + c + 1) * P], PH[:, t, :],
                                          start=t == 0, stop=t == 1)
                    i.then_inc(G_full[b], 1)

            def expert_block(n):
                def unit_in(key, u):
                    m = 4 * EXPERT_AT[key] + u
                    pe.wait_ge(lo_ready, len(UNITS) + n * BLOCK_UNITS + m + 1)
                    return (split(b, len(UNITS) + m, 1 if key[0] == "w2" else 2) for b in (WH, WL))

                def up(kind, s):
                    b = s % 2
                    bank0, fulls = (0, G_full) if kind == "w1" else (2, U_full)
                    if kind == "w1":
                        pe.wait_ge(G_free[b], n * G_USES[b] + s // 2 + 1)
                    elif s >= 2:
                        pe.wait_ge(he_ready, n * NS + s - 1)
                    else:
                        pe.wait_ge(scatter_added[b], 2 * n + 1)
                    for u in range(4):
                        wh, wl = unit_in((kind, s), u)
                        i = split_products(banks[bank0 + b][:, :], False,
                                           [(wh[:, k, :], wl[:, k, :], xg_hi[:, 2 * u + k, :], xg_lo[:, 2 * u + k, :])
                                            for k in (0, 1)], u == 0, u == 3)
                        i.then_inc(unit_done if u < 3 else fulls[b], 1)

                def turn_h(s):
                    pe.wait_ge(he_ready, n * NS + s + 1)
                    if s > 0:
                        pe.wait_ge(heT_ready, n * NS + s)
                    for j in range(JC):
                        i = pe.transpose(banks[4][:, j * P:(j + 1) * P], HE[:, s % 2, j * P:(j + 1) * P], ident[:, :])
                    i.then_inc(heT_full, 1)

                def down_part(s, j, half):
                    wh, wl = unit_in(("w2", s), j)
                    c = slice(j * P, (j + 1) * P)
                    d = slice(half * 512, (half + 1) * 512)
                    return split_products(banks[5 + half][:, :], False,
                                          [(wh[:, 0, d], wl[:, 0, d], het_hi[:, s % 2, c], het_lo[:, s % 2, c])],
                                          s == 0 and j == 0, s == NS - 1 and j == JC - 1)

                def down(s):
                    pe.wait_ge(heT_ready, n * NS + s + 1)
                    for j in range(JC):
                        down_part(s, j, 0)
                        down_part(s, j, 1).then_inc(unit_done if j < JC - 1 else down_done, 1)

                def down_last():
                    s = NS - 1
                    pe.wait_ge(heT_ready, n * NS + s + 1)
                    for j in range(JC):
                        i = down_part(s, j, 0)
                    i.then_inc(y_half_full, 1)
                    for j in range(JC):
                        down_part(s, j, 1).then_inc(unit_done if j < JC - 1 else down_done, 1)

                pe.wait_ge(G_free[1], n * G_USES[1] + 1)
                for s in range(NS):
                    up("w1", s)
                    if s == 0:
                        pe.wait_ge(pg_ready, n + 1)
                        for t in (0, 1):
                            i = pe.transpose(banks[7][:, t * P:(t + 1) * P], PG[:, t, :], ident[:, :])
                        i.then_inc(pT_full, 1)
                    else:
                        turn_h(s - 1)
                    up("w3", s)
                    if s > 0:
                        down(s - 1)
                turn_h(NS - 1)
                gather(n + 1, True)
                down_last()
                pe.wait_ge(pT_ready, n + 1)
                for half in (0, 1):
                    pe.wait_ge(y_ready[half], n + 1)
                    for t in (0, 1):
                        if half == 1:
                            pe.wait_ge(scatter_added[t], 2 * n + 2)
                        pe.matmul(banks[2 + t][:, :], PT[:, t, :], YS[:, half * 512:(half + 1) * 512],
                                  start=True, stop=True).then_inc(U_full[t], 1)

            gather(0, False)
            with pe.Fori(0, NE) as e:
                expert_block(e)
            pe.wait_ge(regs_ready, 1)
            over = pe.value_load(regs[0:1, 0:1], min_val=0, max_val=OVER)
            for j in range(OVER):
                with pe.If(over > j):
                    expert_block(NE + j)

        @block.scalar
        def _(act):
            link = chain(act, act_step)
            act.preload_act_table_set("natural_log_exp_and_others")
            act.dma_start(VEC[0:16, :], A["norm_mix"].rearrange("l (c p) -> (l c) p", p=P)).then_inc(vec_in, 16)
            act.dma_start(VEC[16:32, :], A["norm_ffn"].rearrange("l (c p) -> (l c) p", p=P)).then_inc(vec_in, 16)
            act.dma_start(VEC[32:40, :], A["hg_lb_logits"].rearrange("l (c p) -> (l c) p", p=P)).then_inc(vec_in, 16)
            act.dma_start(VEC[40:42, :], A["hg_norm_w"]).then_inc(vec_in, 16)
            act.dma_start(VEC[42:44, :], A["da_subln_w"]).then_inc(vec_in, 16)
            act.dma_start(REL[0:32, :], A["rel_bias"]).then_inc(vec_in, 16)
            act.dma_start(ONEHOT, A["buckets"]).then_inc(vec_in, 16)
            act.dma_start(ident[:, :], A["ident"]).then_inc(consts_in, 16)
            act.dma_start(MASKF, A["masks"]).then_inc(consts_in, 16)
            act.dma_start(LAMIN, A["da_lambda"].rearrange("l a d -> (l a d)").partition_broadcast(P)).then_inc(lam_in, 16)
            full(act, ("rel",))
            drain(act.copy(RELROW, gbank(("rel",))[0:HEADS, 0:RELW]), ("rel",))
            drained(act, ("rel",))
            act.dma_start(scratch.ap(), RELROW.unsqueeze(1).to_broadcast([HEADS, P, RELW])).then_inc(rows_out, 16)
            act.wait_ge(rows_out, 16)
            shifted = scratch.ap().rearrange("h p j -> (h p j)")
            act.dma_start(bias[:, :, :], bass.AP(shifted.tensor, P - 1, [[RELW - 1, P], [P * RELW, HEADS], [1, T]])
                          ).then_inc(bias_in, 16)

            act.wait_ge(lam_ready, 1)
            act.activation(lamt[:, 4:8], lamt[:, 0:4], ACT.Exp).then_inc(lam_ready, 1)
            act.wait_ge(lam_ready, 3)
            act.activation(lbt[:, 1, :], lbt[:, 1, :], ACT.Exp).then_inc(lam_ready, 1)
            act.wait_ge(init_done, 2)

            def squares(k):
                if k == 0:
                    for c in range(DC):
                        drained(act, ("xT", c))
                        act.activation(SQ[:, c, :], hT[:, c, :], ACT.Square).then_inc(sq_ready, 1)
                inverse_root(k)

            def inverse_root(k):
                task = ("ssq", k)
                full(act, task)
                drain(act.activation(rstd, gbank(task)[:, 0:T], ACT.Ln, scale=1.0 / D, bias=eps_t[:, 0:1]), task)
                drained(act, task)
                act.activation(rstd, rstd, ACT.Exp, scale=-0.5).then_inc(rstd_ready, 1)

            def halves(k):
                for c in range(DC):
                    act.wait_ge(uf_ready, DC * k + c + 1)
                    act.copy(XH[:, c, :], UF[:, c, :]).then_inc(xh_ready, 1)

            def copy_proj(l, s, dst):
                for j in range(JC):
                    task = ("proj", l, s, j)
                    split_hi(act, UNIT_OF[task] + AHEAD)
                    full(act, task)
                    drain(act.copy(dst[:, j, :], gbank(task)[:, 0:T]), task)

            def copy_vt(l, name, k):
                for g, (t0, tn) in enumerate(SEG):
                    task = ("vt", l, name, g)
                    full(act, task)
                    drain(act.copy(vtok[0:tn, k, g, :], gbank(task)[0:tn, :]), task)

            units0 = 0
            av0 = 0
            for n in range(AHEAD):
                split_hi(act, n)
            for l in (0, 1):
                squares(2 * l)
                halves(2 * l)
                copy_proj(l, "dq", DQ)
                copy_proj(l, "dk", DK)
                copy_proj(l, "dv", DV)
                copy_vt(l, "dv", 0)
                units = attention_units(l)

                def exps(i):
                    q, h = units[i]
                    qn = SEG[q][1]
                    kn = SEG[q][0] + qn
                    b = i % 2
                    act.wait_ge(biased, units0 + i + 1)
                    for c in (0, 1):
                        ins = act.activation(S2[b][0:qn, c, 0:kn], S2[b][0:qn, c, 0:kn], ACT.Exp,
                                             bias=stat[0:qn, 4 * b + c:4 * b + c + 1],
                                             accum_out=stat[0:qn, 8 + 4 * b + c:8 + 4 * b + c + 1])
                    ins.then_inc(exp_done, 1)

                def copy_at(i):
                    q, h = units[i]
                    qn = SEG[q][1]
                    act.wait_ge(aT_full, units0 + i + 1)
                    if i > 0:
                        act.wait_ge(av_full, units0 + i)
                    for g in range(q + 1):
                        kn = SEG[g][1]
                        ins = act.copy(AT[0:kn, g, 0:qn], banks[5][0:kn, g * P:g * P + qn])
                    ins.then_inc(aT_drained, 1)

                def copy_av(i):
                    q = units[i][0]
                    t0, tn = SEG[q]
                    n = av0 + i // HEADS
                    act.wait_ge(av_full, units0 + i + 1)
                    act.copy(ODA[:, :, t0:t0 + tn],
                             banks[6 + n % 2][:, :].rearrange("p (h t) -> p h t", h=HEADS)[:, :, 0:tn]
                             ).then_inc(av_drained, 1)

                def sigmoid_of_tmp(i):
                    act.wait_ge(t_clamped, 2 * l + i + 1)
                    link(act.activation(TMP, TMP, ACT.Exp, scale=-1.0))
                    link(act.activation(TMP, TMP, ACT.Ln, bias=1.0))
                    act.activation(TMP, TMP, ACT.Exp, scale=-1.0).then_inc(t_sig, 1)

                dsts = {"hq": Q, "hg": G, "hv": HV}
                for i in range(16):
                    s, j = ORDER2[i // 4], i % 4
                    split_hi(act, UNIT_OF[("proj", l, s, j)] + AHEAD)
                    if i < len(units):
                        exps(i)
                    if s != "hf":
                        task = ("proj", l, s, j)
                        full(act, task)
                        drain(act.copy(dsts[s][:, j, :], gbank(task)[:, 0:T]), task)
                    if 0 <= i - 2 < len(units):
                        copy_at(i - 2)
                    if 0 <= i - 3 < len(units) and (i - 3) % HEADS == HEADS - 1:
                        copy_av(i - 3)
                    if i == 5:
                        drained(act, ("proj", l, "hf", JC - 1))
                        act.activation(EF, EF, ACT.Exp, scale=-1.0).then_inc(f_exp, 1)
                        act.wait_ge(f_exp, l + 1)
                        link(act.activation(SG, EF, ACT.Ln, bias=1.0))
                        act.activation(SG, SG, ACT.Exp, scale=-1.0).then_inc(f_sig, 1)
                    if i == 8:
                        act.wait_ge(f_gate, l + 1)
                        act.activation(LF, LF, ACT.Ln).then_inc(f_log, 1)
                    if i == 10:
                        sigmoid_of_tmp(0)
                    if i == 14:
                        act.wait_ge(b_ready, l + 1)
                        act.wait_ge(k_ready, l + 1)
                        act.wait_ge(kdiff, l + 1)
                        act.activation(SG, B, ACT.Exp).then_inc(expb, 1)
                        act.activation(bend[:, :], B[:, :, SEG[1][0] + P - 1], ACT.Exp).then_inc(expb, 1)
                        act.activation(KEND[:, :, 0:SEG[2][0]], KEND[:, :, 0:SEG[2][0]], ACT.Exp).then_inc(kexp, 1)
                sigmoid_of_tmp(1)
                copy_vt(l, "hv", 1)
                for g in (0, 1):
                    tn = SEG[g][1]
                    task = ("kt", l, g)
                    full(act, task)
                    drain(act.copy(KTOK[0:tn, g, :], gbank(task)[0:tn, :]), task)
                for v in range(1, len(LEVELS)):
                    m = LEVELS[v]
                    act.wait_ge(diff_ready, 7 * l + v)
                    for half in (0, 1):
                        part = level_part(DD[v % 2], m, half)
                        ins = act.activation(part, part, ACT.Exp, scale=1.0 if half else -1.0)
                    ins.then_inc(decay_ready, 1)
                for g in segs_out(l):
                    t0, tn = SEG[g]
                    task = ("o", l, g)
                    full(act, task)
                    drain(act.copy(OHG[:, :, t0:t0 + tn],
                                   gbank(task)[:, :].rearrange("p (h t) -> p h t", h=HEADS)[:, :, 0:tn]), task)
                o0 = 0 if l == 0 else META
                act.wait_ge(av_drained, av0 + len(units) // HEADS)
                act.activation(LF[:, :, o0:T], ODA[:, :, o0:T], ACT.Square).then_inc(mix_sq, 1)
                drained(act, ("o", l, 2))
                act.activation(DQ[:, :, o0:T], OHG[:, :, o0:T], ACT.Square).then_inc(mix_sq, 1)
                for c in (4, 5, 6, 7, 0, 1, 2, 3):
                    task = ("ms", l, c)
                    dst = LF if c >= 4 else DQ
                    full(act, task)
                    drain(act.activation(dst[:, c % 4, o0:T], gbank(task)[:, o0:T], ACT.Ln, scale=1.0 / P,
                                         bias=eps_t[:, 0:1]), task)
                    if c % 4 == 3:
                        drained(act, task)
                        act.activation(dst[:, :, o0:T], dst[:, :, o0:T], ACT.Exp, scale=-0.5).then_inc(mix_rstd, 1)
                units0 += len(units)
                av0 += len(units) // HEADS
                for h in (4, 5, 6, 7, 0, 1, 2, 3):
                    act.wait_ge(mix_float, 8 * l + (h + 4) % 8 + 1)
                    act.copy(XH[:, h, o0:T], (ODA if h >= 4 else OHG)[:, h % 4, o0:T]).then_inc(mh_ready, 1)
                if l == 0:
                    for c in range(DC):
                        split_hi(act, UNIT_OF[("wo", c)] + AHEAD)
                        drained(act, ("wo", c))
                        act.activation(SQ[:, c, :], hT[:, c, :], ACT.Square).then_inc(sq_ready, 1)
                    inverse_root(1)
                    halves(1)

                    def act_high(f):
                        drained(act, ("u", f))
                        act.copy(act_hi[:, f, :], ACTF[:, f % 2, :]).then_inc(ah_ready, 1)

                    for i in range(0, FC, JC):
                        n = min(JC, FC - i)
                        for f in range(i, i + n):
                            split_hi(act, UNIT_OF[("g", f)] + AHEAD)
                            task = ("g", f)
                            full(act, task)
                            drain(act.activation(SGF[:, f % JC, :], gbank(task)[:, 0:T], ACT.Silu), task)
                        for f in range(i, i + n):
                            split_hi(act, UNIT_OF[("u", f)] + AHEAD)
                            act_high(f)
                    act.preload_act_table_set("natural_log_exp_and_others")
                    for u in range(FC):
                        split_hi(act, UNIT_OF[("u", FC - 1)] + 1 + u + AHEAD)
                    for c in range(DC):
                        act.wait_ge(down_drained, c + 1)
                        act.activation(SQ[:, c, :], hT[:, c, :], ACT.Square).then_inc(sq_ready, 1)
            act.wait_ge(mix_ready, 16)
            for t in (0, 1):
                for g in (0, 1):
                    task = ("hTt", t, g)
                    full(act, task)
                    drain(act.copy(HTOK[:, t, g * 512:(g + 1) * 512], gbank(task)[:, :]), task)
            for u in range(DC):
                split_hi(act, UNIT_OF[("wo1", 1, 1)] - DC + 1 + u + AHEAD)
            for t in (0, 1):
                drained(act, ("wo1", 0, t))
                drained(act, ("wo1", 1, t))
                act.activation(JUNK[:, :], HTOK[:, t, :], ACT.Square, accum_out=RSUM[:, t:t + 1]).then_inc(tok_sum, 1)
                act.wait_ge(tok_sum, t + 1)
                link(act.activation(RSUM[:, t:t + 1], RSUM[:, t:t + 1], ACT.Ln, scale=1.0 / D, bias=eps_t[:, 0:1]))
                act.activation(RSUM[:, t:t + 1], RSUM[:, t:t + 1], ACT.Exp, scale=-0.5).then_inc(tok_rstd, 1)
            for t in (0, 1):
                for g in (0, 1):
                    task = ("rT", t, g)
                    full(act, task)
                    drain(act.copy(UTR[:, 4 * g:4 * g + 4, t * P:(t + 1) * P],
                                   gbank(task)[:, :].rearrange("p (c t) -> p c t", c=4)), task)
            act.wait_ge(top_ready, 2)
            act.activation(GATE2[:, :, 1], GATE2[:, :, 1], ACT.Exp).then_inc(gate_exp, 1)

            def gather_high(b, n):
                act.wait_ge(G_full[b], n)
                act.copy(xg_hi[:, 4 * b:4 * b + 4, :], banks[b][:, :].rearrange("p (c s) -> p c s", c=4)
                         ).then_inc(xg_hi_ready, 1)

            for b in (0, 1):
                gather_high(b, 1)

            def high_unit(n, m):
                half = m // 2
                if m % 2 == 0:
                    act.wait_ge(half_full[half % HRING],
                                n * (16 * BLOCK_HALVES // HRING) + 16 * (half // HRING + 1))
                if m >= NW:
                    expert_unit_used(act, n, m - NW)
                elif type(n) is not int or n > 0:
                    expert_unit_used(act, n - 1, BLOCK_UNITS + m - NW)
                else:
                    unit_used(act, len(UNITS) + m - NW)
                src = half_slot(half)[:, (m % 2) * UNIT:(m % 2 + 1) * UNIT]
                act.copy(WH[:, (len(UNITS) + m) % NW, :], src).then_inc(hi_ready, 1)

            def expert_block(n):
                def high(m):
                    if m < BLOCK_UNITS:
                        high_unit(n, m)
                    else:
                        high_unit(n + 1, m - BLOCK_UNITS)

                def turn(s):
                    act.wait_ge(heT_full, n * NS + s + 1)
                    if s >= 2:
                        act.wait_ge(down_done, n * NS + s)
                    act.copy(het_hi[:, s % 2, :], banks[4][:, :]).then_inc(het_hi_ready, 1)

                m = 0
                for kind, s in EXPERT:
                    for u in range(4):
                        high(m + AHEAD)
                        if kind == "w3" and u == 0 and s > 0:
                            turn(s - 1)
                        if (kind, s) == ("w2", NS - 1) and u == 0:
                            act.wait_ge(y_half_full, n + 1)
                            act.copy(YS[:, 0:512], banks[5][:, :]).then_inc(y_ready[0], 1)
                        m += 1
                    if kind == "w1":
                        b = s % 2
                        act.wait_ge(G_full[b], n * G_USES[b] + s // 2 + 2)
                        if s >= 2:
                            act.wait_ge(he_ready, n * NS + s - 1)
                        act.activation(SGE[:, b, :], banks[b][:, :], ACT.Silu).then_inc(G_free[b], 1)
                        if s == 0:
                            act.wait_ge(pT_full, n + 1)
                            act.copy(PT, banks[7][:, 0:2 * P].rearrange("p (t s) -> p t s", t=2)).then_inc(pT_ready, 1)
                    if (kind, s) == ("w2", NS - 2):
                        turn(NS - 1)
                        for b in (0, 1):
                            gather_high(b, n * G_USES[b] + G_USES[b] + 1)

            for m in range(AHEAD):
                high_unit(0, m)
            act.preload_act_table(ACT.Silu)
            with act.Fori(0, NE) as e:
                expert_block(e)
            act.wait_ge(regs_ready, 1)
            over = act.value_load(regs[0:1, 0:1], min_val=0, max_val=OVER)
            for j in range(OVER):
                with act.If(over > j):
                    expert_block(NE + j)
            act.preload_act_table_set("natural_log_exp_and_others")
            act.wait_ge(tok_sum, 3)
            for t in (0, 1):
                link(act.activation(JUNK[:, :], HTOK[:, t, :], ACT.Square, accum_out=RSUM[:, 2 + t:3 + t]))
            link(act.activation(RSUM[:, 2:4], RSUM[:, 2:4], ACT.Ln, scale=1.0 / D, bias=eps_t[:, 0:1]))
            act.activation(RSUM[:, 2:4], RSUM[:, 2:4], ACT.Exp, scale=-0.5).then_inc(tok_rstd, 1)

        @block.vector
        def _(dve):
            link = chain(dve, dve_step)
            dve.memset(ones[:, :], 1.0)
            dve.wait_ge(consts_in, 32)
            dve.tensor_copy(masks[:, :, :], MASKF)
            dve.memset(eps_t[:, :], EPS)
            dve.memset(ONE8, 1.0)
            dve.memset(lbt[:, 0, :], 0.0)
            dve.memset(omlb[:, 0, :], 1.0)
            dve.memset(REL[32:33, :], NEG).then_inc(init_done, 1)
            dve.wait_ge(lam_in, 16)
            lv = LAMIN.rearrange("p (k two d) -> p k two d", two=2, d=64)
            link(dve.tensor_tensor(LAMP.rearrange("p (k d) -> p k d", d=64), lv[:, :, 0, :], lv[:, :, 1, :], ALU.mult))
            dve.tensor_reduce(lamt[:, 0:4], LAMP.rearrange("p (k d) -> p k d", d=64), AX.X, ALU.add).then_inc(lam_ready, 1)
            full(dve, ("vec",))
            drain(dve.tensor_copy(vecT[:, 0:44], gbank(("vec",))[:, 0:44]), ("vec",))
            drained(dve, ("vec",))
            dve.wait_ge(lam_ready, 2)
            link(dve.tensor_tensor(lbt[:, 1, :], vecT[:, 32:36], vecT[:, 36:40], ALU.subtract))
            dve.tensor_scalar(lbt[:, 1, :], lbt[:, 1, :], -FLOOR, None, ALU.min).then_inc(lam_ready, 1)
            for l in (0, 1):
                e = lamt[:, 4 + 2 * l:6 + 2 * l]
                link(dve.tensor_tensor(lamt[:, 8 + l:9 + l], e[:, 1:2], e[:, 0:1], ALU.subtract))
                link(dve.tensor_scalar(lamt[:, 8 + l:9 + l], lamt[:, 8 + l:9 + l], -lam_init(l), None, ALU.add))
                link(dve.tensor_scalar(subw[:, l:l + 1], vecT[:, 42 + l:43 + l], 1.0 - lam_init(l), None, ALU.mult))
            dve.wait_ge(lam_ready, 4)
            link(dve.tensor_scalar(lbt[:, 1, :], lbt[:, 1, :], 1.0, None, ALU.add))
            link(dve.reciprocal(lbt[:, 1, :], lbt[:, 1, :]))
            link(dve.tensor_scalar(lbt[:, 1, :], lbt[:, 1, :], 0.0, LB_MAX, ALU.max, ALU.min))
            dve.tensor_scalar(omlb[:, 1, :], lbt[:, 1, :], -1.0, 1.0, ALU.mult, ALU.add).then_inc(init_done, 1)
            for c in range(DC):
                task = ("xT", c)
                full(dve, task)
                drain(dve.tensor_copy(hT[:, c, :], gbank(task)[:, 0:T]), task)

            def normed(k, col):
                dve.wait_ge(rstd_ready, k + 1)
                for c in range(DC):
                    dve.scalar_tensor_tensor(UF[:, c, :], hT[:, c, :], vecT[:, col + c:col + c + 1], rstd,
                                             ALU.mult, ALU.mult).then_inc(uf_ready, 1)
                for c in range(DC):
                    dve.wait_ge(xh_ready, DC * k + c + 1)
                    dve.tensor_tensor(XL[:, c, :], UF[:, c, :], XH[:, c, :].bitcast(F32),
                                      ALU.subtract).then_inc(u_ready, 1)

            def softmax_in(l, i):
                q, h = attention_units(l)[i]
                qn = SEG[q][1]
                kn = SEG[q][0] + qn
                b = i % 2
                n = units0 + i
                dve.wait_ge(score_full, n + 1)
                if n >= 2:
                    dve.wait_ge(a_ready, n - 1)
                if n == 0:
                    dve.wait_ge(bias_in, 16)
                b0 = SEG[2][0] - SEG[q][0]
                for c in (0, 1):
                    ins = dve.scalar_tensor_tensor(S2[b][0:qn, c, 0:kn], banks[3 + c][0:qn, 0:kn], 0.125,
                                                   bias[0:qn, h, b0:b0 + kn], ALU.mult, ALU.add)
                link(ins)
                link(dve.tensor_reduce(stat[0:qn, 4 * b:4 * b + 2], S2[b][0:qn, :, 0:kn], AX.X, ALU.max))
                dve.tensor_scalar(stat[0:qn, 4 * b:4 * b + 2], stat[0:qn, 4 * b:4 * b + 2], -1.0, None,
                                  ALU.mult).then_inc(biased, 1)

            def softmax_out(l, i):
                q, h = attention_units(l)[i]
                qn = SEG[q][1]
                kn = SEG[q][0] + qn
                b = i % 2
                n = units0 + i
                r = stat[0:qn, 8 + 4 * b:10 + 4 * b]
                dve.wait_ge(exp_done, n + 1)
                link(dve.reciprocal(r, r))
                link(dve.tensor_tensor(r[:, 1:2], r[:, 1:2], lamt[0:qn, 8 + l:9 + l], ALU.mult))
                if i >= 2:
                    dve.wait_ge(aT_full, n - 1)
                link(dve.tensor_scalar(AA[b][0:qn, 0:kn], S2[b][0:qn, 1, 0:kn], r[:, 1:2], None, ALU.mult))
                dve.scalar_tensor_tensor(AA[b][0:qn, 0:kn], S2[b][0:qn, 0, 0:kn], r[:, 0:1], AA[b][0:qn, 0:kn],
                                         ALU.mult, ALU.add).then_inc(a_ready, 1)

            units0 = 0
            lv0 = 0
            for l in (0, 1):
                if l == 0:
                    for n in range(AHEAD):
                        split_lo(dve, n)
                normed(2 * l, 8 * l)
                units = attention_units(l)
                for s in ORDER1:
                    for j in range(JC):
                        split_lo(dve, UNIT_OF[("proj", l, s, j)] + AHEAD)
                for i in range(16):
                    split_lo(dve, UNIT_OF[("proj", l, ORDER2[i // 4], i % 4)] + AHEAD)
                    if i < 4:
                        task = ("proj", l, "hf", i)
                        full(dve, task)
                        drain(dve.tensor_scalar(EF[:, i, :], gbank(task)[:, 0:T], FLOOR, None, ALU.max), task)
                    if i < len(units):
                        softmax_in(l, i)
                    if 0 <= i - 1 < len(units):
                        softmax_out(l, i - 1)
                    if i == 7:
                        dve.wait_ge(f_sig, l + 1)
                        for h in range(HEADS):
                            ins = dve.scalar_tensor_tensor(K[:, h, :], EF[:, h, :], omlb[:, l, h:h + 1], SG[:, h, :],
                                                           ALU.mult, ALU.mult)
                        ins.then_inc(k_ready, 1)
                    if i == 10:
                        dve.wait_ge(f_log, l + 1)
                        for h in range(HEADS):
                            for t0, tn in SEG:
                                ins = dve.tensor_tensor_scan(B[:, h, t0:t0 + tn], ones[:, 0:tn], LF[:, h, t0:t0 + tn],
                                                             0.0, ALU.mult, ALU.add)
                        ins.then_inc(b_ready, 1)
                levels = level_tasks(l)
                dve.wait_ge(qg_ready, 2 * l + 1)
                dve.wait_ge(st_zero, l + 1)

                def decayed_q(v):
                    m = LEVELS[v]
                    dve.wait_ge(decay_ready, 7 * l + v)
                    if v > 2:
                        dve.wait_ge(lv_full, lv0 + sum(1 for a, _ in levels if a <= v - 2))
                    dve.tensor_tensor(level_part(X[v % 2], m, 1), level_part(Q, m, 1), level_part(DD[v % 2], m, 1),
                                      ALU.mult).then_inc(xq_ready, 1)

                for v in range(len(LEVELS)):
                    if v + 1 < len(LEVELS):
                        decayed_q(v + 1)
                    for i, (a, g) in enumerate(levels):
                        if a != v:
                            continue
                        tn = SEG[g][1]
                        n = lv0 + i
                        dve.wait_ge(lv_full, n + 1)
                        if n > 0:
                            dve.wait_ge(lv_drained, n)
                        m = masks[0:tn, v, 0:tn].unsqueeze(1).to_broadcast([tn, HEADS, tn])
                        dve.copy_predicated(ST[g][0:tn, :, :], m,
                                            banks[6 + n % 2][0:tn, :].rearrange("p (h t) -> p h t", h=HEADS)[:, :, 0:tn]
                                            ).then_inc(lv_drained, 1)
                for g in (0, 1):
                    task = ("state", l, g)
                    full(dve, task)
                    if g == 0:
                        drain(dve.tensor_copy(STATE[0].rearrange("p h v -> p (h v)"), gbank(task)[:, :]), task)
                        drained(dve, task)
                        dve.wait_ge(expb, 2 * l + 2)
                    else:
                        for h in range(HEADS):
                            ins = dve.scalar_tensor_tensor(STATE[1][:, h, :], STATE[0][:, h, :], bend[:, h:h + 1],
                                                           gbank(task)[:, h * P:(h + 1) * P], ALU.mult, ALU.add)
                        drain(ins, task)
                o0 = 0 if l == 0 else META
                full(dve, ("o", l, 2))
                dve.wait_ge(mix_rstd, 2 * l + 1)
                for h in range(HEADS):
                    dve.scalar_tensor_tensor(ODA[:, h, o0:T], ODA[:, h, o0:T], subw[:, l:l + 1], LF[:, h, o0:T],
                                             ALU.mult, ALU.mult).then_inc(mix_float, 1)
                dve.wait_ge(mix_rstd, 2 * l + 2)
                dve.wait_ge(qg_ready, 2 * l + 2)
                for h in range(HEADS):
                    link(dve.scalar_tensor_tensor(OHG[:, h, o0:T], OHG[:, h, o0:T], vecT[:, 40 + l:41 + l],
                                                  DQ[:, h, o0:T], ALU.mult, ALU.mult))
                    dve.tensor_tensor(OHG[:, h, o0:T], OHG[:, h, o0:T], G[:, h, o0:T], ALU.mult).then_inc(mix_float, 1)
                for h in (4, 5, 6, 7, 0, 1, 2, 3):
                    dve.wait_ge(mh_ready, 8 * l + (h + 4) % 8 + 1)
                    dve.tensor_tensor(XL[:, h, o0:T], (ODA if h >= 4 else OHG)[:, h % 4, o0:T],
                                      XH[:, h, o0:T].bitcast(F32), ALU.subtract).then_inc(mix_ready, 1)
                units0 += len(units)
                lv0 += len(levels)
                if l == 0:
                    for d in range(DC):
                        task = ("wo", d)
                        split_lo(dve, UNIT_OF[task] + AHEAD)
                        full(dve, task)
                        drain(dve.tensor_tensor(hT[:, d, :], hT[:, d, :], gbank(task)[:, 0:T], ALU.add), task)
                    drained(dve, ("wo", DC - 1))
                    normed(1, 16)

                    def act_low(f):
                        dve.wait_ge(ah_ready, f + 1)
                        dve.tensor_tensor(act_lo[:, f, :], ACTF[:, f % 2, :], act_hi[:, f, :].bitcast(F32),
                                          ALU.subtract).then_inc(al_ready, 1)

                    for i in range(0, FC, JC):
                        n = min(JC, FC - i)
                        for f in range(i, i + n):
                            split_lo(dve, UNIT_OF[("g", f)] + AHEAD)
                        for f in range(i, i + n):
                            task = ("u", f)
                            split_lo(dve, UNIT_OF[task] + AHEAD)
                            full(dve, task)
                            drained(dve, ("g", f))
                            if f >= 2:
                                dve.wait_ge(al_ready, f - 1)
                            drain(dve.tensor_tensor(ACTF[:, f % 2, :], SGF[:, f % JC, :], gbank(task)[:, 0:T],
                                                    ALU.mult), task)
                            act_low(f)
                    for half in (0, 1):
                        for u in range(FC // 2):
                            split_lo(dve, UNIT_OF[("u", FC - 1)] + 1 + half * (FC // 2) + u + AHEAD)
                        for d in range(4):
                            dve.wait_ge(down_full, 4 * half + d + 1)
                            h = hT[:, 4 * half + d, :]
                            dve.tensor_tensor(h, h, banks[(3 + 4 * half + d) % 8][:, 0:T], ALU.add
                                              ).then_inc(down_drained, 1)
                    dve.wait_ge(down_drained, 8)
            for half in (0, 1):
                for u in range(DC // 2):
                    split_lo(dve, UNIT_OF[("wo1", 1, 1)] - (2 - half) * (DC // 2) + 1 + u + AHEAD)
                for t in (0, 1):
                    task = ("wo1", half, t)
                    full(dve, task)
                    drained(dve, ("hTt", t, half))
                    h = HTOK[:, t, half * 512:(half + 1) * 512]
                    drain(dve.tensor_tensor(h, h, gbank(task)[:, :], ALU.add), task)
            drained(dve, ("wo1", 1, 1))
            dve.wait_ge(tables_in, 16 * 4)
            for t in (0, 1):
                dve.wait_ge(tok_rstd, t + 1)
                dve.scalar_tensor_tensor(UTOK[:, t, :], HTOK[:, t, :], RSUM[:, t:t + 1], NFW[:, :], ALU.mult,
                                         ALU.mult).then_inc(utok_ready, 1)
            for t in (0, 1):
                task = ("logit", t)
                full(dve, task)
                drain(dve.tensor_copy(LG[:, t, :], gbank(task)[:, 0:NE]), task)
                drained(dve, task)
                link(dve.max(MX[:, t, :], LG[:, t, :]))
                link(dve.max_index(rti[:, 8 * t:8 * t + 8], MX[:, t, :], LG[:, t, :]))
                link(dve.tensor_copy(IDXF[:, t, :], rti[:, 8 * t:8 * t + 2]))
                for k in (0, 1):
                    link(dve.tensor_scalar(OH[:, t, k, :], IOTA[:, 0:NE], IDXF[:, t, k:k + 1], None, ALU.is_equal))
                dve.tensor_tensor(MASK[:, t, :], OH[:, t, 0, :], OH[:, t, 1, :], ALU.add).then_inc(mask_ready, 1)
                dve.tensor_tensor(GATE2[:, t, 1:2], MX[:, t, 1:2], MX[:, t, 0:1], ALU.subtract).then_inc(top_ready, 1)
            dve.wait_ge(mask_ready, 2)
            dve.wait_ge(gate_exp, 1)
            link(dve.tensor_scalar(GATE2[:, :, 0], GATE2[:, :, 1], 1.0, None, ALU.add))
            link(dve.reciprocal(GATE2[:, :, 0], GATE2[:, :, 0]))
            link(dve.tensor_tensor(GATE2[:, :, 1], GATE2[:, :, 1], GATE2[:, :, 0], ALU.mult))
            link(dve.memset(rt[:, 88:136], 0.0))
            for t in (0, 1):
                link(dve.tensor_scalar(TMP8[:, t, :], OH[:, t, 0, :], GATE2[:, t, 0:1], None, ALU.mult))
                link(dve.scalar_tensor_tensor(GX[:, t, 0:NE], OH[:, t, 1, :], GATE2[:, t, 1:2], TMP8[:, t, :],
                                              ALU.mult, ALU.add))
                task = ("rank", t)
                full(dve, task)
                link(dve.tensor_scalar(TMP8[:, t, :], gbank(task)[:, 0:NE], 1.0, None, ALU.add))
                drain(dve.tensor_tensor(TMP8[:, t, :], TMP8[:, t, :], MASK[:, t, :], ALU.mult), task)
                drained(dve, task)
                link(dve.tensor_scalar(RM[:, t, 0:NE], TMP8[:, t, :], -1.0, None, ALU.add))
            full(dve, ("cnt",))
            drain(dve.tensor_scalar(OV, gbank(("cnt",))[:, 0:NE], float(P), None, ALU.is_gt), ("cnt",))
            drained(dve, ("cnt",))
            link(dve.tensor_tensor_scan(CUM, ONE8, OV, 0.0, ALU.mult, ALU.add))
            link(dve.tensor_copy(EID[:, 0:1], CUM[:, 7:8]))
            for j in range(OVER):
                link(dve.tensor_scalar(SEL, CUM, float(j + 1), None, ALU.is_equal))
                link(dve.tensor_tensor(SEL, SEL, OV, ALU.mult))
                link(dve.tensor_tensor(TMPG, SEL, IOTA[:, 0:NE], ALU.mult))
                link(dve.tensor_reduce(EID[:, 1 + j:2 + j], TMPG, AX.X, ALU.add))
                for t in (0, 1):
                    link(dve.tensor_scalar(TMP8[:, t, :], RM[:, t, 0:NE], -float(P), None, ALU.add))
                    link(dve.tensor_tensor(TMP8[:, t, :], TMP8[:, t, :], SEL, ALU.mult))
                    link(dve.tensor_reduce(RM[:, t, NE + j:NE + j + 1], TMP8[:, t, :], AX.X, ALU.add))
                    link(dve.tensor_tensor(TMP8[:, t, :], GX[:, t, 0:NE], SEL, ALU.mult))
                    link(dve.tensor_reduce(GX[:, t, NE + j:NE + j + 1], TMP8[:, t, :], AX.X, ALU.add))
            dve.tensor_copy(regs[:, 0:4], EID).then_inc(regs_ready, 1)

            def low_unit(n, m):
                dve.wait_ge(hi_ready, len(UNITS) + n * BLOCK_UNITS + m + 1)
                i = (len(UNITS) + m) % NW
                src = half_slot(m // 2)[:, (m % 2) * UNIT:(m % 2 + 1) * UNIT]
                dve.tensor_tensor(WL[:, i, :], src, WH[:, i, :].bitcast(F32), ALU.subtract).then_inc(lo_ready, 1)

            def gather_low(b, n):
                dve.wait_ge(xg_hi_ready, 2 * n + b + 1)
                dve.tensor_tensor(xg_lo[:, 4 * b:4 * b + 4, :], banks[b][:, :].rearrange("p (c s) -> p c s", c=4),
                                  xg_hi[:, 4 * b:4 * b + 4, :].bitcast(F32), ALU.subtract).then_inc(G_free[b], 1)

            def onehot(n, step):
                dve.tensor_copy(TMPG[:, 0:2], RM[:, :, n]).then_inc(col_ready, 1)
                dve.wait_ge(col_ready, step)
                for t in (0, 1):
                    ins = dve.tensor_scalar(PH[:, t, :], IOTA, TMPG[:, t:t + 1], None, ALU.is_equal)
                ins.then_inc(p_ready, 1)

            dve.wait_ge(regs_ready, 1)
            for b in (0, 1):
                dve.memset(TMPG[:, 6 + b:7 + b], 0.0).then_inc(scatter_added[b], 1)
            dve.memset(TMPG[:, 3:4], 0.0).then_inc(down_done, 1)
            onehot(0, 1)
            for b in (0, 1):
                gather_low(b, 0)

            def expert_block(n):
                dve.wait_ge(p_ready, n + 1)
                dve.tensor_copy(TMPG[:, 4:6], GX[:, :, n]).then_inc(col_ready, 1)
                dve.wait_ge(col_ready, 2 * n + 2)
                for t in (0, 1):
                    ins = dve.tensor_scalar(PG[:, t, :], PH[:, t, :], TMPG[:, 4 + t:5 + t], None, ALU.mult)
                ins.then_inc(pg_ready, 1)
                dve.wait_ge(pg_ready, n + 1)
                dve.wait_ge(G_full[1], n * G_USES[1] + 1)
                onehot(n + 1, 2 * n + 3)

                def low(m):
                    low_unit(n, m)

                def turn(s):
                    dve.wait_ge(het_hi_ready, n * NS + s + 1)
                    dve.tensor_tensor(het_lo[:, s % 2, :], banks[4][:, :], het_hi[:, s % 2, :].bitcast(F32),
                                      ALU.subtract).then_inc(heT_ready, 1)

                def product(s):
                    b = s % 2
                    dve.wait_ge(U_full[b], n * U_USES[b] + s // 2 + 1)
                    dve.wait_ge(G_free[b], n * G_USES[b] + s // 2 + 2)
                    if s >= 2:
                        dve.wait_ge(heT_full, n * NS + s - 1)
                    dve.tensor_tensor(HE[:, b, :], SGE[:, b, :], banks[2 + b][:, :], ALU.mult).then_inc(he_ready, 1)

                m = 0
                for kind, s in EXPERT:
                    for u in range(4):
                        low(m + AHEAD)
                        if kind == "w3" and u == 0 and s > 0:
                            turn(s - 1)
                        m += 1
                    if kind == "w3":
                        product(s)
                    if (kind, s) == ("w2", NS - 2):
                        turn(NS - 1)
                        for b in (0, 1):
                            gather_low(b, n + 1)
                dve.wait_ge(down_done, n * NS + NS + 1)
                dve.tensor_copy(YS[:, 512:1024], banks[6][:, :]).then_inc(y_ready[1], 1)
                for half in (0, 1):
                    for t in (0, 1):
                        dve.wait_ge(U_full[t], n * U_USES[t] + (5 if t == 0 else 4) + half)
                        h = HTOK[:, t, half * 512:(half + 1) * 512]
                        dve.tensor_tensor(h, h, banks[2 + t][:, :], ALU.add
                                          ).then_inc(scatter_added[t], 1)

            for m in range(AHEAD):
                low_unit(0, m)
            with dve.Fori(0, NE) as e:
                expert_block(e)
            over = dve.value_load(regs[0:1, 0:1], min_val=0, max_val=OVER)
            for j in range(OVER):
                with dve.If(over > j):
                    expert_block(NE + j)
            dve.wait_ge(fnw_in, 16)
            dve.memset(stat[:, 0:1], 0.0).then_inc(tok_sum, 1)
            dve.wait_ge(tok_rstd, 3)
            for t in (0, 1):
                ins = dve.scalar_tensor_tensor(OUTT[:, t, :], HTOK[:, t, :], RSUM[:, 2 + t:3 + t], FNW[:, :], ALU.mult, ALU.mult)
            ins.then_inc(out_ready, 1)

        @block.gpsimd
        def _(pool):
            link = chain(pool, pool_step)
            pool.wait_ge(init_done, 2)
            for l in (0, 1):
                pool.wait_ge(f_sig, l + 1)
                for h in range(HEADS):
                    ins = pool.tensor_scalar(LF[:, h, :], SG[:, h, :], omlb[:, l, h:h + 1], lbt[:, l, h:h + 1],
                                             ALU.mult, ALU.add)
                ins.then_inc(f_gate, 1)
                full(pool, ("vt", l, "dv", 2))
                drained(pool, ("proj", l, "hq", JC - 1))
                pool.tensor_scalar(TMP, Q, 3e38, FLOOR, ALU.min, ALU.max).then_inc(t_clamped, 1)
                pool.wait_ge(t_sig, 2 * l + 1)
                pool.tensor_tensor(Q, Q, TMP, ALU.mult).then_inc(qg_ready, 1)
                pool.wait_ge(b_ready, l + 1)
                pool.wait_ge(k_ready, l + 1)
                for t0, tn in SEG[0:2]:
                    end = B[:, :, t0 + tn - 1:t0 + tn].to_broadcast([P, HEADS, tn])
                    ins = pool.tensor_tensor(KEND[:, :, t0:t0 + tn], end, B[:, :, t0:t0 + tn], ALU.subtract)
                ins.then_inc(kdiff, 1)
                drained(pool, ("proj", l, "hg", JC - 1))
                pool.wait_ge(qg_ready, 2 * l + 1)
                pool.tensor_scalar(TMP, G, 3e38, FLOOR, ALU.min, ALU.max).then_inc(t_clamped, 1)
                pool.wait_ge(expb, 2 * l + 1)
                pool.tensor_tensor(QB[:, :, META:T], Q[:, :, META:T], SG[:, :, META:T], ALU.mult).then_inc(qb_ready, 1)
                pool.wait_ge(kexp, l + 1)
                pool.tensor_tensor(KEND[:, :, 0:SEG[2][0]], K[:, :, 0:SEG[2][0]], KEND[:, :, 0:SEG[2][0]],
                                   ALU.mult).then_inc(kend_ready, 1)
                pool.wait_ge(t_sig, 2 * l + 2)
                pool.tensor_tensor(G, G, TMP, ALU.mult).then_inc(qg_ready, 1)
                full(pool, ("proj", l, "hv", JC - 1))
                pool.memset(scores[:, 0:2 * HW + 64], 0.0).then_inc(st_zero, 1)
                full(pool, ("vt", l, "hv", 2))
                pool.wait_ge(qg_ready, 2 * l + 2)

                def difference(v):
                    m = LEVELS[v]
                    if v > 2:
                        pool.wait_ge(xq_ready, 7 * l + v - 2)
                    for half in (0, 1):
                        src = level_part(B, m, half)
                        ref = level_part(B, m, 0)
                        ref = ref[:, :, m - 1:m] if m <= 8 else ref[:, :, :, m - 1:m]
                        ins = pool.tensor_tensor(level_part(DD[v % 2], m, half), src,
                                                 ref.to_broadcast(list(src.shape)), ALU.subtract)
                    ins.then_inc(diff_ready, 1)

                difference(1)
                for v in range(1, len(LEVELS)):
                    if v + 1 < len(LEVELS):
                        if v + 1 > 2:
                            pool.wait_ge(xk_ready, 7 * l + v - 1)
                        difference(v + 1)
                    m = LEVELS[v]
                    pool.wait_ge(decay_ready, 7 * l + v)
                    if v > 2:
                        levels = level_tasks(l)
                        pool.wait_ge(lv_full, (0 if l == 0 else len(level_tasks(0)))
                                     + sum(1 for a, _ in levels if a <= v - 2))
                    pool.tensor_tensor(level_part(X[v % 2], m, 0), level_part(K, m, 0), level_part(DD[v % 2], m, 0),
                                       ALU.mult).then_inc(xk_ready, 1)
            pool.wait_ge(mix_ready, 16)
            pool.dma_start(NFW[:, :], A["norm_ffn"][1].partition_broadcast(P)).then_inc(tables_in, 16)
            pool.dma_start(IOTA, A["iota"]).then_inc(tables_in, 16)
            pool.dma_start(UPPER, A["upper"]).then_inc(tables_in, 16)
            pool.dma_start(ROUT, A["moe_router"][0].rearrange("(c p) e -> p c e", p=P)).then_inc(tables_in, 16)
            pool.wait_ge(tables_in, 16 * 4)
            pool.wait_ge(utok_ready, 2)
            pool.dma_start(FNW[:, :], A["final_norm"].partition_broadcast(P)).then_inc(fnw_in, 16)
            pool.wait_ge(fnw_in, 16)


_INS = ['x', 'meta', 'rel_bias', 'norm_mix', 'w_in', 'hg_lb_logits', 'hg_norm_w', 'da_lambda', 'da_subln_w',
        'w_out', 'norm_ffn', 'dense_w1', 'dense_w3', 'dense_w2', 'moe_router', 'moe_w1', 'moe_w3', 'moe_w2',
        'final_norm']


def constants():
    dist = T - 1 - np.arange(RELW)
    exact = BUCKETS // 2
    n = np.maximum(dist, 0)
    nf = np.maximum(n, exact).astype(np.float32)
    large = exact + (np.log(nf / np.float32(exact)) / np.float32(math.log(MAXD / exact))
                     * np.float32(BUCKETS - exact)).astype(np.int32)
    bucket = np.where(n < exact, n, np.minimum(large, BUCKETS - 1))
    buckets = np.zeros((BUCKETS + 1, RELW), np.float32)
    for j in range(RELW):
        buckets[bucket[j] if dist[j] >= 0 else BUCKETS, j] = 1.0
    s = np.arange(P)[:, None]
    t = np.arange(P)[None, :]
    masks = np.zeros((P, len(LEVELS), P), np.float32)
    for v, m in enumerate(LEVELS):
        if m == 0:
            masks[:, v, :] = s == t
        else:
            masks[:, v, :] = (s // (2 * m) == t // (2 * m)) & (s % (2 * m) < m) & (t % (2 * m) >= m)
    return {
        "ident": np.eye(P, dtype=np.float32),
        "masks": masks,
        "buckets": buckets,
        "iota": np.broadcast_to(np.arange(P, dtype=np.float32), (P, P)).copy(),
        "upper": (s < t).astype(np.float32),
    }


def kernel(**inputs):
    import numpy as _np
    import concourse.bacc as _bacc
    from concourse import mybir as _mybir
    from concourse.bass_utils import run_bass_kernel_spmd as _run

    nc = _bacc.Bacc("TRN2", target_bir_lowering=False, num_devices=1)
    arrays, aps = {}, {}
    everything = {name: _np.ascontiguousarray(inputs[name]) for name in _INS}
    everything.update(constants())
    for name, a in everything.items():
        arrays[f"in_{name}_dram"] = a
        aps[name] = nc.dram_tensor(f"in_{name}_dram", a.shape, _mybir.dt.from_np(a.dtype), kind="ExternalInput").ap()
    out = nc.dram_tensor("out_0_dram", (1, SEQ, D), F32, kind="ExternalOutput").ap()
    build(nc, aps, out)
    r = _run(nc, [arrays], core_ids=[0])
    return r.results[0]["out_0_dram"]
```

```python
from contextlib import ExitStack
import math

import numpy as np
import concourse.bass as bass
from concourse import mybir

P = 128
D = 1024
DC = D // P
META = 16
SEQ = 256
T = META + SEQ
SEG = [(0, META), (META, P), (META + P, P)]
HEADS = 4
HW = 512
PROJ = {"hq": 0, "hf": 1, "hv": 2, "hg": 3, "dq": 4, "dk": 5, "dv": 6}
ORDER1 = ["dq", "dk", "dv"]
ORDER2 = ["hf", "hq", "hv", "hg"]
MIX_ORDER = (4, 5, 6, 7, 0, 1, 2, 3)
FD = 2816
FC = FD // P
FE = 3584
NE = 8
SL = 512
NS = FE // SL
JC = SL // P
AT_VT = 12
AT_KT = 13
AT_LEVEL = 13
RING = 3
SLOT = 4096
HRING = 14
HSLOT = SLOT // 2
UNIT = 1024
NW = 4
AHEAD = NW - 1
OVER = 3
BUCKETS = 32
MAXD = 128
RELW = 400
EPS = 1e-6
NEG = -1e30
LB_MAX = 0.999
FLOOR = -87.0
LEVEL_BANKS = (3, 4, 5, 7)
LEVELS = [0, 1, 2, 4, 8, 16, 32, 64]
NGB = 3

F32 = mybir.dt.float32
F32R = mybir.dt.float32r
I32 = mybir.dt.int32
U32 = mybir.dt.uint32
U8 = mybir.dt.uint8
ALU = mybir.AluOpType
ACT = mybir.ActivationFunctionType
AX = mybir.AxisListType


def lam_init(layer):
    return 0.8 - 0.6 * math.exp(-0.3 * layer)


def segs_out(layer):
    return [0, 1, 2] if layer == 0 else [1, 2]


def attention_units(layer):
    return [(q, h) for q in reversed(segs_out(layer)) for h in range(HEADS)]


def level_tasks(layer):
    return [(v, s) for v in range(len(LEVELS)) for s in segs_out(layer)
            if LEVELS[v] * 2 <= SEG[s][1]]


def general_tasks():
    order = [("vec",), ("rel",)] + [("xT", c) for c in range(DC)]
    for l in (0, 1):
        order.append(("ssq", 2 * l))
        order += [("proj", l, s, j) for s in ORDER1 for j in range(JC)]
        order += [("vt", l, "dv", g) for g in range(3)]
        for i in range(16):
            order.append(("proj", l, ORDER2[i // 4], i % 4))
            if i == AT_VT:
                order += [("vt", l, "hv", g) for g in range(3)]
            if i == AT_KT:
                order += [("kt", l, g) for g in (0, 1)]
        order += [("state", l, g) for g in (0, 1)]
        order += [("ms", l, c) for c in MIX_ORDER[0:4]]
        if l == 1:
            order += [("hTt", t, g) for t in (0, 1) for g in (0, 1)]
        order += [("o", l, g) for g in segs_out(l)]
        order += [("ms", l, c) for c in MIX_ORDER[4:8]]
        if l == 0:
            order += [("wo", d) for d in range(DC)]
            order.append(("ssq", 1))
            for i in range(0, FC, JC):
                order += [(k, f) for k in ("g", "u") for f in range(i, min(i + JC, FC))]
        else:
            order += [("wo1", half, t) for half in (0, 1) for t in (0, 1)]
            order += [("rT", t, g) for t in (0, 1) for g in (0, 1)]
            order += [("logit",), ("rank",)]
    return order


TURN = {name: i for i, name in enumerate(general_tasks())}


def prefix_slots():
    slots = []
    for l in (0, 1):
        slots += [("w_in", (l, s)) for s in ORDER1 + ORDER2]
        slots += [("w_out", (l, half)) for half in (0, 1)]
        if l == 0:
            slots += [(w, i) for i in range(-(-FC // JC)) for w in ("w1", "w3")]
            slots += [("w2", (half, i)) for half in (0, 1) for i in range(3)]
    return slots


PREFIX = prefix_slots()
SLOT_OF = {key: n for n, key in enumerate(PREFIX)}


def prefix_units():
    units = []
    done = [0]

    def count():
        done[0] += 1
        return ("count", done[0])

    for l in (0, 1):
        for s in ORDER1 + ORDER2:
            units += [(SLOT_OF[("w_in", (l, s))], "cols", j, HW, ("proj", l, s, j)) for j in range(JC)]
        if l == 0:
            units += [(SLOT_OF[("w_out", (0, d // 4))], "cols", d % 4, HW, ("wo", d)) for d in range(DC)]
            for i in range(0, FC, JC):
                n = min(JC, FC - i)
                for k, w in (("g", "w1"), ("u", "w3")):
                    units += [(SLOT_OF[(w, i // JC)], "cols", j, n * P, (k, i + j)) for j in range(n)]
            for half in (0, 1):
                for u in range(FC // 2):
                    units.append((SLOT_OF[("w2", (half, u // 4))], "rows", u % 4, HW,
                                  count() if u < FC // 2 - 1 else ("down", half)))
        else:
            for half in (0, 1):
                for u in range(DC // 2):
                    units.append((SLOT_OF[("w_out", (1, half))], "rows", MIX_ORDER[2 * u] // 2, HW,
                                  count() if u < DC // 2 - 1 else ("wo1", half, 1)))
    return units, done[0]


UNITS, UNITS_COUNTED = prefix_units()
UNIT_OF = {u[4]: n for n, u in enumerate(UNITS)}
LAST_UNIT = {u[0]: n for n, u in enumerate(UNITS)}


def expert_slots():
    order = [("w1", 0), ("w3", 0)]
    for s in range(1, NS):
        order += [("w1", s), ("w3", s), ("w2", s - 1)]
    return order + [("w2", NS - 1)]


EXPERT = expert_slots()
EXPERT_AT = {key: n for n, key in enumerate(EXPERT)}
BLOCK_HALVES = 2 * len(EXPERT)
BLOCK_UNITS = 4 * len(EXPERT)
assert BLOCK_HALVES % HRING == 0 and BLOCK_UNITS % NW == 0
EARLY = AHEAD // 2 + 1
COUNTED = 3 * len(EXPERT)
G_USES = [5, 4]
U_USES = [6, 5]


def build(nc, A, out):
    with ExitStack() as ctx:
        def sb(name, shape, dt=F32):
            return ctx.enter_context(nc.sbuf_tensor(name, shape, dt))

        def sem(name):
            return ctx.enter_context(nc.semaphore(name))

        ident = sb("ident", [P, P])
        ones = sb("ones", [P, P])
        masks = sb("masks", [P, len(LEVELS), P], U8)
        vecT = sb("vecT", [P, 48])
        lbt = sb("lbt", [P, 2, HEADS])
        omlb = sb("omlb", [P, 2, HEADS])
        lamt = sb("lamt", [P, 16])
        subw = sb("subw", [P, 2])
        eps_t = sb("eps_t", [P, 1])
        stat = sb("stat", [P, 16])
        bend = sb("bend", [P, HEADS])
        rt = sb("rt", [P, 216])
        rti = sb("rti", [P, 32], U32)
        regs = sb("regs", [P, 8], I32)
        MAP = 51800
        base = nc.sbuf_base
        sb("plan", [P, MAP])

        def at(name, word, shape, dt=F32):
            assert word + int(np.prod(shape[1:])) <= MAP, name
            return nc.alloc_sbuf_tensor_at(name, shape, dt, offset=base + 4 * word)

        W_TILES = HRING // 2 * HSLOT
        W_SPLIT = HRING * HSLOT
        W_HT = W_SPLIT + 2 * NW * UNIT
        W_X = W_HT + DC * T
        W_VTOK = W_X + 2 * DC * T
        W_BIAS = W_VTOK + 6 * HW
        W_END = W_BIAS + HEADS * T
        ring = at("ring", 0, [P, HRING * HSLOT])
        tiles = at("tiles", W_TILES, [P, 13 * HEADS * T])
        level_x = at("level_operands", W_END + 4 * T + 2 * T + 3 * P, [P, 2, HEADS, T])
        WH = at("w_hi", W_SPLIT, [P, NW, UNIT], F32R)
        WL = at("w_lo", W_SPLIT + NW * UNIT, [P, NW, UNIT], F32R)
        hT = at("hT", W_HT, [P, DC, T])
        XH = at("x_hi", W_X, [P, DC, T], F32R)
        XL = at("x_lo", W_X + DC * T, [P, DC, T], F32R)
        states = at("hgrn_states", W_X, [P, 2 * HW])
        vtok = at("vtok", W_VTOK, [P, 2, 3, HW])
        bias = at("bias", W_BIAS, [P, HEADS, T])
        small = at("small", W_END, [P, 2 * 2 * T + 2 * T + 3 * P])
        act_hi = at("act_hi", W_TILES, [P, FC, T], F32R)
        act_lo = at("act_lo", W_TILES + FC * T, [P, FC, T], F32R)
        xg_hi = at("xg_hi", W_X + DC * T, [P, DC, P], F32R)
        xg_lo = at("xg_lo", W_X + DC * T + D, [P, DC, P], F32R)
        h_tok = at("h_tok", W_VTOK, [P, 2, D])
        HE = at("expert_h", W_VTOK + 2 * D, [P, 2, SL])
        u_tok = at("u_tok", W_X, [P, 2, D])
        norm_w = at("norm_w", W_BIAS, [P, D])
        u_tokT = at("u_tokT", W_HT, [P, DC, 2 * P])
        junk = at("junk", W_HT, [P, D])
        y_sb = at("expert_y", W_HT + D, [P, D])
        SGE = at("expert_silu", W_END, [P, 2, SL])
        het_hi = at("expert_hT_hi", W_END + 2 * SL, [P, 2, SL], F32R)
        het_lo = at("expert_hT_lo", W_END + 4 * SL, [P, 2, SL], F32R)
        tabs = at("expert_tables", W_END + 6 * SL, [P, 8 * P + DC * NE])
        scratch = nc.dram_tensor("bias_rows", [HEADS, P, RELW], F32, kind="Internal")

        def tile(i, n=1):
            return tiles[:, i * HEADS * T:(i + n) * HEADS * T]

        def heads(i):
            return tile(i).rearrange("p (h t) -> p h t", h=HEADS)

        DQ, DK, DV, HV = heads(0), heads(1), heads(2), heads(3)
        EF, SG, Q, G, K, LF, B, ODA = (heads(i) for i in range(4, 12))
        TMP = heads(12)
        X = [level_x[:, i] for i in (0, 1)]
        DD = [DV, LF]
        MS_DA, MS_HG = DQ, EF
        OHG = K
        KEND, QB = EF, SG
        VEC = tile(4)[0:48, 0:P]
        ONEHOT = tile(5)[0:33, 0:RELW]
        REL = tile(6)[0:33, 0:HEADS]
        RELROW = tile(7)[0:HEADS, 0:RELW]
        LAMIN = tile(8)[:, 0:512]
        LAMP = tile(9)[:, 0:256]
        XTOK = tile(10, 2)[:, 0:2 * D].rearrange("p (t d) -> p t d", t=2)
        MTOK = tile(2)[0:META, 0:D]
        MASKF = tile(3)[:, 0:len(LEVELS) * P].rearrange("p (v t) -> p v t", t=P)
        SQ = tile(0, 2).rearrange("p (c t) -> p c t", c=DC)
        UF = tile(2, 2).rearrange("p (c t) -> p c t", c=DC)
        rstd = SQ[:, 0, :]
        S2 = [small[:, i * 2 * T:(i + 1) * 2 * T].rearrange("p (c t) -> p c t", c=2) for i in (0, 1)]
        AA = [small[:, 4 * T + i * T:4 * T + (i + 1) * T] for i in (0, 1)]
        AT = small[:, 6 * T:6 * T + 3 * P].rearrange("p (g q) -> p g q", g=3)
        KTOK = small[:, 0:2 * HW].rearrange("p (g n) -> p g n", g=2)
        ST = [tile(1)[:, 2 * HW:2 * HW + 64].rearrange("p (h t) -> p h t", h=HEADS),
              tile(1)[:, 0:HW].rearrange("p (h t) -> p h t", h=HEADS),
              tile(1)[:, HW:2 * HW].rearrange("p (h t) -> p h t", h=HEADS)]
        STATE = [states[:, i * HW:(i + 1) * HW].rearrange("p (h v) -> p h v", h=HEADS) for i in (0, 1)]
        SGF = tile(11).rearrange("p (b t) -> p b t", b=JC)
        ACTF = small[:, 0:2 * T].rearrange("p (b t) -> p b t", b=2)
        HTOK, UTOK, UTR, NFW, FNW, YS, JUNK, OUTT = h_tok, u_tok, u_tokT, norm_w, norm_w, y_sb, junk, u_tok
        PH, PG, PT = (tabs[:, 2 * i * P:2 * (i + 1) * P].rearrange("p (t s) -> p t s", t=2) for i in range(3))
        IOTA = tabs[:, 6 * P:7 * P]
        UPPER = tabs[:, 7 * P:8 * P]
        ROUT = tabs[:, 8 * P:8 * P + DC * NE].rearrange("p (c e) -> p c e", c=DC)

        def cols(at, n):
            return rt[:, at:at + n]
        LG = cols(0, 16).rearrange("p (t e) -> p t e", t=2)
        MX = cols(16, 16).rearrange("p (t e) -> p t e", t=2)
        IDXF = cols(32, 4).rearrange("p (t k) -> p t k", t=2)
        OH = cols(36, 32).rearrange("p (t k e) -> p t k e", t=2, k=2)
        MASK = cols(68, 16).rearrange("p (t e) -> p t e", t=2)
        GATE2 = cols(84, 4).rearrange("p (t k) -> p t k", t=2)
        RM = cols(88, 24).rearrange("p (t i) -> p t i", t=2)
        GX = cols(112, 24).rearrange("p (t i) -> p t i", t=2)
        OV = cols(144, 8)
        CUM = cols(152, 8)
        TMP8 = cols(168, 16).rearrange("p (t e) -> p t e", t=2)
        EID = cols(184, 4)
        ONE8 = cols(188, 8)
        RSUM = cols(204, 4)
        TMPG = cols(208, 8)
        SEL = y_sb[:, 0:OVER * NE].rearrange("p (j e) -> p j e", j=OVER)
        SELE = y_sb[:, 32:32 + OVER * NE].rearrange("p (j e) -> p j e", j=OVER)
        SELR, SELG = (y_sb[:, a:a + 2 * OVER * NE].rearrange("p (t j e) -> p t j e", t=2, j=OVER) for a in (64, 128))
        OHG2 = y_sb[:, 192:192 + 4 * NE].rearrange("p (t k e) -> p t k e", t=2, k=2)

        banks = [ctx.enter_context(nc.psum_tensor(f"bank{i}", [P, 512], F32)) for i in range(8)]

        g_full = [sem(f"general_full{i}") for i in range(NGB)]
        g_drained = [sem(f"general_drained{i}") for i in range(NGB)]

        def gbank(task):
            return banks[TURN[task] % NGB]

        def full(eng, task):
            i = TURN[task]
            eng.wait_ge(g_full[i % NGB], i // NGB + 1)

        def drained(eng, task):
            i = TURN[task]
            eng.wait_ge(g_drained[i % NGB], i // NGB + 1)

        def drain(ins, task):
            return ins.then_inc(g_drained[TURN[task] % NGB], 1)

        slot_full = [sem(f"slot_full{i}") for i in range(RING)]
        half_full = [sem(f"half_slot_full{i}") for i in range(HRING)]
        hi_ready = sem("weights_hi_ready")
        lo_ready = sem("weights_lo_ready")
        unit_done = sem("unit_done")
        down_full = sem("dense_down_full")
        down_drained = sem("dense_down_drained")
        uf_ready = sem("u_float_ready")
        xh_ready = sem("u_hi_ready")
        mh_ready = sem("mix_hi_ready")
        ah_ready = sem("act_hi_ready")
        al_ready = sem("act_lo_ready")

        def slot(n):
            return ring[:, (n % RING) * SLOT:(n % RING + 1) * SLOT]

        def half_slot(g):
            return ring[:, (g % HRING) * HSLOT:(g % HRING + 1) * HSLOT]

        def unit_used(eng, n):
            end = UNITS[n][4]
            if end[0] == "count":
                eng.wait_ge(unit_done, end[1])
            elif end[0] == "down":
                eng.wait_ge(down_full, 4 * end[1] + 4)
            else:
                full(eng, end)

        def unit_source(n):
            slot_n, kind, i, width, _ = UNITS[n]
            if kind == "cols":
                w = slot(slot_n)[:, 0:DC * width].rearrange("p (c n) -> p c n", c=DC)
                return w[:, :, i * P:(i + 1) * P], DC
            return slot(slot_n)[:, 2 * i * HW:(2 * i + 2) * HW].rearrange("p (c n) -> p c n", c=2), 2

        def split(buffer, n, chunks):
            return buffer[:, n % NW, :].rearrange("p (c n) -> p c n", c=chunks)

        def expert_unit_used(eng, n, m):
            kind, s = EXPERT[m // 4]
            if m % 4 < 3:
                eng.wait_ge(unit_done, UNITS_COUNTED + n * COUNTED + 3 * (m // 4) + m % 4 + 1)
            elif kind == "w1":
                eng.wait_ge(G_full[s % 2], n * G_USES[s % 2] + s // 2 + 2)
            elif kind == "w3":
                eng.wait_ge(U_full[s % 2], n * U_USES[s % 2] + s // 2 + 1)
            else:
                eng.wait_ge(down_done, n * NS + s + 2)

        def scatter_bank(half, t):
            return banks[(2, 4)[half] + t][:, :]

        def split_hi(act, n):
            if n >= len(UNITS):
                return
            src, chunks = unit_source(n)
            act.wait_ge(slot_full[UNITS[n][0] % RING], 16 * (UNITS[n][0] // RING + 1))
            if n >= NW:
                unit_used(act, n - NW)
            act.copy(split(WH, n, chunks), src).then_inc(hi_ready, 1)

        def split_lo(dve, n):
            if n >= len(UNITS):
                return
            src, chunks = unit_source(n)
            dve.wait_ge(hi_ready, n + 1)
            dve.tensor_tensor(split(WL, n, chunks), src, split(WH, n, chunks).bitcast(F32),
                              ALU.subtract).then_inc(lo_ready, 1)

        ident_in = sem("identity_in")
        masks_in = sem("masks_in")
        vec_in = sem("vec_in")
        x_in = sem("x_in")
        rows_out = sem("bias_rows_written")
        bias_in = sem("bias_in")
        lam_in = sem("lambda_in")
        tables_in = sem("expert_tables_in")
        fnw_in = sem("final_norm_in")
        init_done = sem("init_done")
        sq_ready = sem("squares_ready")
        rstd_ready = sem("rstd_ready")
        u_ready = sem("u_ready")
        lam_ready = sem("lambda_ready")
        score_full = sem("attention_scores_full")
        biased = sem("attention_biased")
        exp_done = sem("attention_exp_done")
        a_ready = sem("attention_weights_ready")
        aT_full = sem("attention_weightsT_full")
        aT_drained = sem("attention_weightsT_drained")
        av_full = sem("attention_out_full")
        av_drained = sem("attention_out_drained")
        f_exp = sem("forget_exp_ready")
        f_ln = sem("forget_log1p_ready")
        f_sig = sem("forget_sigmoid_ready")
        f_gate = sem("forget_gate_ready")
        f_log = sem("forget_log_ready")
        k_ready = sem("k_ready")
        b_ready = sem("b_ready")
        t_clamped = sem("silu_clamped")
        t_step = sem("silu_step")
        t_sig = sem("silu_sigmoid_ready")
        qg_ready = sem("silu_ready")
        expb = sem("exp_b_ready")
        qb_ready = sem("qb_ready")
        kdiff = sem("kend_difference_ready")
        kexp = sem("kend_exp_ready")
        kend_ready = sem("kend_ready")
        st_zero = sem("scores_zeroed")
        diff_ready = [sem(f"level_difference_ready{i}") for i in (0, 1)]
        decay_ready = sem("level_decay_ready")
        xq_ready = sem("level_q_ready")
        xk_ready = sem("level_k_ready")
        lv_full = sem("level_scores_full")
        lv_drained = sem("level_scores_drained")
        mix_sq = sem("mix_squares_ready")
        mix_rstd = sem("mix_rstd_ready")
        mix_ready = sem("mix_ready")
        tok_sum = sem("token_sum_ready")
        tok_rstd = sem("token_rstd_ready")
        utok_ready = sem("u_token_ready")
        top_ready = sem("top_values_ready")
        gate_exp = sem("gate_exp_ready")
        mask_ready = sem("mask_ready")
        regs_ready = sem("registers_ready")
        p_ready = sem("onehot_ready")
        pg_ready = sem("gated_onehot_ready")
        G_full = [sem(f"gate_full{i}") for i in (0, 1)]
        G_free = [sem(f"gate_free{i}") for i in (0, 1)]
        U_full = [sem(f"up_full{i}") for i in (0, 1)]
        scatter_added = [sem(f"scatter_added{i}") for i in (0, 1)]
        col_ready = sem("routing_column_ready")
        het_hi_ready = sem("expert_hT_hi_ready")
        he_ready = sem("expert_h_ready")
        heT_full = sem("expert_hT_full")
        heT_ready = sem("expert_hT_ready")
        down_done = sem("expert_down_done")
        y_half_full = sem("expert_y_half_full")
        y_ready = [sem(f"expert_y_ready{i}") for i in (0, 1)]
        pT_full = sem("scatter_onehot_full")
        pT_ready = sem("scatter_onehot_ready")
        xg_hi_ready = sem("gathered_hi_ready")
        gated = sem("hgrn_out_gated")
        mix_float = sem("mix_float_ready")
        out_ready = sem("out_ready")
        out_written = sem("out_written")
        dve_step = sem("dve_step")
        act_step = sem("act_step")
        pool_step = sem("pool_step")

        def chain(eng, signal):
            count = [0]

            def link(ins):
                count[0] += 1
                ins.then_inc(signal, 1)
                eng.wait_ge(signal, count[0])
            return link

        def level_part(x, m, half):
            if m <= 8:
                return x.rearrange("p h (n two m) -> p (h n) two m", two=2, m=m)[:, :, half, :]
            return x[:, :, META:T].rearrange("p h (n two m) -> p h n two m", two=2, m=m)[:, :, :, half, :]

        def second_halves(x, v):
            return x if v == 0 else x.rearrange("p (n two m) -> p n two m", two=2, m=LEVELS[v])[:, :, 1, :]

        def level_blocks(x, m):
            if m <= 8:
                return x.rearrange("p h (n m) -> p (h n) m", m=2 * m)
            return x[:, :, META:T].rearrange("p h (n m) -> p h n m", m=2 * m)

        def difference(eng, v, l):
            m = LEVELS[v]
            if v > 2:
                eng.wait_ge(xq_ready, 7 * l + v - 2)
                eng.wait_ge(xk_ready, 7 * l + v - 2)
            src = level_blocks(B, m)
            ref = src[:, :, m - 1:m] if m <= 8 else src[:, :, :, m - 1:m]
            eng.tensor_tensor(level_blocks(DD[v % 2], m), src, ref.to_broadcast(list(src.shape)),
                              ALU.subtract).then_inc(diff_ready[v % 2], 1)

        def differences(l, v):
            return 4 * l + (v + 1) // 2 if v % 2 else 3 * l + v // 2

        w_in = A["w_in"].rearrange("l (c p) n -> l p c n", p=P)
        w_out = A["w_out"].rearrange("l (c p) n -> l p c n", p=P)
        d1 = A["dense_w1"][0].rearrange("(c p) n -> p c n", p=P)
        d3 = A["dense_w3"][0].rearrange("(c p) n -> p c n", p=P)
        d2 = A["dense_w2"][0].rearrange("(c p) n -> p c n", p=P)
        e1 = A["moe_w1"][0].rearrange("e (c p) n -> e p c n", p=P)
        e3 = A["moe_w3"][0].rearrange("e (c p) n -> e p c n", p=P)
        e2 = A["moe_w2"][0].rearrange("e (c p) n -> e p c n", p=P)

        block = ctx.enter_context(nc.Block())

        @block.sync
        def _(sp):
            sp.dma_start(XTOK, A["x"][0].rearrange("(t p) d -> p t d", p=P)).then_inc(x_in, 16)
            sp.dma_start(MTOK, A["meta"]).then_inc(x_in, 16)
            sp.wait_ge(x_in, 32)
            sp.wait_ge(ident_in, 16)
            sp.wait_ge(vec_in, 16 * 7)
            for n, (kind, i) in enumerate(PREFIX):
                if n >= RING:
                    sp.wait_ge(lo_ready, LAST_UNIT[n - RING] + 1)
                if kind == "w_in":
                    c0 = PROJ[i[1]] * HW
                    src = w_in[i[0]][:, :, c0:c0 + HW]
                elif kind == "w_out":
                    src = w_out[i[0]][:, :, i[1] * HW:(i[1] + 1) * HW]
                elif kind == "w2":
                    src = d2[:, 8 * i[1]:min(8 * i[1] + 8, FC), i[0] * HW:(i[0] + 1) * HW]
                else:
                    src = (d1 if kind == "w1" else d3)[:, :, i * SL:min((i + 1) * SL, FD)]
                dst = slot(n)[:, 0:src.shape[1] * src.shape[2]].rearrange("p (c n) -> p c n", c=src.shape[1])
                sp.dma_start(dst, src).then_inc(slot_full[n % RING], 16)
                if n == 0:
                    sp.dma_start(MASKF, A["masks"]).then_inc(masks_in, 16)

            def half_load(m, expert):
                kind, s = EXPERT[m // 2]
                if kind == "w2":
                    c = s * JC + (m % 2) * 2
                    sp.dma_start(half_slot(m).rearrange("p (c n) -> p c n", c=2),
                                 e2[expert, :, c:c + 2, :]).then_inc(half_full[m % HRING], 16)
                else:
                    c = (m % 2) * 4
                    sp.dma_start(half_slot(m).rearrange("p (c n) -> p c n", c=4),
                                 (e1 if kind == "w1" else e3)[expert, :, c:c + 4, s * SL:(s + 1) * SL]
                                 ).then_inc(half_full[m % HRING], 16)

            def load_when_split(m, expert, blk):
                sp.wait_ge(lo_ready, len(UNITS) + blk * BLOCK_UNITS + 2 * (m - HRING) + 2)
                half_load(m, expert)

            def block_load(expert, blk, after):
                for m in range(EARLY, BLOCK_HALVES):
                    load_when_split(m, expert, blk)
                for m in range(EARLY):
                    load_when_split(m, after, blk + 1)

            for m in range(BLOCK_HALVES):
                if m < 2 * RING:
                    sp.wait_ge(lo_ready, LAST_UNIT[len(PREFIX) - RING + m // 2] + 1)
                elif m == HRING // 2:
                    sp.wait_ge(mix_ready, 16)
                elif m >= HRING:
                    sp.wait_ge(lo_ready, len(UNITS) + 2 * (m - HRING) + 2)
                half_load(m, 0)
            for m in range(EARLY):
                load_when_split(m, 1, 1)
            with sp.Fori(1, NE - 1) as e:
                block_load(e, e, e + 1)
            sp.wait_ge(regs_ready, 1)
            over = sp.value_load(regs[0:1, 0:1], min_val=0, max_val=OVER)
            eids = [sp.value_load(regs[0:1, 1 + j:2 + j], min_val=0, max_val=NE - 1) for j in range(OVER)]
            block_load(NE - 1, NE - 1, eids[0])
            for j in range(OVER):
                with sp.If(over > j):
                    block_load(eids[j], NE + j, eids[min(j + 1, OVER - 1)])
            for t in (0, 1):
                sp.wait_ge(out_ready, t + 1)
                sp.dma_start(out[0, t * P:(t + 1) * P, :], OUTT[:, t, :]).then_inc(out_written, 16)
            sp.wait_ge(out_written, 32)

        @block.tensor
        def _(pe):
            def bank_free(task):
                i = TURN[task]
                if i >= NGB:
                    pe.wait_ge(g_drained[i % NGB], i // NGB)

            def fin(ins, task):
                ins.then_inc(g_full[TURN[task] % NGB], 1)

            pe.wait_ge(ident_in, 16)
            pe.wait_ge(vec_in, 16 * 7)
            pe.transpose(gbank(("vec",))[:, 0:44], VEC[0:44, :], ident[0:44, 0:44]).then_inc(
                g_full[TURN[("vec",)] % NGB], 1)
            pe.wait_ge(init_done, 1)
            fin(pe.matmul(gbank(("rel",))[0:HEADS, 0:RELW], REL, ONEHOT, start=True, stop=True), ("rel",))
            pe.wait_ge(x_in, 32)
            for c in range(DC):
                task = ("xT", c)
                bank_free(task)
                pe.transpose(gbank(task)[:, 0:META], MTOK[:, c * P:(c + 1) * P], ident[0:META, 0:META])
                for t in (0, 1):
                    i = pe.transpose(gbank(task)[:, META + t * P:META + (t + 1) * P],
                                     XTOK[:, t, c * P:(c + 1) * P], ident[:, :])
                fin(i, task)

            def sum_squares(k):
                task = ("ssq", k)
                bank_free(task)
                for c in range(DC):
                    pe.wait_ge(sq_ready, DC * k + c + 1)
                    i = pe.matmul(gbank(task)[:, 0:T], ones[:, :], SQ[:, c, :], start=c == 0, stop=c == DC - 1)
                fin(i, task)

            def split_products(out, w_first, pairs, start, stop, ready=None, count=0):
                for k, (wh, wl, xh, xl) in enumerate(pairs):
                    if ready is not None:
                        pe.wait_ge(ready, count + k + 1)
                    for p, (w, x) in enumerate(((wh, xh), (wh, xl), (wl, xh))):
                        i = pe.matmul(out, *((w, x) if w_first else (x, w)), start=start and k == 0 and p == 0,
                                      stop=stop and k == len(pairs) - 1 and p == 2)
                return i

            def product(task, order=range(DC), ready=None, count=0):
                n = UNIT_OF[task]
                wh, wl = split(WH, n, DC), split(WL, n, DC)
                bank_free(task)
                pe.wait_ge(lo_ready, n + 1)
                fin(split_products(gbank(task)[:, 0:T], True,
                                   [(wh[:, c, :], wl[:, c, :], XH[:, c, :], XL[:, c, :]) for c in order],
                                   True, True, ready, count), task)

            def project(l, s, j):
                first = (s, j) == (ORDER1[0], 0)
                product(("proj", l, s, j), range(DC), u_ready if first else None, 2 * DC * l)

            def mean_squares(l, heads):
                o0 = 0 if l == 0 else META
                for c in heads:
                    task = ("ms", l, c)
                    src = MS_DA if c >= 4 else MS_HG
                    pe.wait_ge(mix_sq, 2 * l + (1 if c >= 4 else 2))
                    bank_free(task)
                    fin(pe.matmul(gbank(task)[:, o0:T], ones[:, :], src[:, c % 4, o0:T], start=True, stop=True), task)

            def to_tokens(l, name, src, k):
                for g, (t0, tn) in enumerate(SEG):
                    task = ("vt", l, name, g)
                    bank_free(task)
                    for h in range(HEADS):
                        i = pe.transpose(gbank(task)[0:tn, h * P:(h + 1) * P], src[:, h, t0:t0 + tn], ident[:, :])
                    fin(i, task)

            units0 = 0
            lv0 = 0
            av0 = 0
            for l in (0, 1):
                sum_squares(2 * l)
                for s in ORDER1:
                    for j in range(JC):
                        project(l, s, j)
                drained(pe, ("proj", l, "dv", JC - 1))
                to_tokens(l, "dv", DV, 0)

                units = attention_units(l)

                def score(i):
                    q, h = units[i]
                    q0, qn = SEG[q]
                    kn = q0 + qn
                    if units0 + i > 0:
                        pe.wait_ge(biased, units0 + i)
                    for c in (0, 1):
                        r = slice(64 * c, 64 * c + 64)
                        ins = pe.matmul(banks[3 + c][0:qn, 0:kn], DQ[r, h, q0:q0 + qn], DK[r, h, 0:kn],
                                        start=True, stop=True)
                    ins.then_inc(score_full, 1)

                def weights_t(i):
                    q, h = units[i]
                    qn = SEG[q][1]
                    pe.wait_ge(a_ready, units0 + i + 1)
                    if units0 + i > 0:
                        pe.wait_ge(aT_drained, units0 + i)
                    for g in range(q + 1):
                        k0, kn = SEG[g]
                        ins = pe.transpose(banks[5][0:kn, g * P:g * P + qn], AA[i % 2][0:qn, k0:k0 + kn],
                                           ident[0:qn, 0:qn])
                    ins.then_inc(aT_full, 1)

                def weigh_v(i):
                    q, h = units[i]
                    qn = SEG[q][1]
                    n = av0 + i // HEADS
                    pe.wait_ge(aT_drained, units0 + i + 1)
                    if h == 0 and n >= 2:
                        pe.wait_ge(av_drained, n - 1)
                    for g in range(q + 1):
                        kn = SEG[g][1]
                        ins = pe.matmul(banks[6 + n % 2][:, h * P:h * P + qn], vtok[0:kn, 0, g, h * P:(h + 1) * P],
                                        AT[0:kn, g, 0:qn], start=g == 0, stop=g == q)
                    ins.then_inc(av_full, 1)

                levels = level_tasks(l)

                def level_scores(v):
                    if v == 0:
                        pe.wait_ge(k_ready, l + 1)
                        pe.wait_ge(qg_ready, 2 * l + 1)
                        pe.wait_ge(biased, units0 + len(units))
                        pe.wait_ge(aT_drained, units0 + len(units))
                        pe.wait_ge(av_drained, av0 + len(units) // HEADS - 1)
                    else:
                        pe.wait_ge(xq_ready, 7 * l + v)
                        pe.wait_ge(xk_ready, 7 * l + v)
                    for i, (a, g) in enumerate(levels):
                        if a != v:
                            continue
                        t0, tn = SEG[g]
                        n = lv0 + i
                        if n >= 4:
                            pe.wait_ge(lv_drained, n - 3)
                        for h in range(HEADS):
                            out = banks[LEVEL_BANKS[n % 4]][0:tn, h * P:h * P + tn]
                            k, q = ((K, Q) if v == 0 else (X[v % 2], X[v % 2]))
                            ins = pe.matmul(out, k[:, h, t0:t0 + tn], q[:, h, t0:t0 + tn], start=True, stop=True)
                        ins.then_inc(lv_full, 1)

                if l == 0:
                    pe.wait_ge(bias_in, 16)
                drained(pe, ("vt", l, "dv", 2))
                for i in range(16):
                    project(l, ORDER2[i // 4], i % 4)
                    if i < len(units):
                        score(i)
                    if 0 <= i - 2 < len(units):
                        weights_t(i - 2)
                    if 0 <= i - 3 < len(units):
                        weigh_v(i - 3)
                    if i == AT_VT:
                        drained(pe, ("proj", l, "hv", JC - 1))
                        to_tokens(l, "hv", HV, 1)
                    if i == AT_KT:
                        pe.wait_ge(kend_ready, l + 1)
                        for g in (0, 1):
                            t0, tn = SEG[g]
                            task = ("kt", l, g)
                            bank_free(task)
                            for h in range(HEADS):
                                ins = pe.transpose(gbank(task)[0:tn, h * P:(h + 1) * P], KEND[:, h, t0:t0 + tn],
                                                   ident[:, :])
                            fin(ins, task)
                    if i >= AT_LEVEL:
                        level_scores(i - AT_LEVEL)
                for g in (0, 1):
                    tn = SEG[g][1]
                    task = ("state", l, g)
                    drained(pe, ("kt", l, g))
                    drained(pe, ("vt", l, "hv", g))
                    bank_free(task)
                    for h in range(HEADS):
                        i = pe.matmul(gbank(task)[:, h * P:(h + 1) * P], KTOK[0:tn, g, h * P:(h + 1) * P],
                                      vtok[0:tn, 1, g, h * P:(h + 1) * P], start=True, stop=True)
                    fin(i, task)
                mean_squares(l, MIX_ORDER[0:4])
                if l == 1:
                    for t in (0, 1):
                        for g in (0, 1):
                            task = ("hTt", t, g)
                            bank_free(task)
                            for c in range(4):
                                i = pe.transpose(gbank(task)[:, c * P:(c + 1) * P],
                                                 hT[:, 4 * g + c, META + t * P:META + (t + 1) * P], ident[:, :])
                            fin(i, task)
                for v in range(16 - AT_LEVEL, len(LEVELS)):
                    level_scores(v)
                pe.wait_ge(lv_drained, lv0 + len(levels))
                pe.wait_ge(qb_ready, l + 1)
                for g in segs_out(l):
                    t0, tn = SEG[g]
                    task = ("o", l, g)
                    drained(pe, ("vt", l, "hv", g))
                    if g > 0:
                        drained(pe, ("state", l, g - 1))
                    bank_free(task)
                    for h in range(HEADS):
                        o = gbank(task)[:, h * P:h * P + tn]
                        i = pe.matmul(o, vtok[0:tn, 1, g, h * P:(h + 1) * P], ST[g][0:tn, h, :], start=True,
                                      stop=g == 0)
                        if g > 0:
                            i = pe.matmul(o, STATE[g - 1][:, h, :], QB[:, h, t0:t0 + tn], start=False, stop=True)
                    fin(i, task)
                mean_squares(l, MIX_ORDER[4:8])
                units0 += len(units)
                lv0 += len(levels)
                av0 += len(units) // HEADS
                if l == 0:
                    for d in range(DC):
                        product(("wo", d), MIX_ORDER, mix_ready if d == 0 else None)
                    sum_squares(1)
                    for i in range(0, FC, JC):
                        for k in ("g", "u"):
                            for f in range(i, min(i + JC, FC)):
                                product((k, f), range(DC), u_ready if (k, f) == ("g", 0) else None, DC)
                    drained(pe, ("u", FC - 1))
                    for half in (0, 1):
                        for u in range(FC // 2):
                            n = UNIT_OF[("down", 1)] - (2 - half) * (FC // 2) + 1 + u
                            wh, wl = split(WH, n, 2), split(WL, n, 2)
                            pe.wait_ge(lo_ready, n + 1)
                            pe.wait_ge(al_ready, 2 * u + 2)
                            for d in range(4):
                                c = slice(d * P, (d + 1) * P)
                                i = split_products(banks[(3 + 4 * half + d) % 8][:, 0:T], True,
                                                   [(wh[:, k, c], wl[:, k, c], act_hi[:, 2 * u + k, :],
                                                     act_lo[:, 2 * u + k, :]) for k in (0, 1)],
                                                   u == 0, u == FC // 2 - 1)
                                if u == FC // 2 - 1:
                                    i.then_inc(down_full, 1)
                            if u < FC // 2 - 1:
                                i.then_inc(unit_done, 1)
                    pe.wait_ge(down_drained, 8)
            for half in (0, 1):
                for t in (0, 1):
                    bank_free(("wo1", half, t))
                for u in range(DC // 2):
                    n = UNIT_OF[("wo1", 1, 1)] - (2 - half) * (DC // 2) + 1 + u
                    wh, wl = split(WH, n, 2), split(WL, n, 2)
                    pe.wait_ge(lo_ready, n + 1)
                    last = u == DC // 2 - 1
                    if half == 0:
                        pe.wait_ge(mix_ready, DC + 2 * u + 2)
                    c = MIX_ORDER[2 * u]
                    for t in (0, 1):
                        task = ("wo1", half, t)
                        r = slice(META + t * P, META + (t + 1) * P)
                        i = split_products(gbank(task)[:, :], False,
                                           [(wh[:, k, :], wl[:, k, :], XH[:, c + k, r], XL[:, c + k, r])
                                            for k in (0, 1)], u == 0, last)
                        if last:
                            fin(i, task)
                    if not last:
                        i.then_inc(unit_done, 1)
            for t in (0, 1):
                pe.wait_ge(utok_ready, t + 1)
                for g in (0, 1):
                    task = ("rT", t, g)
                    bank_free(task)
                    for c in range(4):
                        i = pe.transpose(gbank(task)[:, c * P:(c + 1) * P], UTOK[:, t, (4 * g + c) * P:(4 * g + c + 1) * P],
                                         ident[:, :])
                    fin(i, task)
            pe.wait_ge(tables_in, 16 * 4)
            task = ("logit",)
            bank_free(task)
            for t in (0, 1):
                drained(pe, ("rT", t, 0))
                drained(pe, ("rT", t, 1))
                for c in range(DC):
                    i = pe.matmul(gbank(task)[:, t * NE:(t + 1) * NE], UTR[:, c, t * P:(t + 1) * P], ROUT[:, c, :],
                                  start=c == 0, stop=c == DC - 1)
            fin(i, task)
            pe.wait_ge(mask_ready, 1)
            task = ("rank",)
            bank_free(task)
            r = gbank(task)
            pe.matmul(r[:, 0:NE], UPPER, MASK[:, 0, :], start=True, stop=True)
            for i, first in ((1, UPPER), (2, ones[:, :])):
                pe.matmul(r[:, i * NE:(i + 1) * NE], ones[:, :], MASK[:, 0, :], start=True, stop=False)
                ins = pe.matmul(r[:, i * NE:(i + 1) * NE], first, MASK[:, 1, :], start=False, stop=True)
            fin(ins, task)
            drained(pe, task)

            def gather(n, wait_banks):
                pe.wait_ge(p_ready, n + 1)
                for b in (0, 1):
                    if wait_banks:
                        pe.wait_ge(G_free[b], n * G_USES[b])
                    for c in range(4):
                        o = banks[b][:, c * P:(c + 1) * P]
                        for t in (0, 1):
                            i = pe.matmul(o, UTOK[:, t, (4 * b + c) * P:(4 * b + c + 1) * P], PH[:, t, :],
                                          start=t == 0, stop=t == 1)
                    i.then_inc(G_full[b], 1)

            def expert_block(n):
                def unit_in(key, u):
                    m = 4 * EXPERT_AT[key] + u
                    pe.wait_ge(lo_ready, len(UNITS) + n * BLOCK_UNITS + m + 1)
                    return (split(b, len(UNITS) + m, 1 if key[0] == "w2" else 2) for b in (WH, WL))

                def up(kind, s):
                    b = s % 2
                    bank0, fulls = (0, G_full) if kind == "w1" else (2, U_full)
                    if kind == "w1":
                        pe.wait_ge(G_free[b], n * G_USES[b] + s // 2 + 1)
                    elif s >= 2:
                        pe.wait_ge(he_ready, n * NS + s - 1)
                    else:
                        pe.wait_ge(scatter_added[b], 2 * n + 1)
                    for u in range(4):
                        wh, wl = unit_in((kind, s), u)
                        i = split_products(banks[bank0 + b][:, :], False,
                                           [(wh[:, k, :], wl[:, k, :], xg_hi[:, 2 * u + k, :], xg_lo[:, 2 * u + k, :])
                                            for k in (0, 1)], u == 0, u == 3)
                        i.then_inc(unit_done if u < 3 else fulls[b], 1)

                def turn_h(s):
                    pe.wait_ge(he_ready, n * NS + s + 1)
                    if s > 0:
                        pe.wait_ge(heT_ready, n * NS + s)
                    for j in range(JC):
                        i = pe.transpose(banks[4][:, j * P:(j + 1) * P], HE[:, s % 2, j * P:(j + 1) * P], ident[:, :])
                    i.then_inc(heT_full, 1)

                def down_part(s, j, half):
                    wh, wl = unit_in(("w2", s), j)
                    c = slice(j * P, (j + 1) * P)
                    d = slice(half * 512, (half + 1) * 512)
                    return split_products(banks[5 + half][:, :], False,
                                          [(wh[:, 0, d], wl[:, 0, d], het_hi[:, s % 2, c], het_lo[:, s % 2, c])],
                                          s == 0 and j == 0, s == NS - 1 and j == JC - 1)

                def down(s):
                    pe.wait_ge(heT_ready, n * NS + s + 1)
                    for j in range(JC):
                        down_part(s, j, 0)
                        down_part(s, j, 1).then_inc(unit_done if j < JC - 1 else down_done, 1)

                def down_last():
                    s = NS - 1
                    pe.wait_ge(heT_ready, n * NS + s + 1)
                    for j in range(JC):
                        i = down_part(s, j, 0)
                    i.then_inc(y_half_full, 1)
                    for j in range(JC):
                        down_part(s, j, 1).then_inc(unit_done if j < JC - 1 else down_done, 1)

                pe.wait_ge(G_free[1], n * G_USES[1] + 1)
                for s in range(NS):
                    up("w1", s)
                    if s == 0:
                        pe.wait_ge(pg_ready, n + 1)
                        for t in (0, 1):
                            i = pe.transpose(banks[7][:, t * P:(t + 1) * P], PG[:, t, :], ident[:, :])
                        i.then_inc(pT_full, 1)
                    else:
                        turn_h(s - 1)
                    up("w3", s)
                    if s > 0:
                        down(s - 1)
                turn_h(NS - 1)
                gather(n + 1, True)
                down_last()
                pe.wait_ge(pT_ready, n + 1)
                for half in (0, 1):
                    pe.wait_ge(y_ready[half], n + 1)
                    for t in (0, 1):
                        pe.matmul(scatter_bank(half, t), PT[:, t, :], YS[:, half * 512:(half + 1) * 512],
                                  start=True, stop=True).then_inc(U_full[t], 1)

            gather(0, False)
            with pe.Fori(0, NE) as e:
                expert_block(e)
            pe.wait_ge(regs_ready, 1)
            over = pe.value_load(regs[0:1, 0:1], min_val=0, max_val=OVER)
            for j in range(OVER):
                with pe.If(over > j):
                    expert_block(NE + j)

        @block.scalar
        def _(act):
            link = chain(act, act_step)
            act.preload_act_table_set("natural_log_exp_and_others")
            act.dma_start(ident[:, :], A["ident"]).then_inc(ident_in, 16)
            act.dma_start(VEC[0:16, :], A["norm_mix"].rearrange("l (c p) -> (l c) p", p=P)).then_inc(vec_in, 16)
            act.dma_start(VEC[16:32, :], A["norm_ffn"].rearrange("l (c p) -> (l c) p", p=P)).then_inc(vec_in, 16)
            act.dma_start(VEC[32:40, :], A["hg_lb_logits"].rearrange("l (c p) -> (l c) p", p=P)).then_inc(vec_in, 16)
            act.dma_start(VEC[40:42, :], A["hg_norm_w"]).then_inc(vec_in, 16)
            act.dma_start(VEC[42:44, :], A["da_subln_w"]).then_inc(vec_in, 16)
            act.dma_start(REL[0:32, :], A["rel_bias"]).then_inc(vec_in, 16)
            act.dma_start(ONEHOT, A["buckets"]).then_inc(vec_in, 16)
            act.dma_start(LAMIN, A["da_lambda"].rearrange("l a d -> (l a d)").partition_broadcast(P)).then_inc(lam_in, 16)
            full(act, ("rel",))
            drain(act.copy(RELROW, gbank(("rel",))[0:HEADS, 0:RELW]), ("rel",))

            def squares(k):
                if k == 0:
                    for c in range(DC):
                        drained(act, ("xT", c))
                        act.activation(SQ[:, c, :], hT[:, c, :], ACT.Square).then_inc(sq_ready, 1)
                    for n in range(AHEAD - 1):
                        split_hi(act, n)
                inverse_root(k)
                if k == 0:
                    split_hi(act, AHEAD - 1)

            def inverse_root(k):
                task = ("ssq", k)
                full(act, task)
                drain(act.activation(rstd, gbank(task)[:, 0:T], ACT.Ln, scale=1.0 / D, bias=eps_t[:, 0:1]), task)
                drained(act, task)
                act.activation(rstd, rstd, ACT.Exp, scale=-0.5).then_inc(rstd_ready, 1)

            def halves(k):
                for c in range(DC):
                    act.wait_ge(uf_ready, DC * k + c + 1)
                    act.copy(XH[:, c, :], UF[:, c, :]).then_inc(xh_ready, 1)

            def inverse_roots(l, heads):
                o0 = 0 if l == 0 else META
                for c in heads:
                    task = ("ms", l, c)
                    dst = (MS_DA if c >= 4 else MS_HG)[:, c % 4, o0:T]
                    full(act, task)
                    drain(act.activation(dst, gbank(task)[:, o0:T], ACT.Ln, scale=1.0 / P, bias=eps_t[:, 0:1]), task)
                for c in heads:
                    drained(act, ("ms", l, c))
                    dst = (MS_DA if c >= 4 else MS_HG)[:, c % 4, o0:T]
                    act.activation(dst, dst, ACT.Exp, scale=-0.5).then_inc(mix_rstd, 1)

            def mix_halves(l, heads):
                o0 = 0 if l == 0 else META
                for h in heads:
                    act.wait_ge(mix_float, 8 * l + (h + 4) % 8 + 1)
                    act.copy(XH[:, h, o0:T], (ODA if h >= 4 else OHG)[:, h % 4, o0:T]).then_inc(mh_ready, 1)

            def copy_proj(l, s, dst):
                for j in range(JC):
                    task = ("proj", l, s, j)
                    split_hi(act, UNIT_OF[task] + AHEAD)
                    full(act, task)
                    drain(act.copy(dst[:, j, :], gbank(task)[:, 0:T]), task)

            def copy_vt(l, name, k):
                for g, (t0, tn) in enumerate(SEG):
                    task = ("vt", l, name, g)
                    full(act, task)
                    drain(act.copy(vtok[0:tn, k, g, :], gbank(task)[0:tn, :]), task)

            units0 = 0
            av0 = 0
            for l in (0, 1):
                squares(2 * l)
                halves(2 * l)
                if l == 0:
                    act.wait_ge(lam_ready, 1)
                    act.activation(lamt[:, 4:8], lamt[:, 0:4], ACT.Exp).then_inc(lam_ready, 1)
                    act.wait_ge(lam_ready, 3)
                    act.activation(lbt[:, 1, :], lbt[:, 1, :], ACT.Exp).then_inc(lam_ready, 1)
                copy_proj(l, "dq", DQ)
                copy_proj(l, "dk", DK)
                copy_proj(l, "dv", DV)
                copy_vt(l, "dv", 0)
                units = attention_units(l)

                def exps(i):
                    q, h = units[i]
                    qn = SEG[q][1]
                    kn = SEG[q][0] + qn
                    b = i % 2
                    act.wait_ge(biased, units0 + i + 1)
                    for c in (0, 1):
                        ins = act.activation(S2[b][0:qn, c, 0:kn], S2[b][0:qn, c, 0:kn], ACT.Exp,
                                             bias=stat[0:qn, 4 * b + c:4 * b + c + 1],
                                             accum_out=stat[0:qn, 8 + 4 * b + c:8 + 4 * b + c + 1])
                    ins.then_inc(exp_done, 1)

                def copy_at(i):
                    q, h = units[i]
                    qn = SEG[q][1]
                    act.wait_ge(aT_full, units0 + i + 1)
                    if i > 0:
                        act.wait_ge(av_full, units0 + i)
                    for g in range(q + 1):
                        kn = SEG[g][1]
                        ins = act.copy(AT[0:kn, g, 0:qn], banks[5][0:kn, g * P:g * P + qn])
                    ins.then_inc(aT_drained, 1)

                def copy_av(i):
                    q = units[i][0]
                    t0, tn = SEG[q]
                    n = av0 + i // HEADS
                    act.wait_ge(av_full, units0 + i + 1)
                    act.copy(ODA[:, :, t0:t0 + tn],
                             banks[6 + n % 2][:, :].rearrange("p (h t) -> p h t", h=HEADS)[:, :, 0:tn]
                             ).then_inc(av_drained, 1)

                def decays(v):
                    m = LEVELS[v]
                    act.wait_ge(diff_ready[v % 2], differences(l, v))
                    for half in (0, 1):
                        part = level_part(DD[v % 2], m, half)
                        ins = act.activation(part, part, ACT.Exp, scale=1.0 if half else -1.0)
                    ins.then_inc(decay_ready, 1)

                def sigmoid_of_tmp(i, step):
                    if step == 0:
                        act.wait_ge(t_clamped, 2 * l + i + 1)
                        act.activation(TMP, TMP, ACT.Exp, scale=-1.0).then_inc(t_step, 1)
                    elif step == 1:
                        act.wait_ge(t_step, 4 * l + 2 * i + 1)
                        act.activation(TMP, TMP, ACT.Ln, bias=1.0).then_inc(t_step, 1)
                    else:
                        act.wait_ge(t_step, 4 * l + 2 * i + 2)
                        act.activation(TMP, TMP, ACT.Exp, scale=-1.0).then_inc(t_sig, 1)

                dsts = {"hq": Q, "hg": G, "hv": HV}
                for i in range(16):
                    s, j = ORDER2[i // 4], i % 4
                    split_hi(act, UNIT_OF[("proj", l, s, j)] + AHEAD)
                    if i < len(units):
                        exps(i)
                    if s != "hf":
                        task = ("proj", l, s, j)
                        full(act, task)
                        drain(act.copy(dsts[s][:, j, :], gbank(task)[:, 0:T]), task)
                    if 0 <= i - 2 < len(units):
                        copy_at(i - 2)
                    if 0 <= i - 3 < len(units) and (i - 3) % HEADS == HEADS - 1:
                        copy_av(i - 3)
                    if i == 4:
                        drained(act, ("proj", l, "hf", JC - 1))
                        act.activation(EF, EF, ACT.Exp, scale=-1.0).then_inc(f_exp, 1)
                    if i == 5:
                        act.wait_ge(f_exp, l + 1)
                        act.activation(SG, EF, ACT.Ln, bias=1.0).then_inc(f_ln, 1)
                    if i == 6:
                        act.wait_ge(f_ln, l + 1)
                        act.activation(SG, SG, ACT.Exp, scale=-1.0).then_inc(f_sig, 1)
                    if i == 8:
                        act.wait_ge(f_gate, l + 1)
                        act.activation(LF, LF, ACT.Ln).then_inc(f_log, 1)
                    if i in (9, 10, 11):
                        sigmoid_of_tmp(0, i - 9)
                    if i == 12:
                        act.wait_ge(kdiff, l + 1)
                        act.activation(KEND[:, :, 0:SEG[2][0]], KEND[:, :, 0:SEG[2][0]], ACT.Exp).then_inc(kexp, 1)
                    if i in (12, 13):
                        decays(i - 11)
                    if i == 14:
                        act.wait_ge(b_ready, l + 1)
                        act.wait_ge(k_ready, l + 1)
                        act.activation(SG, B, ACT.Exp).then_inc(expb, 1)
                        act.activation(bend[:, :], B[:, :, SEG[1][0] + P - 1], ACT.Exp).then_inc(expb, 1)
                    if i == AT_VT:
                        copy_vt(l, "hv", 1)
                    if i == AT_KT:
                        for g in (0, 1):
                            tn = SEG[g][1]
                            task = ("kt", l, g)
                            full(act, task)
                            drain(act.copy(KTOK[0:tn, g, :], gbank(task)[0:tn, :]), task)
                decays(3)
                o0 = 0 if l == 0 else META
                act.wait_ge(av_drained, av0 + len(units) // HEADS)
                act.activation(MS_DA[:, :, o0:T], ODA[:, :, o0:T], ACT.Square).then_inc(mix_sq, 1)
                decays(4)
                inverse_roots(l, MIX_ORDER[0:4])
                decays(5)
                if l == 1:
                    for t in (0, 1):
                        for g in (0, 1):
                            task = ("hTt", t, g)
                            full(act, task)
                            full(act, ("state", l, 0))
                            drain(act.copy(HTOK[:, t, g * 512:(g + 1) * 512], gbank(task)[:, :]), task)
                decays(6)
                decays(7)
                sigmoid_of_tmp(1, 0)
                mix_halves(l, MIX_ORDER[0:4])
                sigmoid_of_tmp(1, 1)
                sigmoid_of_tmp(1, 2)
                for g in segs_out(l):
                    t0, tn = SEG[g]
                    task = ("o", l, g)
                    full(act, task)
                    drain(act.copy(OHG[:, :, t0:t0 + tn],
                                   gbank(task)[:, :].rearrange("p (h t) -> p h t", h=HEADS)[:, :, 0:tn]), task)
                    if g == 1:
                        for k in segs_out(l)[:-1]:
                            drained(act, ("o", l, k))
                        act.activation(MS_HG[:, :, o0:SEG[2][0]], OHG[:, :, o0:SEG[2][0]], ACT.Square)
                drained(act, ("o", l, 2))
                act.activation(MS_HG[:, :, SEG[2][0]:T], OHG[:, :, SEG[2][0]:T], ACT.Square).then_inc(mix_sq, 1)
                inverse_roots(l, MIX_ORDER[4:8])
                mix_halves(l, MIX_ORDER[4:8])
                units0 += len(units)
                av0 += len(units) // HEADS
                if l == 0:
                    for c in range(DC):
                        split_hi(act, UNIT_OF[("wo", c)] + AHEAD)
                        drained(act, ("wo", c))
                        act.activation(SQ[:, c, :], hT[:, c, :], ACT.Square).then_inc(sq_ready, 1)
                    inverse_root(1)
                    halves(1)

                    def act_high(f):
                        drained(act, ("u", f))
                        act.copy(act_hi[:, f, :], ACTF[:, f % 2, :]).then_inc(ah_ready, 1)

                    for i in range(0, FC, JC):
                        n = min(JC, FC - i)
                        for f in range(i, i + n):
                            split_hi(act, UNIT_OF[("g", f)] + AHEAD)
                            task = ("g", f)
                            full(act, task)
                            drain(act.activation(SGF[:, f % JC, :], gbank(task)[:, 0:T], ACT.Silu), task)
                        for f in range(i, i + n):
                            split_hi(act, UNIT_OF[("u", f)] + AHEAD)
                            act_high(f)
                    act.preload_act_table_set("natural_log_exp_and_others")
                    for u in range(FC):
                        split_hi(act, UNIT_OF[("u", FC - 1)] + 1 + u + AHEAD)
                    for c in range(DC):
                        act.wait_ge(down_drained, c + 1)
                        act.activation(SQ[:, c, :], hT[:, c, :], ACT.Square).then_inc(sq_ready, 1)
            for u in range(DC):
                split_hi(act, UNIT_OF[("wo1", 1, 1)] - DC + 1 + u + AHEAD)
            for t in (0, 1):
                drained(act, ("wo1", 0, t))
                drained(act, ("wo1", 1, t))
                act.activation(JUNK[:, :], HTOK[:, t, :], ACT.Square, accum_out=RSUM[:, t:t + 1]).then_inc(tok_sum, 1)
                act.wait_ge(tok_sum, t + 1)
                link(act.activation(RSUM[:, t:t + 1], RSUM[:, t:t + 1], ACT.Ln, scale=1.0 / D, bias=eps_t[:, 0:1]))
                act.activation(RSUM[:, t:t + 1], RSUM[:, t:t + 1], ACT.Exp, scale=-0.5).then_inc(tok_rstd, 1)

            def high_unit(n, m):
                half = m // 2
                if m % 2 == 0:
                    act.wait_ge(half_full[half % HRING],
                                n * (16 * BLOCK_HALVES // HRING) + 16 * (half // HRING + 1))
                if m >= NW:
                    expert_unit_used(act, n, m - NW)
                elif type(n) is not int or n > 0:
                    expert_unit_used(act, n - 1, BLOCK_UNITS + m - NW)
                else:
                    unit_used(act, len(UNITS) + m - NW)
                src = half_slot(half)[:, (m % 2) * UNIT:(m % 2 + 1) * UNIT]
                act.copy(WH[:, (len(UNITS) + m) % NW, :], src).then_inc(hi_ready, 1)

            for m in range(AHEAD):
                high_unit(0, m)
            for t in (0, 1):
                for g in (0, 1):
                    task = ("rT", t, g)
                    full(act, task)
                    drain(act.copy(UTR[:, 4 * g:4 * g + 4, t * P:(t + 1) * P],
                                   gbank(task)[:, :].rearrange("p (c t) -> p c t", c=4)), task)
            act.wait_ge(top_ready, 1)
            act.activation(GATE2[:, :, 1], GATE2[:, :, 1], ACT.Exp).then_inc(gate_exp, 1)

            def gather_high(b, n):
                act.wait_ge(G_full[b], n)
                act.copy(xg_hi[:, 4 * b:4 * b + 4, :], banks[b][:, :].rearrange("p (c s) -> p c s", c=4)
                         ).then_inc(xg_hi_ready, 1)

            for b in (0, 1):
                gather_high(b, 1)

            def expert_block(n):
                def high(m):
                    if m < BLOCK_UNITS:
                        high_unit(n, m)
                    else:
                        high_unit(n + 1, m - BLOCK_UNITS)

                def turn(s):
                    act.wait_ge(heT_full, n * NS + s + 1)
                    if s >= 2:
                        act.wait_ge(down_done, n * NS + s)
                    act.copy(het_hi[:, s % 2, :], banks[4][:, :]).then_inc(het_hi_ready, 1)

                m = 0
                for kind, s in EXPERT:
                    for u in range(4):
                        if m + AHEAD != BLOCK_UNITS - 1:
                            high(m + AHEAD)
                        if kind == "w3" and u == 0 and s > 0:
                            turn(s - 1)
                        if (kind, s) == ("w2", NS - 1) and u == 0:
                            act.wait_ge(y_half_full, n + 1)
                            act.copy(YS[:, 0:512], banks[5][:, :]).then_inc(y_ready[0], 1)
                        m += 1
                    if kind == "w1":
                        b = s % 2
                        act.wait_ge(G_full[b], n * G_USES[b] + s // 2 + 2)
                        if s >= 2:
                            act.wait_ge(he_ready, n * NS + s - 1)
                        act.activation(SGE[:, b, :], banks[b][:, :], ACT.Silu).then_inc(G_free[b], 1)
                        if s == 0:
                            act.wait_ge(pT_full, n + 1)
                            act.copy(PT, banks[7][:, 0:2 * P].rearrange("p (t s) -> p t s", t=2)).then_inc(pT_ready, 1)
                    if (kind, s) == ("w2", NS - 2):
                        turn(NS - 1)
                        high(BLOCK_UNITS - 1)
                        for b in (0, 1):
                            gather_high(b, n * G_USES[b] + G_USES[b] + 1)

            act.preload_act_table(ACT.Silu)
            with act.Fori(0, NE) as e:
                expert_block(e)
            act.wait_ge(regs_ready, 1)
            over = act.value_load(regs[0:1, 0:1], min_val=0, max_val=OVER)
            for j in range(OVER):
                with act.If(over > j):
                    expert_block(NE + j)
            act.preload_act_table_set("natural_log_exp_and_others")
            act.wait_ge(tok_sum, 3)
            for t in (0, 1):
                link(act.activation(JUNK[:, :], HTOK[:, t, :], ACT.Square, accum_out=RSUM[:, 2 + t:3 + t]))
            link(act.activation(RSUM[:, 2:4], RSUM[:, 2:4], ACT.Ln, scale=1.0 / D, bias=eps_t[:, 0:1]))
            act.activation(RSUM[:, 2:4], RSUM[:, 2:4], ACT.Exp, scale=-0.5).then_inc(tok_rstd, 1)

        @block.vector
        def _(dve):
            link = chain(dve, dve_step)
            dve.memset(ones[:, :], 1.0)
            dve.memset(eps_t[:, :], EPS)
            dve.memset(ONE8, 1.0)
            dve.memset(lbt[:, 0, :], 0.0)
            dve.memset(omlb[:, 0, :], 1.0)
            dve.memset(REL[32:33, :], NEG).then_inc(init_done, 1)
            full(dve, ("vec",))
            drain(dve.tensor_copy(vecT[:, 0:44], gbank(("vec",))[:, 0:44]), ("vec",))
            drained(dve, ("vec",))
            for c in range(DC):
                task = ("xT", c)
                full(dve, task)
                drain(dve.tensor_copy(hT[:, c, :], gbank(task)[:, 0:T]), task)

            def normed(k, col):
                dve.wait_ge(rstd_ready, k + 1)
                for c in range(DC + 2):
                    if c < DC:
                        dve.scalar_tensor_tensor(UF[:, c, :], hT[:, c, :], vecT[:, col + c:col + c + 1], rstd,
                                                 ALU.mult, ALU.mult).then_inc(uf_ready, 1)
                    if c >= 2:
                        dve.wait_ge(xh_ready, DC * k + c - 1)
                        dve.tensor_tensor(XL[:, c - 2, :], UF[:, c - 2, :], XH[:, c - 2, :].bitcast(F32),
                                          ALU.subtract).then_inc(u_ready, 1)

            def softmax_in(l, i):
                q, h = attention_units(l)[i]
                qn = SEG[q][1]
                kn = SEG[q][0] + qn
                b = i % 2
                n = units0 + i
                dve.wait_ge(score_full, n + 1)
                if n >= 2:
                    dve.wait_ge(a_ready, n - 1)
                if n == 0:
                    dve.wait_ge(bias_in, 16)
                b0 = SEG[2][0] - SEG[q][0]
                for c in (0, 1):
                    ins = dve.scalar_tensor_tensor(S2[b][0:qn, c, 0:kn], banks[3 + c][0:qn, 0:kn], 0.125,
                                                   bias[0:qn, h, b0:b0 + kn], ALU.mult, ALU.add)
                link(ins)
                link(dve.tensor_reduce(stat[0:qn, 4 * b:4 * b + 2], S2[b][0:qn, :, 0:kn], AX.X, ALU.max))
                dve.tensor_scalar(stat[0:qn, 4 * b:4 * b + 2], stat[0:qn, 4 * b:4 * b + 2], -1.0, None,
                                  ALU.mult).then_inc(biased, 1)

            def softmax_out(l, i):
                q, h = attention_units(l)[i]
                qn = SEG[q][1]
                kn = SEG[q][0] + qn
                b = i % 2
                n = units0 + i
                r = stat[0:qn, 8 + 4 * b:10 + 4 * b]
                dve.wait_ge(exp_done, n + 1)
                link(dve.reciprocal(r, r))
                link(dve.tensor_tensor(r[:, 1:2], r[:, 1:2], lamt[0:qn, 8 + l:9 + l], ALU.mult))
                if i >= 2:
                    dve.wait_ge(aT_full, n - 1)
                link(dve.tensor_scalar(AA[b][0:qn, 0:kn], S2[b][0:qn, 1, 0:kn], r[:, 1:2], None, ALU.mult))
                dve.scalar_tensor_tensor(AA[b][0:qn, 0:kn], S2[b][0:qn, 0, 0:kn], r[:, 0:1], AA[b][0:qn, 0:kn],
                                         ALU.mult, ALU.add).then_inc(a_ready, 1)

            units0 = 0
            lv0 = 0
            for l in (0, 1):
                if l == 0:
                    for n in range(AHEAD - 1):
                        split_lo(dve, n)
                    dve.wait_ge(masks_in, 16)
                    link(dve.tensor_copy(masks[:, :, :], MASKF))
                normed(2 * l, 8 * l)
                if l == 0:
                    split_lo(dve, AHEAD - 1)
                    dve.wait_ge(lam_in, 16)
                    lv = LAMIN.rearrange("p (k two d) -> p k two d", two=2, d=64)
                    link(dve.tensor_tensor(LAMP.rearrange("p (k d) -> p k d", d=64), lv[:, :, 0, :], lv[:, :, 1, :], ALU.mult))
                    dve.tensor_reduce(lamt[:, 0:4], LAMP.rearrange("p (k d) -> p k d", d=64), AX.X, ALU.add).then_inc(lam_ready, 1)
                    dve.wait_ge(lam_ready, 2)
                    link(dve.tensor_tensor(lbt[:, 1, :], vecT[:, 32:36], vecT[:, 36:40], ALU.subtract))
                    dve.tensor_scalar(lbt[:, 1, :], lbt[:, 1, :], -FLOOR, None, ALU.min).then_inc(lam_ready, 1)
                    for k in (0, 1):
                        e = lamt[:, 4 + 2 * k:6 + 2 * k]
                        link(dve.tensor_tensor(lamt[:, 8 + k:9 + k], e[:, 1:2], e[:, 0:1], ALU.subtract))
                        link(dve.tensor_scalar(lamt[:, 8 + k:9 + k], lamt[:, 8 + k:9 + k], -lam_init(k), None, ALU.add))
                        link(dve.tensor_scalar(subw[:, k:k + 1], vecT[:, 42 + k:43 + k], 1.0 - lam_init(k), None, ALU.mult))
                    dve.wait_ge(lam_ready, 4)
                    link(dve.tensor_scalar(lbt[:, 1, :], lbt[:, 1, :], 1.0, None, ALU.add))
                    link(dve.reciprocal(lbt[:, 1, :], lbt[:, 1, :]))
                    link(dve.tensor_scalar(lbt[:, 1, :], lbt[:, 1, :], 0.0, LB_MAX, ALU.max, ALU.min))
                    dve.tensor_scalar(omlb[:, 1, :], lbt[:, 1, :], -1.0, 1.0, ALU.mult, ALU.add).then_inc(init_done, 1)
                units = attention_units(l)
                levels = level_tasks(l)

                def decayed_q(v):
                    m = LEVELS[v]
                    dve.wait_ge(decay_ready, 7 * l + v)
                    if v > 2:
                        dve.wait_ge(lv_full, lv0 + sum(1 for a, _ in levels if a <= v - 2))
                    dve.tensor_tensor(level_part(X[v % 2], m, 1), level_part(Q, m, 1), level_part(DD[v % 2], m, 1),
                                      ALU.mult).then_inc(xq_ready, 1)

                def level_drain(v):
                    for i, (a, g) in enumerate(levels):
                        if a != v:
                            continue
                        tn = SEG[g][1]
                        n = lv0 + i
                        dve.wait_ge(lv_full, n + 1)
                        if n > 0:
                            dve.wait_ge(lv_drained, n)
                        bank = banks[LEVEL_BANKS[n % 4]][0:tn, :].rearrange("p (h t) -> p h t", h=HEADS)[:, :, 0:tn]
                        m = second_halves(masks[0:tn, v, 0:tn], v).unsqueeze(1)
                        out = ST[g][0:tn, :, :]
                        if v > 0:
                            out, bank = (x.rearrange("p h (n two m) -> p h n two m", two=2, m=LEVELS[v])[:, :, :, 1, :]
                                         for x in (out, bank))
                        dve.copy_predicated(out, m.to_broadcast(list(out.shape)), bank).then_inc(lv_drained, 1)

                for s in ORDER1:
                    for j in range(JC):
                        split_lo(dve, UNIT_OF[("proj", l, s, j)] + AHEAD)
                for i in range(16):
                    if i > AT_LEVEL:
                        dve.wait_ge(st_zero, l + 1)
                        level_drain(i - AT_LEVEL - 1)
                    if i < 4:
                        task = ("proj", l, "hf", i)
                        full(dve, task)
                        drain(dve.tensor_scalar(EF[:, i, :], gbank(task)[:, 0:T], FLOOR, None, ALU.max), task)
                    if i < len(units):
                        softmax_in(l, i)
                    split_lo(dve, UNIT_OF[("proj", l, ORDER2[i // 4], i % 4)] + AHEAD)
                    if 0 <= i - 1 < len(units):
                        softmax_out(l, i - 1)
                    if i == 7:
                        dve.wait_ge(f_sig, l + 1)
                        for h in range(HEADS):
                            ins = dve.scalar_tensor_tensor(K[:, h, :], EF[:, h, :], omlb[:, l, h:h + 1], SG[:, h, :],
                                                           ALU.mult, ALU.mult)
                        ins.then_inc(k_ready, 1)
                    if i == 9:
                        dve.wait_ge(f_log, l + 1)
                        for h in range(HEADS):
                            for t0, tn in SEG:
                                ins = dve.tensor_tensor_scan(B[:, h, t0:t0 + tn], ones[:, 0:tn], LF[:, h, t0:t0 + tn],
                                                             0.0, ALU.mult, ALU.add)
                        ins.then_inc(b_ready, 1)
                    if i == 8:
                        drained(dve, ("proj", l, "hq", JC - 1))
                        dve.tensor_scalar(TMP, Q, FLOOR, None, ALU.max).then_inc(t_clamped, 1)
                    if i in (10, 11):
                        if i == 10:
                            dve.wait_ge(b_ready, l + 1)
                            full(dve, ("vt", l, "dv", 2))
                        difference(dve, i - 9, l)
                    if i == 13:
                        dve.wait_ge(qg_ready, 2 * l + 1)
                        decayed_q(1)
                    if i == 14:
                        decayed_q(2)
                        difference(dve, 3, l)
                    if i == 15:
                        decayed_q(3)
                level_drain(15 - AT_LEVEL)
                for g in (0, 1):
                    task = ("state", l, g)
                    full(dve, task)
                    if g == 0:
                        drain(dve.tensor_copy(STATE[0].rearrange("p h v -> p (h v)"), gbank(task)[:, :]), task)
                        drained(dve, task)
                        dve.wait_ge(expb, 2 * l + 2)
                    else:
                        for h in range(HEADS):
                            ins = dve.scalar_tensor_tensor(STATE[1][:, h, :], STATE[0][:, h, :], bend[:, h:h + 1],
                                                           gbank(task)[:, h * P:(h + 1) * P], ALU.mult, ALU.add)
                        drain(ins, task)
                def mix_low(h):
                    dve.wait_ge(mh_ready, 8 * l + (h + 4) % 8 + 1)
                    dve.tensor_tensor(XL[:, h, o0:T], (ODA if h >= 4 else OHG)[:, h % 4, o0:T],
                                      XH[:, h, o0:T].bitcast(F32), ALU.subtract).then_inc(mix_ready, 1)

                o0 = 0 if l == 0 else META
                for v in range(15 - AT_LEVEL, len(LEVELS)):
                    if v > 15 - AT_LEVEL:
                        level_drain(v)
                    if v + 2 < len(LEVELS):
                        decayed_q(v + 2)
                    if v in (2, 4):
                        difference(dve, v + 3, l)
                    if v == 4:
                        drained(dve, ("proj", l, "hg", JC - 1))
                        dve.tensor_scalar(TMP, G, FLOOR, None, ALU.max).then_inc(t_clamped, 1)
                    if v == 5:
                        for h in range(HEADS):
                            dve.wait_ge(mix_rstd, 8 * l + h + 1)
                            dve.scalar_tensor_tensor(ODA[:, h, o0:T], ODA[:, h, o0:T], subw[:, l:l + 1],
                                                     MS_DA[:, h, o0:T], ALU.mult, ALU.mult).then_inc(mix_float, 1)

                for h in MIX_ORDER[0:4]:
                    mix_low(h)
                dve.wait_ge(mix_sq, 2 * l + 2)
                dve.wait_ge(qg_ready, 2 * l + 2)
                dve.tensor_tensor(OHG[:, :, o0:T], OHG[:, :, o0:T], G[:, :, o0:T], ALU.mult).then_inc(gated, 1)
                dve.wait_ge(gated, l + 1)
                for h in range(HEADS):
                    dve.wait_ge(mix_rstd, 8 * l + 4 + h + 1)
                    dve.scalar_tensor_tensor(OHG[:, h, o0:T], OHG[:, h, o0:T], vecT[:, 40 + l:41 + l],
                                             MS_HG[:, h, o0:T], ALU.mult, ALU.mult).then_inc(mix_float, 1)
                    if h > 0:
                        mix_low(h - 1)
                mix_low(HEADS - 1)
                units0 += len(units)
                lv0 += len(levels)
                if l == 0:
                    for d in range(DC):
                        task = ("wo", d)
                        split_lo(dve, UNIT_OF[task] + AHEAD)
                        full(dve, task)
                        drain(dve.tensor_tensor(hT[:, d, :], hT[:, d, :], gbank(task)[:, 0:T], ALU.add), task)
                    drained(dve, ("wo", DC - 1))
                    normed(1, 16)

                    def act_low(f):
                        dve.wait_ge(ah_ready, f + 1)
                        dve.tensor_tensor(act_lo[:, f, :], ACTF[:, f % 2, :], act_hi[:, f, :].bitcast(F32),
                                          ALU.subtract).then_inc(al_ready, 1)

                    for i in range(0, FC, JC):
                        n = min(JC, FC - i)
                        for f in range(i, i + n):
                            split_lo(dve, UNIT_OF[("g", f)] + AHEAD)
                        for f in range(i, i + n):
                            task = ("u", f)
                            split_lo(dve, UNIT_OF[task] + AHEAD)
                            full(dve, task)
                            drained(dve, ("g", f))
                            if f >= 2:
                                dve.wait_ge(al_ready, f - 1)
                            drain(dve.tensor_tensor(ACTF[:, f % 2, :], SGF[:, f % JC, :], gbank(task)[:, 0:T],
                                                    ALU.mult), task)
                            act_low(f)
                    for half in (0, 1):
                        for u in range(FC // 2):
                            split_lo(dve, UNIT_OF[("u", FC - 1)] + 1 + half * (FC // 2) + u + AHEAD)
                        for d in range(4):
                            dve.wait_ge(down_full, 4 * half + d + 1)
                            h = hT[:, 4 * half + d, :]
                            dve.tensor_tensor(h, h, banks[(3 + 4 * half + d) % 8][:, 0:T], ALU.add
                                              ).then_inc(down_drained, 1)
                    dve.wait_ge(down_drained, 8)
            for half in (0, 1):
                for u in range(DC // 2):
                    split_lo(dve, UNIT_OF[("wo1", 1, 1)] - (2 - half) * (DC // 2) + 1 + u + AHEAD)
                for t in (0, 1):
                    task = ("wo1", half, t)
                    full(dve, task)
                    drained(dve, ("hTt", t, half))
                    h = HTOK[:, t, half * 512:(half + 1) * 512]
                    drain(dve.tensor_tensor(h, h, gbank(task)[:, :], ALU.add), task)
            drained(dve, ("wo1", 1, 1))
            dve.wait_ge(tables_in, 16 * 4)
            for t in (0, 1):
                dve.wait_ge(tok_rstd, t + 1)
                dve.scalar_tensor_tensor(UTOK[:, t, :], HTOK[:, t, :], RSUM[:, t:t + 1], NFW[:, :], ALU.mult,
                                         ALU.mult).then_inc(utok_ready, 1)
            def low_unit(n, m):
                dve.wait_ge(hi_ready, len(UNITS) + n * BLOCK_UNITS + m + 1)
                i = (len(UNITS) + m) % NW
                src = half_slot(m // 2)[:, (m % 2) * UNIT:(m % 2 + 1) * UNIT]
                dve.tensor_tensor(WL[:, i, :], src, WH[:, i, :].bitcast(F32), ALU.subtract).then_inc(lo_ready, 1)

            for m in range(AHEAD):
                low_unit(0, m)
            link(dve.memset(rt[:, 88:136], 0.0))
            task = ("logit",)
            full(dve, task)
            drain(dve.tensor_copy(LG, gbank(task)[:, 0:2 * NE].rearrange("p (t e) -> p t e", t=2)), task)
            drained(dve, task)
            for t in (0, 1):
                ins = dve.max(MX[:, t, :], LG[:, t, :])
            link(ins)
            for t in (0, 1):
                ins = dve.max_index(rti[:, 8 * t:8 * t + 8], MX[:, t, :], LG[:, t, :])
            link(ins)
            link(dve.tensor_copy(IDXF, rti[:, 0:16].rearrange("p (t k) -> p t k", t=2)[:, :, 0:2]))
            link(dve.tensor_tensor(OH.rearrange("p t k e -> p (t k) e"), IOTA[:, 0:NE].unsqueeze(1).to_broadcast([P, 4, NE]),
                                   IDXF.rearrange("p t k -> p (t k)").unsqueeze(2).to_broadcast([P, 4, NE]), ALU.is_equal))
            dve.tensor_tensor(MASK, OH[:, :, 0, :], OH[:, :, 1, :], ALU.add).then_inc(mask_ready, 1)
            dve.tensor_tensor(GATE2[:, :, 1], MX[:, :, 1], MX[:, :, 0], ALU.subtract).then_inc(top_ready, 1)
            dve.wait_ge(mask_ready, 1)
            task = ("rank",)
            full(dve, task)
            link(dve.scalar_tensor_tensor(TMP8, gbank(task)[:, 0:2 * NE].rearrange("p (t e) -> p t e", t=2), 1.0, MASK,
                                          ALU.add, ALU.mult))
            link(dve.tensor_scalar(RM[:, :, 0:NE], TMP8, -1.0, None, ALU.add))
            drain(dve.tensor_scalar(OV, gbank(task)[:, 2 * NE:3 * NE], float(P), None, ALU.is_gt), task)
            drained(dve, task)

            def gather_low(b, n):
                dve.wait_ge(xg_hi_ready, 2 * n + b + 1)
                dve.tensor_tensor(xg_lo[:, 4 * b:4 * b + 4, :], banks[b][:, :].rearrange("p (c s) -> p c s", c=4),
                                  xg_hi[:, 4 * b:4 * b + 4, :].bitcast(F32), ALU.subtract).then_inc(G_free[b], 1)

            def onehot(n, step):
                dve.tensor_copy(TMPG[:, 0:2], RM[:, :, n]).then_inc(col_ready, 1)
                dve.wait_ge(col_ready, step)
                for t in (0, 1):
                    ins = dve.tensor_scalar(PH[:, t, :], IOTA, TMPG[:, t:t + 1], None, ALU.is_equal)
                ins.then_inc(p_ready, 1)

            for b in (0, 1):
                dve.memset(TMPG[:, 6 + b:7 + b], 0.0).then_inc(scatter_added[b], 1)
            dve.memset(TMPG[:, 3:4], 0.0).then_inc(down_done, 1)
            onehot(0, 1)
            dve.wait_ge(gate_exp, 1)
            link(dve.tensor_scalar(GATE2[:, :, 0], GATE2[:, :, 1], 1.0, None, ALU.add))
            link(dve.reciprocal(GATE2[:, :, 0], GATE2[:, :, 0]))
            link(dve.tensor_tensor(GATE2[:, :, 1], GATE2[:, :, 1], GATE2[:, :, 0], ALU.mult))
            link(dve.tensor_tensor(OHG2.rearrange("p t k e -> p (t k) e"), OH.rearrange("p t k e -> p (t k) e"),
                                   GATE2.rearrange("p t k -> p (t k)").unsqueeze(2).to_broadcast([P, 4, NE]), ALU.mult))
            link(dve.tensor_tensor(GX[:, :, 0:NE], OHG2[:, :, 0, :], OHG2[:, :, 1, :], ALU.add))
            link(dve.tensor_tensor_scan(CUM, ONE8, OV, 0.0, ALU.mult, ALU.add))
            for j in range(OVER):
                ins = dve.tensor_scalar(SEL[:, j, :], CUM, float(j + 1), None, ALU.is_equal)
            link(ins)
            dve.tensor_copy(EID[:, 0:1], CUM[:, 7:8])
            dve.tensor_scalar(TMP8, RM[:, :, 0:NE], -float(P), None, ALU.add)
            link(dve.tensor_tensor(SEL, SEL, OV.unsqueeze(1).to_broadcast([P, OVER, NE]), ALU.mult))
            dve.tensor_tensor(SELE, SEL, IOTA[:, 0:NE].unsqueeze(1).to_broadcast([P, OVER, NE]), ALU.mult)
            for t in (0, 1):
                dve.tensor_tensor(SELR[:, t], SEL, TMP8[:, t, :].unsqueeze(1).to_broadcast([P, OVER, NE]), ALU.mult)
                ins = dve.tensor_tensor(SELG[:, t], SEL, GX[:, t, 0:NE].unsqueeze(1).to_broadcast([P, OVER, NE]),
                                        ALU.mult)
            link(ins)
            dve.tensor_reduce(EID[:, 1:1 + OVER], SELE, AX.X, ALU.add)
            for t in (0, 1):
                dve.tensor_reduce(RM[:, t, NE:NE + OVER], SELR[:, t], AX.X, ALU.add)
                ins = dve.tensor_reduce(GX[:, t, NE:NE + OVER], SELG[:, t], AX.X, ALU.add)
            link(ins)
            dve.tensor_copy(regs[:, 0:4], EID).then_inc(regs_ready, 1)
            dve.wait_ge(regs_ready, 1)
            for b in (0, 1):
                gather_low(b, 0)

            def expert_block(n):
                def gated_onehot():
                    dve.tensor_copy(TMPG[:, 4:6], GX[:, :, n]).then_inc(col_ready, 1)
                    dve.wait_ge(col_ready, 2 * n + 2)
                    dve.wait_ge(p_ready, n + 1)
                    for t in (0, 1):
                        ins = dve.tensor_scalar(PG[:, t, :], PH[:, t, :], TMPG[:, 4 + t:5 + t], None, ALU.mult)
                    ins.then_inc(pg_ready, 1)

                def next_onehot():
                    dve.wait_ge(pg_ready, n + 1)
                    dve.wait_ge(G_full[1], n * G_USES[1] + 1)
                    onehot(n + 1, 2 * n + 3)

                def low(m):
                    low_unit(n, m)

                def turn(s):
                    dve.wait_ge(het_hi_ready, n * NS + s + 1)
                    dve.tensor_tensor(het_lo[:, s % 2, :], banks[4][:, :], het_hi[:, s % 2, :].bitcast(F32),
                                      ALU.subtract).then_inc(heT_ready, 1)

                def product(s):
                    b = s % 2
                    dve.wait_ge(U_full[b], n * U_USES[b] + s // 2 + 1)
                    dve.wait_ge(G_free[b], n * G_USES[b] + s // 2 + 2)
                    if s >= 2:
                        dve.wait_ge(heT_full, n * NS + s - 1)
                    dve.tensor_tensor(HE[:, b, :], SGE[:, b, :], banks[2 + b][:, :], ALU.mult).then_inc(he_ready, 1)

                m = 0
                for kind, s in EXPERT:
                    for u in range(4):
                        if m + AHEAD < BLOCK_UNITS - 1:
                            low(m + AHEAD)
                        if m == 0:
                            gated_onehot()
                        if m == 4:
                            next_onehot()
                        if kind == "w3" and u == 0 and s > 0:
                            turn(s - 1)
                        m += 1
                    if kind == "w3":
                        product(s)
                    if (kind, s) == ("w2", NS - 2):
                        turn(NS - 1)
                        low(BLOCK_UNITS - 1)
                        for b in (0, 1):
                            gather_low(b, n + 1)
                low(BLOCK_UNITS)
                dve.wait_ge(down_done, n * NS + NS + 1)
                dve.tensor_copy(YS[:, 512:1024], banks[6][:, :]).then_inc(y_ready[1], 1)
                for half in (0, 1):
                    low(BLOCK_UNITS + 1 + half)
                    for t in (0, 1):
                        dve.wait_ge(U_full[t], n * U_USES[t] + (5 if t == 0 else 4) + half)
                        h = HTOK[:, t, half * 512:(half + 1) * 512]
                        dve.tensor_tensor(h, h, scatter_bank(half, t), ALU.add
                                          ).then_inc(scatter_added[t], 1)

            with dve.Fori(0, NE) as e:
                expert_block(e)
            over = dve.value_load(regs[0:1, 0:1], min_val=0, max_val=OVER)
            for j in range(OVER):
                with dve.If(over > j):
                    expert_block(NE + j)
            dve.wait_ge(fnw_in, 16)
            dve.memset(stat[:, 0:1], 0.0).then_inc(tok_sum, 1)
            dve.wait_ge(tok_rstd, 3)
            for t in (0, 1):
                dve.scalar_tensor_tensor(OUTT[:, t, :], HTOK[:, t, :], RSUM[:, 2 + t:3 + t], FNW[:, :], ALU.mult,
                                         ALU.mult).then_inc(out_ready, 1)

        @block.gpsimd
        def _(pool):
            link = chain(pool, pool_step)
            drained(pool, ("rel",))
            pool.dma_start(scratch.ap(), RELROW.unsqueeze(1).to_broadcast([HEADS, P, RELW])).then_inc(rows_out, 16)
            pool.wait_ge(rows_out, 16)
            shifted = scratch.ap().rearrange("h p j -> (h p j)")
            pool.dma_start(bias[:, :, :], bass.AP(shifted.tensor, P - 1, [[RELW - 1, P], [P * RELW, HEADS], [1, T]])
                           ).then_inc(bias_in, 16)
            pool.wait_ge(init_done, 2)
            for l in (0, 1):
                pool.wait_ge(f_sig, l + 1)
                for h in range(HEADS):
                    ins = pool.tensor_scalar(LF[:, h, :], SG[:, h, :], omlb[:, l, h:h + 1], lbt[:, l, h:h + 1],
                                             ALU.mult, ALU.add)
                ins.then_inc(f_gate, 1)
                pool.wait_ge(b_ready, l + 1)
                pool.wait_ge(k_ready, l + 1)
                for t0, tn in SEG[0:2]:
                    end = B[:, :, t0 + tn - 1:t0 + tn].to_broadcast([P, HEADS, tn])
                    ins = pool.tensor_tensor(KEND[:, :, t0:t0 + tn], end, B[:, :, t0:t0 + tn], ALU.subtract)
                ins.then_inc(kdiff, 1)
                pool.wait_ge(t_sig, 2 * l + 1)
                pool.tensor_tensor(Q, Q, TMP, ALU.mult).then_inc(qg_ready, 1)
                pool.wait_ge(qg_ready, 2 * l + 1)

                pool.wait_ge(score_full, sum(len(attention_units(k)) for k in range(l + 1)))
                pool.memset(tile(1)[:, 0:2 * HW + 64], 0.0).then_inc(st_zero, 1)

                def decayed_k(v):
                    m = LEVELS[v]
                    pool.wait_ge(decay_ready, 7 * l + v)
                    if v > 2:
                        levels = level_tasks(l)
                        pool.wait_ge(lv_full, (0 if l == 0 else len(level_tasks(0)))
                                     + sum(1 for a, _ in levels if a <= v - 2))
                    pool.tensor_tensor(level_part(X[v % 2], m, 0), level_part(K, m, 0), level_part(DD[v % 2], m, 0),
                                       ALU.mult).then_inc(xk_ready, 1)

                pool.wait_ge(kexp, l + 1)
                pool.tensor_tensor(KEND[:, :, 0:SEG[2][0]], K[:, :, 0:SEG[2][0]], KEND[:, :, 0:SEG[2][0]],
                                   ALU.mult).then_inc(kend_ready, 1)
                decayed_k(1)
                decayed_k(2)
                difference(pool, 4, l)
                pool.wait_ge(expb, 2 * l + 1)
                pool.tensor_tensor(QB[:, :, META:T], Q[:, :, META:T], SG[:, :, META:T], ALU.mult).then_inc(qb_ready, 1)
                decayed_k(3)
                decayed_k(4)
                difference(pool, 6, l)
                for v in (5, 6, 7):
                    decayed_k(v)
                pool.wait_ge(t_sig, 2 * l + 2)
                pool.tensor_tensor(G, G, TMP, ALU.mult).then_inc(qg_ready, 1)
            pool.wait_ge(mix_ready, 16)
            pool.dma_start(NFW[:, :], A["norm_ffn"][1].partition_broadcast(P)).then_inc(tables_in, 16)
            pool.dma_start(IOTA, A["iota"]).then_inc(tables_in, 16)
            pool.dma_start(UPPER, A["upper"]).then_inc(tables_in, 16)
            pool.dma_start(ROUT, A["moe_router"][0].rearrange("(c p) e -> p c e", p=P)).then_inc(tables_in, 16)
            pool.wait_ge(tables_in, 16 * 4)
            pool.wait_ge(utok_ready, 2)
            pool.dma_start(FNW[:, :], A["final_norm"].partition_broadcast(P)).then_inc(fnw_in, 16)
            pool.wait_ge(fnw_in, 16)


_INS = ['x', 'meta', 'rel_bias', 'norm_mix', 'w_in', 'hg_lb_logits', 'hg_norm_w', 'da_lambda', 'da_subln_w',
        'w_out', 'norm_ffn', 'dense_w1', 'dense_w3', 'dense_w2', 'moe_router', 'moe_w1', 'moe_w3', 'moe_w2',
        'final_norm']


def constants():
    dist = T - 1 - np.arange(RELW)
    exact = BUCKETS // 2
    n = np.maximum(dist, 0)
    nf = np.maximum(n, exact).astype(np.float32)
    large = exact + (np.log(nf / np.float32(exact)) / np.float32(math.log(MAXD / exact))
                     * np.float32(BUCKETS - exact)).astype(np.int32)
    bucket = np.where(n < exact, n, np.minimum(large, BUCKETS - 1))
    buckets = np.zeros((BUCKETS + 1, RELW), np.float32)
    for j in range(RELW):
        buckets[bucket[j] if dist[j] >= 0 else BUCKETS, j] = 1.0
    s = np.arange(P)[:, None]
    t = np.arange(P)[None, :]
    masks = np.zeros((P, len(LEVELS), P), np.float32)
    for v, m in enumerate(LEVELS):
        if m == 0:
            masks[:, v, :] = s == t
        else:
            masks[:, v, :] = (s // (2 * m) == t // (2 * m)) & (s % (2 * m) < m) & (t % (2 * m) >= m)
    return {
        "ident": np.eye(P, dtype=np.float32),
        "masks": masks,
        "buckets": buckets,
        "iota": np.broadcast_to(np.arange(P, dtype=np.float32), (P, P)).copy(),
        "upper": (s < t).astype(np.float32),
    }


def kernel(**inputs):
    import numpy as _np
    import concourse.bacc as _bacc
    from concourse import mybir as _mybir
    from concourse.bass_utils import run_bass_kernel_spmd as _run

    nc = _bacc.Bacc("TRN2", target_bir_lowering=False, num_devices=1)
    arrays, aps = {}, {}
    everything = {name: _np.ascontiguousarray(inputs[name]) for name in _INS}
    everything.update(constants())
    for name, a in everything.items():
        arrays[f"in_{name}_dram"] = a
        aps[name] = nc.dram_tensor(f"in_{name}_dram", a.shape, _mybir.dt.from_np(a.dtype), kind="ExternalInput").ap()
    out = nc.dram_tensor("out_0_dram", (1, SEQ, D), F32, kind="ExternalOutput").ap()
    build(nc, aps, out)
    r = _run(nc, [arrays], core_ids=[0])
    return r.results[0]["out_0_dram"]
```
